# Optimizing a Trainium2 kernel written in Bass

```python
import jax, jax.numpy as jnp
from jax import lax
import numpy as np

D_MODEL = 1024
BATCH = 1
SEQ = 2048
DEPTH = 1

D_MIX = D_MODEL
D_POOL = D_MIX // 2
POOL_WINDOWS = (2, 4, 8, 16)
N_POOL_GROUPS = len(POOL_WINDOWS)
POOL_GROUP_DIM = D_POOL // N_POOL_GROUPS
D_ATTN = D_MIX - D_POOL
HEAD_DIM = 64
N_HEADS = D_ATTN // HEAD_DIM
Q_BLOCK = 128
D_FF = ((8 * D_MODEL // 3 + 127) // 128) * 128
CONV_WIDTH = 3
EPS = 1e-6
D_IN_PROJ = D_POOL + 3 * D_ATTN

kernel_name = "hymba_pool_stickbreaking_convffn"

def rms_normalize(x):
    xf = x.astype(jnp.float32)
    return xf * lax.rsqrt(jnp.mean(xf * xf, axis=-1, keepdims=True) + EPS)

def rmsnorm(x, gain):
    return (rms_normalize(x) * gain.astype(jnp.float32)).astype(x.dtype)

def multiscale_pool(u, w_pool):
    B, S, _ = u.shape
    uf = u.astype(jnp.float32)
    cs = jnp.pad(jnp.cumsum(uf, axis=1), ((0, 0), (1, 0), (0, 0)))
    t1 = jnp.arange(1, S + 1)
    groups = []
    for g, w in enumerate(POOL_WINDOWS):
        sl = slice(g * POOL_GROUP_DIM, (g + 1) * POOL_GROUP_DIM)
        c = cs[:, :, sl]
        lagged = jnp.pad(c[:, :S + 1 - w], ((0, 0), (w - 1, 0), (0, 0)))
        cnt = jnp.minimum(t1, w).astype(jnp.float32)[None, :, None]
        groups.append((c[:, 1:] - lagged) / cnt - uf[:, :, sl])
    p = jnp.stack(groups, axis=2)
    y = jnp.einsum('bsgc,gcd->bsgd', p, w_pool.astype(jnp.float32))
    return y.reshape(B, S, D_POOL)

def stick_breaking_attention(q, k, v):
    B, H, S, Dh = q.shape
    nb = S // Q_BLOCK
    qb = q.astype(jnp.float32).reshape(B, H, nb, Q_BLOCK, Dh).transpose(2, 0, 1, 3, 4)
    kf = k.astype(jnp.float32)
    vf = v.astype(jnp.float32)
    key_pos = jnp.arange(S)
    scale = Dh ** -0.5

    def block(args):
        i, qi = args
        z = jnp.einsum('bhqd,bhkd->bhqk', qi, kf) * scale
        q_pos = i * Q_BLOCK + jnp.arange(Q_BLOCK)
        causal = key_pos[None, :] < q_pos[:, None]
        log_1m_beta = jnp.where(causal, jax.nn.log_sigmoid(-z), 0.0)
        stick = lax.cumsum(log_1m_beta, axis=3, reverse=True) - log_1m_beta
        a = jnp.where(causal, jnp.exp(jax.nn.log_sigmoid(z) + stick), 0.0)
        return jnp.einsum('bhqk,bhkd->bhqd', a, vf)

    out = lax.map(block, (jnp.arange(nb), qb))
    return out.transpose(1, 2, 0, 3, 4).reshape(B, H, S, Dh)

def causal_depthwise_conv(h, conv_w, conv_b):
    S = h.shape[1]
    hp = jnp.pad(h, ((0, 0), (CONV_WIDTH - 1, 0), (0, 0)))
    y = conv_b
    for kk in range(CONV_WIDTH):
        y = y + conv_w[kk] * hp[:, kk:kk + S]
    return y

def setup_inputs(seed: int = 0) -> dict:
    key = jax.random.key(seed)
    ks = jax.random.split(key, 20)
    f32 = jnp.float32

    def nrm(k, shape, scale):
        return jax.random.normal(k, shape, f32) * scale

    def gain(k, n):
        return 1.0 + 0.05 * jax.random.normal(k, (DEPTH, n), f32)

    return {
        "x": jax.random.normal(ks[0], (BATCH, SEQ, D_MODEL), f32),
        "norm_mix_pre": gain(ks[1], D_MODEL),
        "w_in": nrm(ks[2], (DEPTH, D_MODEL, D_IN_PROJ), D_MODEL ** -0.5),
        "w_pool": nrm(ks[3], (DEPTH, N_POOL_GROUPS, POOL_GROUP_DIM, POOL_GROUP_DIM), POOL_GROUP_DIM ** -0.5),
        "pool_scale": gain(ks[4], D_POOL),
        "attn_scale": gain(ks[5], D_ATTN),
        "w_out": nrm(ks[6], (DEPTH, D_MIX, D_MODEL), D_MIX ** -0.5),
        "norm_mix_post": gain(ks[7], D_MODEL),
        "norm_ffn_pre": gain(ks[8], D_MODEL),
        "w_up": nrm(ks[9], (DEPTH, D_MODEL, 2 * D_FF), D_MODEL ** -0.5),
        "conv_w": nrm(ks[10], (DEPTH, CONV_WIDTH, 2 * D_FF), CONV_WIDTH ** -0.5),
        "conv_b": nrm(ks[11], (DEPTH, 2 * D_FF), 0.01),
        "w_down": nrm(ks[12], (DEPTH, D_FF, D_MODEL), D_FF ** -0.5),
        "norm_ffn_post": gain(ks[13], D_MODEL),
    }

def reference(x, norm_mix_pre, w_in, w_pool, pool_scale, attn_scale, w_out, norm_mix_post,
              norm_ffn_pre, w_up, conv_w, conv_b, w_down, norm_ffn_post):
    B, S, _ = x.shape
    for l in range(DEPTH):
        h = rmsnorm(x, norm_mix_pre[l])
        proj = h @ w_in[l]
        u_pool = proj[..., :D_POOL]
        q = proj[..., D_POOL:D_POOL + D_ATTN]
        k = proj[..., D_POOL + D_ATTN:D_POOL + 2 * D_ATTN]
        v = proj[..., D_POOL + 2 * D_ATTN:]

        pool_out = multiscale_pool(u_pool, w_pool[l])

        def heads(t):
            return t.reshape(B, S, N_HEADS, HEAD_DIM).transpose(0, 2, 1, 3)
        attn_out = stick_breaking_attention(heads(q), heads(k), heads(v))
        attn_out = attn_out.transpose(0, 2, 1, 3).reshape(B, S, D_ATTN)

        merged = jnp.concatenate([
            rms_normalize(pool_out) * pool_scale[l].astype(jnp.float32),
            rms_normalize(attn_out) * attn_scale[l].astype(jnp.float32),
        ], axis=-1).astype(x.dtype)
        mix = merged @ w_out[l]
        x = x + rmsnorm(mix, norm_mix_post[l])

        h = rmsnorm(x, norm_ffn_pre[l])
        up = causal_depthwise_conv(h @ w_up[l], conv_w[l], conv_b[l])
        gate, val = up[..., :D_FF], up[..., D_FF:]
        f = (jax.nn.silu(gate) * val) @ w_down[l]
        x = x + rmsnorm(f, norm_ffn_post[l])
    return x


_drawn_inputs = setup_inputs


def setup_inputs(seed=0):
    import zlib

    import numpy as np

    out = dict(_drawn_inputs(seed))
    spreads = {}
    factors = {'conv_b': 7.054}
    for name, (base, spread) in spreads.items():
        noise = np.random.default_rng([zlib.crc32(name.encode()), seed]).standard_normal(out[name].shape)
        drawn = base * np.exp(spread * noise) if base else spread * noise
        out[name] = __import__('jax').numpy.asarray(drawn.astype(out[name].dtype))
    for name, factor in factors.items():
        out[name] = (out[name] * factor).astype(out[name].dtype)
    return out
```

```python
from contextlib import ExitStack


import concourse.bass as bass
from concourse import mybir

F32 = mybir.dt.float32
F32R = mybir.dt.float32r
ALU = mybir.AluOpType
ACT = mybir.ActivationFunctionType
AX = mybir.AxisListType

P = 128
BANK = 512
EPS = 1e-6
MASKED_SCORE = -1e30
POOL_WINDOWS = (2, 4, 8, 16)
HEAD_DIM = 64
LEAD = 2


def done(step, lead=LEAD):
    return step + 1 + lead


def freed(step, ring=LEAD, lead=LEAD):
    return step + 1 + lead - ring


def stored(uses, each=16):
    return each * uses + 16


class Names:

    def __init__(self, nc, stack):
        self.nc, self.stack = nc, stack

    def sb(self, name, shape, dtype=F32):
        return self.stack.enter_context(self.nc.sbuf_tensor(name, shape, dtype))

    def ps(self, name, shape, dtype=F32):
        return self.stack.enter_context(self.nc.psum_tensor(name, shape, dtype))

    def sem(self, name):
        return self.stack.enter_context(self.nc.semaphore(name))

    def sems(self, name, n):
        return [self.sem(f"{name}{i}") for i in range(n)]


def as_f32(tile):
    return tile.bitcast(F32)


def phase_setup(nc, a, c):
    with ExitStack() as stack:
        n = Names(nc, stack)
        n_conv = a["n_ff2"]
        rows = n.sb("rows", [P, 6, P])
        not_before = n.sb("not_before_f", [P, P])
        cols_ps = n.ps("cols_ps", [P, BANK])
        rows_in, zeroed, ident_done, turned, cols_done = (
            n.sem(s) for s in ("rows_in", "zeroed", "ident_done", "turned", "cols_done"))
        with nc.Block() as block:

            @block.sync
            def _(sp):
                sp.dma_start(rows[0:n_conv, 0, :], a["conv_b"][0].rearrange("(j p) -> j p", p=P)).then_inc(rows_in, 16)
                for k in range(a["conv_width"]):
                    sp.dma_start(rows[0:n_conv, 1 + k, :], a["conv_w"][0, k].rearrange("(j p) -> j p", p=P)).then_inc(rows_in, 16)
                for half, name in enumerate(("pool_scale", "attn_scale")):
                    sp.dma_start(rows[4 * half:4 * half + 4, 4, :], a[name][0].rearrange("(j p) -> j p", p=P)).then_inc(rows_in, 16)
                sp.wait_ge(rows_in, 16 * (3 + a["conv_width"]))

            @block.gpsimd
            def _(pool):
                pool.memset(c["ident"][:, :], 0.0).then_inc(zeroed, 1)
                pool.wait_ge(zeroed, 1)
                pool.affine_select(out=c["ident"][:, :], in_=c["ident"][:, :], compare_op=ALU.not_equal, fill=1.0,
                                   base=0, pattern=[[-1, P]], channel_multiplier=1).then_inc(ident_done, 1)
                pool.memset(not_before[:, :], 0.0).then_inc(zeroed, 1)
                pool.wait_ge(zeroed, 2)
                pool.affine_select(out=not_before[:, :], in_=not_before[:, :], compare_op=ALU.is_gt, fill=MASKED_SCORE,
                                   base=0, pattern=[[-1, P]], channel_multiplier=1).then_inc(ident_done, 1)

            @block.tensor
            def _(pe):
                pe.wait_ge(rows_in, 16 * (3 + a["conv_width"]))
                pe.wait_ge(ident_done, 1)
                for k in range(1 + a["conv_width"]):
                    pe.transpose(cols_ps[:, k * n_conv:(k + 1) * n_conv], rows[0:n_conv, k, :],
                                 c["ident"][0:n_conv, 0:n_conv])
                pe.transpose(cols_ps[:, 4 * n_conv:4 * n_conv + 8], rows[0:8, 4, :], c["ident"][0:8, 0:8]).then_inc(turned, 1)

            @block.vector
            def _(dve):
                dve.memset(c["ones"][:, :], 1.0)
                dve.memset(c["eps"][:, :], EPS)
                dve.wait_ge(ident_done, 2)
                dve.tensor_copy(c["ident_r"][:, :], c["ident"][:, :])
                dve.tensor_copy(c["not_before"][:, :], not_before[:, :])
                dve.wait_ge(turned, 1)
                dve.tensor_copy(c["cols"][:, 0:4 * n_conv + 8], cols_ps[:, 0:4 * n_conv + 8]).then_inc(cols_done, 1)


def phase_values(nc, a, c, s, hT):
    tiles, kc, d = a["tiles"], a["kc"], a["d"]
    d_v = a["d_attn"]
    heads = d_v // HEAD_DIM
    v_cols = a["d_in"] - d_v
    with ExitStack() as stack:
        n = Names(nc, stack)
        wv_f = n.sb("wv_f", [P, 2, d_v])
        wv_hi, wv_lo = n.sb("wv_hi", [P, kc, d_v], F32R), n.sb("wv_lo", [P, kc, d_v], F32R)
        xt = [n.sb(f"xt{i}", [P, d]) for i in range(2)]
        squares = n.sb("squares", [P, d], mybir.dt.bfloat16)
        gain = n.sb("gain", [P, d])
        h_hi = [n.sb(f"h_hi{i}", [P, kc, P], F32R) for i in range(2)]
        h_lo = [n.sb(f"h_lo{i}", [P, kc, P], F32R) for i in range(2)]
        v_out = n.sb("v_out", [P, 2, heads, 2, HEAD_DIM], F32R)
        stat = n.sb("stat", [P, 2, 4])
        turn_ps = [n.ps(f"turn_ps{i}", [P, kc * P]) for i in range(2)]
        v_ps = [n.ps(f"v_ps{i}", [P, d_v]) for i in range(2)]
        wv_in, x_in = n.sems("wv_in", 2), n.sems("x_in", 2)
        hT_out, v_stored = n.sems("hT_out", 2), n.sems("v_stored", 2)
        names = ("gain_in", "wv_hi_done", "wv_done", "sq_done", "root_done", "recip_done", "xn_done", "turn_done",
                 "h_hi_done", "h_lo_done", "v_done", "v_hi_done", "v_lo_done")
        (gain_in, wv_hi_done, wv_done, sq_done, root_done, recip_done, xn_done, turn_done,
         h_hi_done, h_lo_done, v_done, v_hi_done, v_lo_done) = (n.sem(x) for x in names)
        x_tiles = a["x"][0].rearrange("(t p) d -> t p d", p=P)
        w_v = a["w_in"][0].rearrange("(c p) n -> p c n", p=P)

        with nc.Block() as block:

            @block.sync
            def _(sp):
                for sem in hT_out + v_stored:
                    sp.sem_inc(sem, 16)

                def load_x(t, slot):
                    sp.wait_ge(turn_done, freed(t))
                    sp.dma_start(xt[slot][:, :], x_tiles[t]).then_inc(x_in[slot], 16)

                load_x(0, 0)
                sp.dma_start(gain[:, :], a["norm_mix_pre"][0].partition_broadcast(P)).then_inc(gain_in, 16)
                for k in range(kc):
                    if k >= 2:
                        sp.wait_ge(wv_done, k - 1)
                    sp.dma_start(wv_f[:, k % 2, :], w_v[:, k, v_cols:]).then_inc(wv_in[k % 2], 16)
                    if k == 1:
                        load_x(1, 1)

                def store(t, i, slot):
                    sp.wait_ge(h_lo_done, done(t))
                    sp.dma_start(as_f32(hT[0][:, :, bass.ts(t, P)]), as_f32(h_hi[slot][:, :, :])).then_inc(hT_out[slot], 16)
                    sp.dma_start(as_f32(hT[1][:, :, bass.ts(t, P)]), as_f32(h_lo[slot][:, :, :])).then_inc(hT_out[slot], 16)
                    sp.wait_ge(v_lo_done, done(t))
                    sp.dma_start(s["v"][:, :, t, :, :].rearrange("h p a e -> p h a e"),
                                 as_f32(v_out[:, slot, :, :, :])).then_inc(v_stored[slot], 16)

                with sp.Fori(0, tiles // 2 - 1) as i:
                    for e in range(2):
                        load_x(i * 2 + (2 + e), e)
                        store(i * 2 + e, i, e)
                for e in range(2):
                    store(tiles - 2 + e, None, e)
                for e in range(2):
                    sp.wait_ge(hT_out[e], stored(tiles // 2, 32))
                    sp.wait_ge(v_stored[e], stored(tiles // 2))

            @block.scalar
            def _(act):
                for sem in (sq_done, root_done, h_hi_done, v_hi_done):
                    act.sem_inc(sem, LEAD)

                def statistics(t, uses, slot):
                    act.wait_ge(x_in[slot], 16 * uses + 16)
                    act.wait_ge(sq_done, freed(t, 1))
                    act.activation(squares[:, :], xt[slot][:, :], ACT.Square, accum_out=stat[:, slot, 0:1]).then_inc(sq_done, 1)
                    act.wait_ge(sq_done, done(t))
                    act.activation(stat[:, slot, 1:2], stat[:, slot, 0:1], ACT.Sqrt, scale=1.0 / d,
                                   bias=c["eps"][:, 0:1]).then_inc(root_done, 1)

                def h_half(t, uses, slot):
                    act.wait_ge(turn_done, done(t))
                    act.wait_ge(v_done, freed(t))
                    act.wait_ge(hT_out[slot], stored(uses, 32))
                    act.activation(h_hi[slot][:, :, :].rearrange("p c t -> p (c t)"), turn_ps[slot][:, :],
                                   ACT.Copy).then_inc(h_hi_done, 1)

                def v_half(t, uses, slot):
                    act.wait_ge(v_done, done(t))
                    act.wait_ge(v_stored[slot], stored(uses))
                    act.activation(v_out[:, slot, :, 0, :], v_ps[slot][:, :].rearrange("p (h e) -> p h e", h=heads),
                                   ACT.Copy).then_inc(v_hi_done, 1)

                statistics(0, 0, 0)
                statistics(1, 0, 1)
                h_half(0, 0, 0)
                with act.Fori(0, tiles // 2 - 1) as i:
                    for e in range(2):
                        statistics(i * 2 + (2 + e), i + 1, e)
                        h_half(i * 2 + (1 + e), i + e, 1 - e)
                        v_half(i * 2 + e, i, e)
                h_half(tiles - 1, tiles // 2 - 1, 1)
                for e in range(2):
                    v_half(tiles - 2 + e, tiles // 2 - 1, e)

            @block.vector
            def _(dve):
                for sem in (recip_done, xn_done, h_lo_done, v_lo_done):
                    dve.sem_inc(sem, LEAD)
                for k in range(kc):
                    dve.wait_ge(wv_in[k % 2], 16 * (k // 2 + 1))
                    dve.tensor_copy(wv_hi[:, k, :], wv_f[:, k % 2, :]).then_inc(wv_hi_done, 1)
                    dve.wait_ge(wv_hi_done, k + 1)
                    dve.tensor_tensor(wv_lo[:, k, :], wv_f[:, k % 2, :], as_f32(wv_hi[:, k, :]), ALU.subtract).then_inc(wv_done, 1)
                dve.wait_ge(gain_in, 16)

                def scale_x(t, slot):
                    dve.wait_ge(root_done, done(t))
                    dve.reciprocal(stat[:, slot, 2:3], stat[:, slot, 1:2]).then_inc(recip_done, 1)
                    dve.wait_ge(recip_done, done(t))
                    dve.scalar_tensor_tensor(out=xt[slot][:, :], in0=xt[slot][:, :], scalar=stat[:, slot, 2:3],
                                             in1=gain[:, :], op0=ALU.mult, op1=ALU.mult).then_inc(xn_done, 1)

                def h_half(t, uses, slot):
                    dve.wait_ge(h_hi_done, done(t))
                    dve.wait_ge(v_done, freed(t))
                    dve.wait_ge(hT_out[slot], stored(uses, 32))
                    dve.tensor_tensor(h_lo[slot][:, :, :].rearrange("p c t -> p (c t)"), turn_ps[slot][:, :],
                                      as_f32(h_hi[slot][:, :, :].rearrange("p c t -> p (c t)")), ALU.subtract).then_inc(h_lo_done, 1)

                def v_half(t, uses, slot):
                    dve.wait_ge(v_hi_done, done(t))
                    dve.wait_ge(v_stored[slot], stored(uses))
                    dve.tensor_tensor(v_out[:, slot, :, 1, :], v_ps[slot][:, :].rearrange("p (h e) -> p h e", h=heads),
                                      as_f32(v_out[:, slot, :, 0, :]), ALU.subtract).then_inc(v_lo_done, 1)

                scale_x(0, 0)
                scale_x(1, 1)
                h_half(0, 0, 0)
                with dve.Fori(0, tiles // 2 - 1) as i:
                    for e in range(2):
                        scale_x(i * 2 + (2 + e), e)
                        h_half(i * 2 + (1 + e), i + e, 1 - e)
                        v_half(i * 2 + e, i, e)
                h_half(tiles - 1, tiles // 2 - 1, 1)
                for e in range(2):
                    v_half(tiles - 2 + e, tiles // 2 - 1, e)

            @block.tensor
            def _(pe):
                for sem in (turn_done, v_done):
                    pe.sem_inc(sem, LEAD)

                def turn(t, slot):
                    pe.wait_ge(xn_done, done(t))
                    pe.wait_ge(h_lo_done, freed(t))
                    for k in range(kc):
                        m = pe.transpose(turn_ps[slot][:, k * P:(k + 1) * P], xt[slot][:, k * P:(k + 1) * P], c["ident"][:, :])
                    m.then_inc(turn_done, 1)

                def values(t, slot):
                    pe.wait_ge(h_lo_done, done(t))
                    pe.wait_ge(v_lo_done, freed(t))
                    for k in range(kc):
                        for j, (h, w) in enumerate(((h_hi, wv_hi), (h_hi, wv_lo), (h_lo, wv_hi))):
                            m = pe.matmul(v_ps[slot][:, :], h[slot][:, k, :], w[:, k, :],
                                          start=(k == 0 and j == 0), stop=(k == kc - 1 and j == 2))
                    m.then_inc(v_done, 1)

                turn(0, 0)
                pe.wait_ge(wv_done, kc)
                with pe.Fori(0, tiles // 2 - 1) as i:
                    for e in range(2):
                        turn(i * 2 + (e + 1), 1 - e)
                        values(i * 2 + e, e)
                turn(tiles - 1, 1)
                for e in range(2):
                    values(tiles - 2 + e, e)


def phase_projections(nc, a, c, s, hT):
    kc, seq, groups = a["kc"], a["seq"], a["seq"] // BANK
    n_u, n_qk = a["d_pool"] // P, 2 * a["d_attn"] // P
    blocks = n_u + n_qk
    pad = max(POOL_WINDOWS)
    with ExitStack() as stack:
        n = Names(nc, stack)
        w_f = n.sb("w_f", [P, 2, kc, P])
        w_hi = [n.sb(f"w_hi{i}", [P, kc, P], F32R) for i in range(2)]
        w_lo = [n.sb(f"w_lo{i}", [P, kc, P], F32R) for i in range(2)]
        u = n.sb("u", [P, pad + seq])
        run = n.sb("run", [P, 2, pad + seq])
        ramp = n.sb("ramp", [P, pad])
        qk_hi, qk_lo = n.sb("qk_hi", [P, 2, BANK], F32R), n.sb("qk_lo", [P, 2, BANK], F32R)
        out_ps = [n.ps(f"out_ps{i}", [P, BANK]) for i in range(8)]
        w_in_, qk_out = n.sems("w_in", 2), n.sems("qk_out", 2)
        (w_hi_done, w_lo_done, out_done, bank_read, pool_step, pool_done, pooled_out, hi_done) = (
            n.sem(x) for x in ("w_hi_done", "w_lo_done", "out_done", "bank_read", "pool_step", "pool_done",
                               "pooled_out", "hi_done"))
        w_cols = a["w_in"][0].rearrange("(c p) (b n) -> b p c n", p=P, n=P)

        with nc.Block() as block:

            @block.sync
            def _(sp):
                for sem in qk_out:
                    sp.sem_inc(sem, 16)

                def load_w(b, i, slot):
                    sp.wait_ge(w_lo_done, freed(b))
                    sp.dma_start(w_f[:, slot, :, :], w_cols[b]).then_inc(w_in_[slot], 16)

                for b in range(n_u + 2):
                    load_w(b, None, b % 2)
                    if b >= 2:
                        sp.wait_ge(pool_done, b - 1)
                        sp.dma_start(s["pool"][b - 2], run[:, (b - 2 + 1) % 2, pad:]).then_inc(pooled_out, 16)
                def store(b, j, count):
                    slot = j % 2
                    sp.wait_ge(bank_read, done(count + n_u * groups, 8))
                    sp.dma_start(s["qk"][b, 0, :, j * BANK:(j + 1) * BANK], as_f32(qk_hi[:, slot, :])).then_inc(qk_out[slot], 16)
                    sp.dma_start(s["qk"][b, 1, :, j * BANK:(j + 1) * BANK], as_f32(qk_lo[:, slot, :])).then_inc(qk_out[slot], 16)

                with sp.Fori(0, n_qk // 2 - 1) as i:
                    for e in range(2):
                        for j in range(groups):
                            store(i * 2 + e, j, (i * 2 + e) * groups + j)
                        load_w(i * 2 + (n_u + 2 + e), None, e)
                for e in range(2):
                    for j in range(groups):
                        store(n_qk - 2 + e, j, (n_qk - 2 + e) * groups + j)
                for e in range(2):
                    sp.wait_ge(qk_out[e], stored(n_qk * groups // 2, 32))
                sp.wait_ge(pooled_out, 16 * n_u)

            @block.scalar
            def _(act):
                act.sem_inc(hi_done, LEAD)
                act.sem_inc(bank_read, 8)
                for b in range(n_u):
                    for j in range(groups):
                        act.wait_ge(out_done, done(b * groups + j, 8))
                        if j == 0 and b >= 1:
                            act.wait_ge(pool_done, b)
                        act.activation(u[:, pad + j * BANK:pad + (j + 1) * BANK], out_ps[(b * groups + j) % 8][:, :],
                                       ACT.Copy).then_inc(bank_read, 1)
                with act.Fori(0, n_qk // 2) as i:
                    for e in range(2):
                        for j in range(groups):
                            count = (i * 2 + e) * groups + j
                            act.wait_ge(out_done, done(count + n_u * groups, 8))
                            act.wait_ge(qk_out[j % 2], stored((i * 2 + e) * (groups // 2) + j // 2, 32))
                            act.activation(qk_hi[:, j % 2, :], out_ps[(e * groups + j) % 8][:, :], ACT.Copy).then_inc(hi_done, 1)

            @block.vector
            def _(dve):
                for sem in (w_hi_done, w_lo_done):
                    dve.sem_inc(sem, LEAD)

                def split_w(b, i, slot):
                    dve.wait_ge(w_in_[slot], 16 * i + 16)
                    dve.wait_ge(out_done, done(b * groups - 1 - groups, 8))
                    dve.tensor_copy(w_hi[slot][:, :, :], w_f[:, slot, :, :]).then_inc(w_hi_done, 1)
                    dve.wait_ge(w_hi_done, done(b))
                    dve.tensor_tensor(w_lo[slot][:, :, :], w_f[:, slot, :, :], as_f32(w_hi[slot][:, :, :]), ALU.subtract).then_inc(w_lo_done, 1)

                steps = [0]

                def step(ins):
                    steps[0] += 1
                    ins.then_inc(pool_step, 1)
                    dve.wait_ge(pool_step, steps[0])

                split_w(0, 0, 0)
                split_w(1, 0, 1)
                step(dve.memset(u[:, 0:pad], 0.0))
                step(dve.memset(run[:, 0, 0:pad], 0.0))
                step(dve.memset(run[:, 1, 0:pad], 0.0))
                for b, window in enumerate(POOL_WINDOWS):
                    for t in range(pad):
                        last = dve.memset(ramp[:, t:t + 1], 1.0 / min(t + 1, window))
                    step(last)
                    dve.wait_ge(bank_read, done((b + 1) * groups - 1, 8))
                    src, width, side = u[:, :], 1, (b + 1) % 2
                    while width < window:
                        if width == 1 and b >= 1:
                            dve.wait_ge(pooled_out, 16 * b)
                        dst = run[:, side, :]
                        step(dve.tensor_tensor(dst[:, pad:], src[:, pad:], src[:, pad - width:pad + seq - width], ALU.add))
                        src, width, side = dst, 2 * width, 1 - side
                    other = run[:, side, :]
                    step(dve.tensor_tensor(other[:, pad:2 * pad], src[:, pad:2 * pad], ramp[:, :], ALU.mult))
                    step(dve.tensor_tensor(run[:, (b + 1) % 2, pad:2 * pad], other[:, pad:2 * pad], u[:, pad:2 * pad], ALU.subtract))
                    dve.scalar_tensor_tensor(out=run[:, (b + 1) % 2, 2 * pad:], in0=src[:, 2 * pad:], scalar=1.0 / window,
                                             in1=u[:, 2 * pad:], op0=ALU.mult, op1=ALU.subtract).then_inc(pool_done, 1)
                    split_w(b + 2, (b + 2) // 2, b % 2)

                def split_qk(i, e):
                    for j in range(groups):
                        count = (i * 2 + e) * groups + j
                        dve.wait_ge(hi_done, done(count))
                        dve.wait_ge(qk_out[j % 2], stored((i * 2 + e) * (groups // 2) + j // 2, 32))
                        dve.tensor_tensor(qk_lo[:, j % 2, :], out_ps[(e * groups + j) % 8][:, :],
                                          as_f32(qk_hi[:, j % 2, :]), ALU.subtract).then_inc(bank_read, 1)

                with dve.Fori(0, n_qk // 2 - 1) as i:
                    for e in range(2):
                        split_qk(i, e)
                        split_w(i * 2 + (n_u + 2 + e), i + (n_u // 2 + 1), e)
                for e in range(2):
                    split_qk(n_qk // 2 - 1, e)

            @block.tensor
            def _(pe):
                pe.sem_inc(out_done, 8)

                with pe.Fori(0, blocks // 2) as i:
                    for e in range(2):
                        b = i * 2 + e
                        pe.wait_ge(w_lo_done, done(b))
                        for j in range(groups):
                            pe.wait_ge(bank_read, freed(b * groups + j, 8, 8))
                            for k in range(kc):
                                for t, (w, h) in enumerate(((w_hi, 0), (w_hi, 1), (w_lo, 0))):
                                    m = pe.matmul(out_ps[e * groups + j][:, :], w[e][:, k, :], hT[h][:, k, j * BANK:(j + 1) * BANK],
                                                  start=(k == 0 and t == 0), stop=(k == kc - 1 and t == 2))
                            m.then_inc(out_done, 1)


def phase_attention(nc, a, c, s):
    tiles, seq = a["tiles"], a["seq"]
    per = BANK // P
    heads = a["d_attn"] // HEAD_DIM
    scale = HEAD_DIM ** -0.5
    n_u = a["d_pool"] // P
    groups = seq // BANK
    lead = 4
    units = [(e, q, k * BANK, min((q + 1) * P - k * BANK, BANK), k == q // per, k == 0)
             for e in range(2) for q in range(tiles) for k in range(q // per, -1, -1)]
    total = len(units)
    per_head = total // 2
    last_unit = {(e, q): i for i, (e, q, _, _, _, last) in enumerate(units) if last}
    with ExitStack() as stack:
        n = Names(nc, stack)
        q_hi = [n.sb(f"q_hi{i}", [P, seq], F32R) for i in range(2)]
        q_lo = [n.sb(f"q_lo{i}", [P, seq], F32R) for i in range(2)]
        k_both = [n.sb(f"k_both{i}", [P, seq], F32R) for i in range(2)]
        v_both = [n.sb(f"v_both{i}", [P, tiles, 2, HEAD_DIM], F32R) for i in range(2)]
        rest = [n.sb(f"rest{i}", [P, BANK]) for i in range(3)]
        beta = [n.sb(f"beta{i}", [P, BANK]) for i in range(3)]
        stick = [n.sb(f"stick{i}", [P, seq + 1]) for i in range(2)]
        weight = [n.sb(f"weight{i}", [P, BANK]) for i in range(3)]
        wT_hi = [n.sb(f"wT_hi{i}", [P, BANK], F32R) for i in range(2)]
        wT_lo = [n.sb(f"wT_lo{i}", [P, BANK], F32R) for i in range(2)]
        mixed = [n.sb(f"mixed{i}", [HEAD_DIM, seq]) for i in range(2)]
        pooled = n.sb("pooled", [P, 2, seq])
        p_hi, p_lo = n.sb("p_hi", [P, seq], F32R), n.sb("p_lo", [P, seq], F32R)
        wp_f = n.sb("wp_f", [P, n_u, P])
        wp_hi, wp_lo = n.sb("wp_hi", [P, n_u, P], F32R), n.sb("wp_lo", [P, n_u, P], F32R)
        z_ps = [n.ps(f"z_ps{i}", [P, BANK]) for i in range(4)]
        wT_ps = [n.ps(f"wT_ps{i}", [P, BANK]) for i in range(2)]
        o_ps = [n.ps(f"o_ps{i}", [HEAD_DIM, P]) for i in range(2)]
        head_in, mixed_out, pooled_in, pooled_out = (n.sems(x, 2) for x in ("head_in", "mixed_out", "pooled_in2_", "pooled_out2_"))
        (wp_in, wp_hi_done, wp_done, p_hi_done, p_lo_done, pool_mm, pool_read, one_done) = (
            n.sem(x) for x in ("wp_in", "wp_hi_done", "wp_done", "p_hi_done", "p_lo_done", "pool_mm", "pool_read", "one_done"))
        (z_done, rest_done, beta_done, stick_done, weight_done, turned, hi_done, lo_done, pv_done, o_read) = (
            n.sem(x) for x in ("z_done", "rest_done", "beta_done", "stick_done", "weight_done",
                               "wT_turned", "wT_hi_done", "wT_lo_done", "pv_done", "o_read"))

        def col(q, key):
            return seq - (q + 1) * P + key

        with nc.Block() as block:

            @block.sync
            def _(sp):
                for sem in mixed_out:
                    sp.sem_inc(sem, 16)

                def load_head(pair, e, first=False):
                    half = slice(e * HEAD_DIM, (e + 1) * HEAD_DIM)
                    top, bottom = slice(0, HEAD_DIM), slice(HEAD_DIM, P)
                    for part, hi_lo, dst in ((top, 0, q_hi), (bottom, 0, q_hi), (top, 1, q_lo), (bottom, 1, q_lo)):
                        sp.dma_start(as_f32(dst[e][part, :]), s["qk"][pair, hi_lo, half, :]).then_inc(head_in[e], 16)
                    for part, hi_lo in ((top, 0), (bottom, 1)):
                        sp.dma_start(as_f32(k_both[e][part, :]), s["qk"][pair + heads // 2, hi_lo, half, :]).then_inc(head_in[e], 16)
                    sp.dma_start(as_f32(v_both[e][:, :, :, :]), s["v"][pair * 2 + e]).then_inc(head_in[e], 16)

                def store_head(pair, e):
                    sp.wait_ge(o_read, done((pair * 2 + e + 1) * tiles - 1, lead))
                    sp.dma_start(s["merged"][bass.ds(a["d_pool"] + (pair * 2 + e) * HEAD_DIM, HEAD_DIM), :], mixed[e][:, :]).then_inc(mixed_out[e], 16)

                sp.dma_start(wp_f[:, :, :], a["w_pool"][0].rearrange("g c d -> c g d")).then_inc(wp_in, 16)
                for g in range(n_u):
                    if g >= 2:
                        sp.wait_ge(pool_read, groups * (g - 1))
                        sp.dma_start(s["merged"][(g - 2) * P:(g - 1) * P, :], pooled[:, g % 2, :]).then_inc(pooled_out[g % 2], 16)
                        sp.wait_ge(pooled_out[g % 2], 16)
                    sp.dma_start(pooled[:, g % 2, :], s["pool"][g]).then_inc(pooled_in[g % 2], 16)
                    if g == 1:
                        load_head(0, 0)
                load_head(0, 1)
                for g in range(n_u - 2, n_u):
                    sp.wait_ge(pool_read, groups * (g + 1))
                    sp.dma_start(s["merged"][g * P:(g + 1) * P, :], pooled[:, g % 2, :]).then_inc(pooled_out[g % 2], 16)
                with sp.Fori(0, heads // 2 - 1) as i:
                    for e in range(2):
                        sp.wait_ge(pv_done, done(i * total + (e + 1) * per_head - 1, lead))
                        load_head(i + 1, e)
                        store_head(i, e)
                for e in range(2):
                    store_head(heads // 2 - 1, e)
                for e in range(2):
                    sp.wait_ge(mixed_out[e], stored(heads // 2))
                    sp.wait_ge(pooled_out[e], 16 * (n_u // 2))

            @block.scalar
            def _(act):
                for sem in (rest_done, beta_done, hi_done, o_read):
                    act.sem_inc(sem, lead)
                for g in range(n_u):
                    act.wait_ge(pooled_in[g % 2], 16 * (g // 2 + 1))
                    if g >= 1:
                        act.wait_ge(pool_mm, groups * g)
                    act.activation(p_hi[:, :], pooled[:, g % 2, :], ACT.Copy).then_inc(p_hi_done, 1)
                    for j in range(groups):
                        act.wait_ge(pool_mm, groups * g + j + 1)
                        act.wait_ge(p_lo_done, g + 1)
                        act.activation(pooled[:, g % 2, j * BANK:(j + 1) * BANK], z_ps[j][:, :], ACT.Copy).then_inc(pool_read, 1)

                with act.Fori(0, heads // 2) as i:
                    for u in range(total + 5):
                        if u < total:
                            t, w = i * total + u, units[u][3]
                            act.wait_ge(z_done, done(t, lead))
                            act.wait_ge(stick_done, freed(t, 3, lead))
                            act.activation(rest[u % 3][:, 0:w], z_ps[u % 4][:, 0:w], ACT.Sigmoid, scale=-scale).then_inc(rest_done, 1)
                            act.wait_ge(weight_done, freed(t, 3, lead))
                            act.activation(beta[u % 3][:, 0:w], z_ps[u % 4][:, 0:w], ACT.Sigmoid, scale=scale).then_inc(beta_done, 1)
                        if 0 <= u - 2 < total:
                            v = u - 2
                            t, w = i * total + v, units[v][3]
                            act.wait_ge(turned, done(t, lead))
                            act.wait_ge(pv_done, freed(t, 2, lead))
                            act.activation(wT_hi[v % 2][:, 0:w], wT_ps[v % 2][:, 0:w], ACT.Copy).then_inc(hi_done, 1)
                        if 0 <= u - 5 < total and units[u - 5][5]:
                            e, q = units[u - 5][0:2]
                            act.wait_ge(pv_done, done(i * total + (u - 5), lead))
                            if q == 0:
                                act.wait_ge(mixed_out[e], stored(i))
                            act.activation(mixed[e][:, q * P:(q + 1) * P], o_ps[q % 2][:, :], ACT.Copy).then_inc(o_read, 1)

            @block.gpsimd
            def _(pool):
                pool.sem_inc(weight_done, lead)
                with pool.Fori(0, heads // 2) as i:
                    for u in range(total + 1):
                        if u >= 1:
                            v = u - 1
                            e, q, key, w, first, _ = units[v]
                            t = i * total + v
                            pool.wait_ge(beta_done, done(t, lead))
                            pool.wait_ge(stick_done, done(t, lead))
                            pool.wait_ge(turned, freed(t, 3, lead))
                            at = col(q, key) + 1
                            pool.tensor_tensor(weight[v % 3][:, 0:w], beta[v % 3][:, 0:w], stick[q % 2][:, at:at + w],
                                               ALU.mult).then_inc(weight_done, 1)

            @block.vector
            def _(dve):
                for sem in (stick_done, lo_done):
                    dve.sem_inc(sem, lead)
                for i in range(2):
                    dve.memset(stick[i][:, seq:seq + 1], 1.0).then_inc(one_done, 1)
                dve.wait_ge(wp_in, 16)
                dve.tensor_copy(wp_hi[:, :, :], wp_f[:, :, :]).then_inc(wp_hi_done, 1)
                dve.wait_ge(wp_hi_done, 1)
                dve.tensor_tensor(wp_lo[:, :, :], wp_f[:, :, :], as_f32(wp_hi[:, :, :]), ALU.subtract).then_inc(wp_done, 1)
                for g in range(n_u):
                    dve.wait_ge(p_hi_done, g + 1)
                    dve.tensor_tensor(p_lo[:, :], pooled[:, g % 2, :], as_f32(p_hi[:, :]), ALU.subtract).then_inc(p_lo_done, 1)
                with dve.Fori(0, heads // 2) as i:
                    for u in range(total + 3):
                        if 0 <= u - 3:
                            v = u - 3
                            t, w = i * total + v, units[v][3]
                            dve.wait_ge(hi_done, done(t, lead))
                            dve.wait_ge(pv_done, freed(t, 2, lead))
                            dve.tensor_tensor(wT_lo[v % 2][:, 0:w], wT_ps[v % 2][:, 0:w], as_f32(wT_hi[v % 2][:, 0:w]),
                                              ALU.subtract).then_inc(lo_done, 1)
                        if u < total:
                            e, q, key, w, first, _ = units[u]
                            t = i * total + u
                            dve.wait_ge(rest_done, done(t, lead))
                            if first:
                                if e or q >= 2:
                                    before = last_unit[(e, q - 2)] if q >= 2 else last_unit[(0, tiles - 2 + q)]
                                    dve.wait_ge(weight_done, done(i * total + before, lead))
                                else:
                                    dve.wait_ge(weight_done, freed(i * total, 1, lead))
                                start = 1.0
                            else:
                                dve.wait_ge(stick_done, freed(t, 1, lead))
                                start = stick[q % 2][:, col(q, key) + w:col(q, key) + w + 1]
                            at = col(q, key)
                            backwards = rest[u % 3][:, 0:w][:, ::-1]
                            dve.tensor_tensor_scan(stick[q % 2][:, at:at + w][:, ::-1], backwards, backwards, start,
                                                   ALU.mult, ALU.bypass).then_inc(stick_done, 1)

            @block.tensor
            def _(pe):
                for sem in (z_done, turned, pv_done):
                    pe.sem_inc(sem, lead)
                pe.wait_ge(wp_done, 1)
                for g in range(n_u):
                    pe.wait_ge(p_lo_done, g + 1)
                    for j in range(groups):
                        if g >= 1:
                            pe.wait_ge(pool_read, groups * (g - 1) + j + 1)
                        for k, (w, x) in enumerate(((wp_hi, p_hi), (wp_hi, p_lo), (wp_lo, p_hi))):
                            m = pe.matmul(z_ps[j][:, :], w[:, g, :], x[:, j * BANK:(j + 1) * BANK], start=(k == 0), stop=(k == 2))
                        m.then_inc(pool_mm, 1)
                pe.wait_ge(pool_read, groups * n_u)

                with pe.Fori(0, heads // 2) as i:
                    def scores(u):
                        e, q, key, w, first, _ = units[u]
                        if u % per_head == 0:
                            pe.wait_ge(head_in[e], 16 * 7 * i + 16 * 7)
                        pe.wait_ge(beta_done, freed(i * total + u, 4, lead))
                        for k, half in enumerate((q_hi, q_lo)):
                            m = pe.matmul(z_ps[u % 4][:, 0:w], half[e][:, q * P:(q + 1) * P], k_both[e][:, key:key + w],
                                          start=(k == 0), stop=(k == 1))
                            if first and k == 0:
                                pe.matmul(z_ps[u % 4][:, w - P:w], c["ident_r"][:, :], c["not_before"][:, :], start=False, stop=False)
                        m.then_inc(z_done, 1)

                    def turn(u):
                        t, w = i * total + u, units[u][3]
                        pe.wait_ge(weight_done, done(t, lead))
                        pe.wait_ge(lo_done, freed(t, 2, lead))
                        for b in range(w // P):
                            m = pe.transpose(wT_ps[u % 2][:, b * P:(b + 1) * P], weight[u % 3][:, b * P:(b + 1) * P], c["ident"][:, :])
                        m.then_inc(turned, 1)

                    def values(u):
                        e, q, key, w, first, last = units[u]
                        pe.wait_ge(lo_done, done(i * total + u, lead))
                        if first:
                            pe.wait_ge(o_read, freed(i * (2 * tiles) + (e * tiles + q), 2, lead))
                        for b in range(w // P):
                            for k, (half, x) in enumerate(((0, wT_hi), (0, wT_lo), (1, wT_hi))):
                                m = pe.matmul(o_ps[q % 2][:, :], v_both[e][:, key // P + b, half, :], x[u % 2][:, b * P:(b + 1) * P],
                                              start=(first and b == 0 and k == 0), stop=(last and b == w // P - 1 and k == 2))
                        m.then_inc(pv_done, 1)

                    scores(0)
                    for u in range(total + 4):
                        if u + 1 < total:
                            scores(u + 1)
                        if 0 <= u - 2 < total:
                            turn(u - 2)
                        if 0 <= u - 4:
                            values(u - 4)


def phase_mix(nc, a, c, s):
    tiles, kc, d = a["tiles"], a["kc"], a["d"]
    n_pool = a["d_pool"] // P
    part_width = a["d_pool"]
    scales = c["cols"][:, 4 * a["n_ff2"]:4 * a["n_ff2"] + kc]
    with ExitStack() as stack:
        n = Names(nc, stack)
        w_f = n.sb("wo_f", [P, 2, d])
        w_hi, w_lo = n.sb("wo_hi", [P, kc, d], F32R), n.sb("wo_lo", [P, kc, d], F32R)
        merged = [n.sb(f"merged{i}", [P, kc, P]) for i in range(2)]
        m_hi = [n.sb(f"m_hi{i}", [P, kc, P], F32R) for i in range(2)]
        m_lo = [n.sb(f"m_lo{i}", [P, kc, P], F32R) for i in range(2)]
        squares = n.sb("m_squares", [P, kc, P])
        junk = n.sb("junk", [P, d], mybir.dt.bfloat16)
        sums = n.sb("sums", [P, 2, P])
        xt = [n.sb(f"xo{i}", [P, d]) for i in range(2)]
        mix = [n.sb(f"mix{i}", [P, d]) for i in range(2)]
        hn = [n.sb(f"hn{i}", [P, d]) for i in range(2)]
        h_hi = [n.sb(f"h2_hi{i}", [P, kc, P], F32R) for i in range(2)]
        h_lo = [n.sb(f"h2_lo{i}", [P, kc, P], F32R) for i in range(2)]
        gains = n.sb("gains_mix", [P, 2, d])
        stat = n.sb("stat_mix", [P, 2, 12])
        pool_ps, attn_ps = n.ps("pool_ps", [P, d]), n.ps("attn_ps", [P, d])
        turn_ps = n.ps("h2_turn_ps", [P, d])
        ss_ps = n.ps("ss_ps", [P, 2, 2])
        w_in_, merged_in, x_in, x2_out, hT_out = (n.sems(x, 2) for x in ("wo_in", "merged_in", "xo_in", "x2_out", "h2T_out"))
        names = ("gains_in", "wo_hi_done", "wo_done", "m_sq", "m_sum", "m_scaled", "m_hi_done", "m_lo_done", "ss_done",
                 "roots_done", "recips_done", "pool_mm_done", "mix_mm_done", "pool_scaled", "mix_done", "mix_sq", "mix_root", "mix_recip", "y_done",
                 "x2_done", "x2_stored", "x2_sq", "x2_root", "x2_recip", "hn_done", "h2_turned", "h2_hi_done", "h2_lo_done")
        (gains_in, wo_hi_done, wo_done, m_sq, m_sum, m_scaled, m_hi_done, m_lo_done, ss_done, roots_done, recips_done,
         pool_mm_done, mix_mm_done, pool_scaled, mix_done, mix_sq, mix_root, mix_recip, y_done, x2_done, x2_stored, x2_sq, x2_root, x2_recip,
         hn_done, turned, hi_done, lo_done) = (n.sem(x) for x in names)
        x_tiles = a["x"][0].rearrange("(t p) d -> t p d", p=P)
        w_rows = a["w_out"][0].rearrange("(c p) n -> c p n", p=P)
        m_cols = s["merged"].rearrange("(c p) t -> p c t", p=P)

        def steps(eng, step):
            for t in range(2):
                step(t, t % 2, 0)
            with eng.Fori(0, tiles // 2 - 2) as i:
                for e in range(2):
                    step(i * 2 + (2 + e), e, i + 1)
            for t in range(tiles - 2, tiles + 2):
                step(t, t % 2, t // 2)

        def is_tile(t):
            return not isinstance(t, int) or 0 <= t < tiles

        with nc.Block() as block:

            @block.sync
            def _(sp):
                for sem in hT_out:
                    sp.sem_inc(sem, 16)

                def load_merged(t, slot):
                    sp.wait_ge(m_lo_done, freed(t))
                    sp.dma_start(merged[slot][:, :, :], m_cols[:, :, bass.ts(t, P)]).then_inc(merged_in[slot], 16)

                def load_x(t, slot):
                    sp.wait_ge(hn_done, freed(t))
                    sp.wait_ge(x2_stored, freed(t))
                    sp.dma_start(xt[slot][:, :], x_tiles[t]).then_inc(x_in[slot], 16)

                def store_h(t, slot):
                    sp.wait_ge(lo_done, done(t))
                    sp.dma_start(s["h2T"][0][:, :, bass.ts(t, P)], as_f32(h_hi[slot][:, :, :])).then_inc(hT_out[slot], 16)
                    sp.dma_start(s["h2T"][1][:, :, bass.ts(t, P)], as_f32(h_lo[slot][:, :, :])).then_inc(hT_out[slot], 16)

                load_merged(0, 0)
                for k in range(kc):
                    if k >= 2:
                        sp.wait_ge(wo_done, k - 1)
                    sp.dma_start(w_f[:, k % 2, :], w_rows[k]).then_inc(w_in_[k % 2], 16)
                load_merged(1, 1)
                for i, name in enumerate(("norm_mix_post", "norm_ffn_pre")):
                    sp.dma_start(gains[:, i, :], a[name][0].partition_broadcast(P)).then_inc(gains_in, 16)

                def step(t, slot, uses):
                    if is_tile(t):
                        load_x(t, slot)
                    if is_tile(t + 1) and not (isinstance(t, int) and t == 0):
                        load_merged(t + 1, 1 - slot)
                    if is_tile(t - 2):
                        store_h(t - 2, slot)

                steps(sp, step)
                for e in range(2):
                    sp.wait_ge(hT_out[e], stored(tiles // 2, 32))

            @block.gpsimd
            def _(pool):
                for sem in (x2_done, x2_stored):
                    pool.sem_inc(sem, LEAD)

                def step(t, slot, uses):
                    if is_tile(t):
                        pool.wait_ge(y_done, done(t))
                        pool.wait_ge(x_in[slot], 16 * uses + 16)
                        pool.tensor_tensor(xt[slot][:, :], xt[slot][:, :], mix[slot][:, :], ALU.add).then_inc(x2_done, 1)
                        pool.wait_ge(x2_done, done(t))
                        pool.dma_start(s["x2"][t], xt[slot][:, :]).then_inc(x2_out[slot], 16)
                        pool.wait_ge(x2_out[slot], 16 * uses + 16)
                        pool.sem_inc(x2_stored, 1)

                steps(pool, step)

            @block.scalar
            def _(act):
                for sem in (m_sq, m_hi_done, roots_done, pool_scaled, mix_sq, mix_root, x2_sq, x2_root, hi_done):
                    act.sem_inc(sem, LEAD)

                def root(out, in_, width, sem):
                    act.activation(out, in_, ACT.Sqrt, scale=1.0 / width, bias=c["eps"][:, 0:1]).then_inc(sem, 1)

                def square_merged(t, slot, uses):
                    act.wait_ge(merged_in[slot], 16 * uses + 16)
                    act.wait_ge(m_sum, freed(t, 1))
                    act.activation(squares[:, :, :], merged[slot][:, :, :], ACT.Square).then_inc(m_sq, 1)

                def half_merged(t, slot):
                    act.wait_ge(m_scaled, done(t))
                    act.wait_ge(mix_mm_done, freed(t))
                    act.activation(m_hi[slot][:, :, :], merged[slot][:, :, :], ACT.Copy).then_inc(m_hi_done, 1)

                def step(t, slot, uses):
                    if is_tile(t):
                        act.wait_ge(ss_done, done(t))
                        act.wait_ge(recips_done, freed(t))
                        root(stat[:, slot, 0:2], ss_ps[:, slot, :], part_width, roots_done)
                    if is_tile(t + 1):
                        square_merged(t + 1, 1 - slot, uses + slot)
                        half_merged(t + 1, 1 - slot)
                    if is_tile(t - 1):
                        act.wait_ge(x2_done, done(t - 1))
                        act.activation(junk[:, :], xt[1 - slot][:, :], ACT.Square, accum_out=stat[:, 1 - slot, 7:8]).then_inc(x2_sq, 1)
                        act.wait_ge(x2_sq, done(t - 1))
                        root(stat[:, 1 - slot, 8:9], stat[:, 1 - slot, 7:8], d, x2_root)
                    if is_tile(t - 2):
                        act.wait_ge(turned, done(t - 2))
                        act.wait_ge(hT_out[slot], stored(uses - 1, 32))
                        act.activation(h_hi[slot][:, :, :].rearrange("p c t -> p (c t)"), turn_ps[:, :], ACT.Copy).then_inc(hi_done, 1)
                    if is_tile(t):
                        act.wait_ge(recips_done, done(t))
                        act.wait_ge(pool_mm_done, done(t))
                        act.wait_ge(x2_done, freed(t))
                        act.activation(mix[slot][:, :], pool_ps[:, :], ACT.Copy, scale=stat[:, slot, 2:3]).then_inc(pool_scaled, 1)
                        act.wait_ge(mix_done, done(t))
                        act.wait_ge(x2_sq, freed(t, 1))
                        act.activation(junk[:, :], mix[slot][:, :], ACT.Square, accum_out=stat[:, slot, 4:5]).then_inc(mix_sq, 1)
                        act.wait_ge(mix_sq, done(t))
                        root(stat[:, slot, 5:6], stat[:, slot, 4:5], d, mix_root)

                square_merged(0, 0, 0)
                half_merged(0, 0)
                steps(act, step)

            @block.vector
            def _(dve):
                for sem in (m_sum, m_scaled, m_lo_done, recips_done, mix_done, mix_recip, y_done, x2_recip, hn_done, lo_done):
                    dve.sem_inc(sem, LEAD)

                def prepare(t, slot):
                    dve.wait_ge(m_sq, done(t))
                    dve.wait_ge(ss_done, freed(t, 1))
                    dve.tensor_reduce(sums[:, :, :], squares[:, :, :].rearrange("p (h c) t -> p h t c", h=2), AX.X, ALU.add).then_inc(m_sum, 1)
                    dve.tensor_tensor(merged[slot][:, :, :], merged[slot][:, :, :], scales.unsqueeze(2).broadcast_to([P, kc, P]),
                                      ALU.mult).then_inc(m_scaled, 1)
                    dve.wait_ge(m_hi_done, done(t))
                    dve.wait_ge(mix_mm_done, freed(t))
                    dve.tensor_tensor(m_lo[slot][:, :, :], merged[slot][:, :, :], as_f32(m_hi[slot][:, :, :]), ALU.subtract).then_inc(m_lo_done, 1)

                prepare(0, 0)
                for k in range(kc):
                    dve.wait_ge(w_in_[k % 2], 16 * (k // 2 + 1))
                    dve.tensor_copy(w_hi[:, k, :], w_f[:, k % 2, :]).then_inc(wo_hi_done, 1)
                    dve.wait_ge(wo_hi_done, k + 1)
                    dve.tensor_tensor(w_lo[:, k, :], w_f[:, k % 2, :], as_f32(w_hi[:, k, :]), ALU.subtract).then_inc(wo_done, 1)
                dve.wait_ge(gains_in, 32)

                def step(t, slot, uses):
                    if is_tile(t):
                        dve.wait_ge(roots_done, done(t))
                        dve.reciprocal(stat[:, slot, 2:4], stat[:, slot, 0:2]).then_inc(recips_done, 1)
                    if is_tile(t - 1):
                        dve.wait_ge(mix_root, done(t - 1))
                        dve.reciprocal(stat[:, 1 - slot, 6:7], stat[:, 1 - slot, 5:6]).then_inc(mix_recip, 1)
                        dve.wait_ge(mix_recip, done(t - 1))
                        dve.scalar_tensor_tensor(out=mix[1 - slot][:, :], in0=mix[1 - slot][:, :], scalar=stat[:, 1 - slot, 6:7],
                                                 in1=gains[:, 0, :], op0=ALU.mult, op1=ALU.mult).then_inc(y_done, 1)
                    if is_tile(t + 1):
                        prepare(t + 1, 1 - slot)
                    if is_tile(t - 2):
                        dve.wait_ge(hi_done, done(t - 2))
                        dve.wait_ge(hT_out[slot], stored(uses - 1, 32))
                        dve.tensor_tensor(h_lo[slot][:, :, :].rearrange("p c t -> p (c t)"), turn_ps[:, :],
                                          as_f32(h_hi[slot][:, :, :].rearrange("p c t -> p (c t)")), ALU.subtract).then_inc(lo_done, 1)
                    if is_tile(t - 1):
                        dve.wait_ge(x2_root, done(t - 1))
                        dve.reciprocal(stat[:, 1 - slot, 9:10], stat[:, 1 - slot, 8:9]).then_inc(x2_recip, 1)
                        dve.wait_ge(x2_recip, done(t - 1))
                        dve.wait_ge(turned, freed(t - 1))
                        dve.scalar_tensor_tensor(out=hn[1 - slot][:, :], in0=xt[1 - slot][:, :], scalar=stat[:, 1 - slot, 9:10],
                                                 in1=gains[:, 1, :], op0=ALU.mult, op1=ALU.mult).then_inc(hn_done, 1)
                    if is_tile(t):
                        dve.wait_ge(pool_scaled, done(t))
                        dve.wait_ge(mix_mm_done, done(t))
                        dve.scalar_tensor_tensor(out=mix[slot][:, :], in0=attn_ps[:, :], scalar=stat[:, slot, 3:4], in1=mix[slot][:, :],
                                                 op0=ALU.mult, op1=ALU.add).then_inc(mix_done, 1)

                steps(dve, step)

            @block.tensor
            def _(pe):
                for sem in (ss_done, pool_mm_done, mix_mm_done, turned):
                    pe.sem_inc(sem, LEAD)

                def token_sums(t, slot):
                    pe.wait_ge(m_sum, done(t))
                    pe.wait_ge(roots_done, freed(t, 1))
                    for h in range(2):
                        m = pe.matmul(ss_ps[:, slot, h:h + 1], sums[:, h, :], c["ones"][:, 0:1], start=True, stop=True)
                    m.then_inc(ss_done, 1)

                def turn(t, slot):
                    pe.wait_ge(hn_done, done(t))
                    pe.wait_ge(lo_done, freed(t, 1))
                    for k in range(kc):
                        m = pe.transpose(turn_ps[:, k * P:(k + 1) * P], hn[slot][:, k * P:(k + 1) * P], c["ident"][:, :])
                    m.then_inc(turned, 1)

                def part_product(part, t, slot):
                    bank, sem, free = ((pool_ps, pool_mm_done, pool_scaled), (attn_ps, mix_mm_done, mix_done))[part]
                    pe.wait_ge(free, freed(t, 1))
                    for k in range(n_pool):
                        row = part * n_pool + k
                        for j, (m, w) in enumerate(((m_hi, w_hi), (m_hi, w_lo), (m_lo, w_hi))):
                            for half in range(d // BANK):
                                cols = slice(half * BANK, (half + 1) * BANK)
                                mm = pe.matmul(bank[:, cols], m[slot][:, row, :], w[:, row, cols],
                                               start=(k == 0 and j == 0), stop=(k == n_pool - 1 and j == 2))
                    mm.then_inc(sem, 1)

                def step(t, slot, uses):
                    if is_tile(t):
                        pe.wait_ge(m_lo_done, done(t))
                        part_product(0, t, slot)
                    if is_tile(t - 2):
                        turn(t - 2, slot)
                    if is_tile(t):
                        part_product(1, t, slot)
                    if is_tile(t + 1):
                        token_sums(t + 1, 1 - slot)

                token_sums(0, 0)
                pe.wait_ge(wo_done, kc)
                steps(pe, step)


def phase_up(nc, a, c, s):
    kc, seq = a["kc"], a["seq"]
    groups = seq // BANK
    n_ff = a["n_ff2"] // 2
    lead = 4
    with ExitStack() as stack:
        n = Names(nc, stack)
        hT = [[n.sb(f"h2T{i}_{j}", [P, kc, BANK], F32R) for j in range(groups)] for i in range(2)]
        w_f = [n.sb(f"wu_f{i}", [P, 2, kc, P]) for i in range(2)]
        w_hi = [n.sb(f"wu_hi{i}", [P, 2, kc, P], F32R) for i in range(2)]
        w_lo = [n.sb(f"wu_lo{i}", [P, 2, kc, P], F32R) for i in range(2)]
        conv = [[n.sb(f"conv{i}_{x}", [P, BANK]) for x in range(2)] for i in range(2)]
        f = [n.sb(f"f{i}", [P, BANK]) for i in range(2)]
        ps = [n.ps("gate_ps", [P, seq]), n.ps("value_ps", [P, seq])]
        w_in_, f_out = n.sems("wu_in", 2), n.sems("f_out", 2)
        h_in = n.sems("h2T_in", groups)
        names = ("wu_hi_done", "wu_done", "up_done", "tap_done", "conv_step", "silu_done", "f_done", "taps_done")
        wu_hi_done, wu_done, up_done, tap_done, conv_step, silu_done, f_done, taps_done = (n.sem(x) for x in names)
        w_cols = a["w_up"][0].rearrange("(c p) (h b n) -> b p h c n", p=P, h=2, n=P)
        taps = n.sb("taps", [P, 2, 4, 2, 1])
        columns = c["cols"][:, 0:4 * a["n_ff2"]].rearrange("p (k h j) -> p k h j", k=4, h=2)

        def column(kind, h, slot):
            return taps[:, slot, kind, h, :]

        with nc.Block() as block:

            @block.sync
            def _(sp):
                for sem in f_out:
                    sp.sem_inc(sem, 16)

                def load_w(j, slot):
                    sp.wait_ge(wu_done, freed(j))
                    for h in range(2):
                        sp.dma_start(w_f[slot][:, h, :, :], w_cols[j][:, h, :, :]).then_inc(w_in_[slot], 16)

                def load_h(j):
                    for i in range(2):
                        sp.dma_start(as_f32(hT[i][j][:, :, :]), s["h2T"][i][:, :, j * BANK:(j + 1) * BANK]).then_inc(h_in[j], 16)

                load_w(0, 0)
                load_h(0)
                load_w(1, 1)
                for j in range(1, groups):
                    load_h(j)

                def store(j, g):
                    sp.wait_ge(f_done, done(j * groups + g, lead))
                    sp.dma_start(s["f"][j][:, g * BANK:(g + 1) * BANK], f[g % 2][:, :]).then_inc(f_out[g % 2], 16)

                with sp.Fori(0, n_ff // 2 - 1) as i:
                    for e in range(2):
                        load_w(i * 2 + (2 + e), e)
                        for g in range(groups):
                            store(i * 2 + e, g)
                for e in range(2):
                    for g in range(groups):
                        store(n_ff - 2 + e, g)
                for e in range(2):
                    sp.wait_ge(f_out[e], stored(n_ff * groups // 2))

            def blocks_of(eng, block_step):
                with eng.Fori(0, n_ff // 2 - 1) as i:
                    for e in range(2):
                        block_step(i * 2 + e, i, e, False)
                for e in range(2):
                    block_step(n_ff - 2 + e, n_ff // 2 - 1, e, e == 1)

            @block.scalar
            def _(act):
                for sem in (tap_done, silu_done, wu_hi_done):
                    act.sem_inc(sem, LEAD)

                def half_w(j, i, slot):
                    act.wait_ge(w_in_[slot], 32 * i + 32)
                    act.wait_ge(up_done, freed(j * 2 * groups - 1, 2 * groups, 4 * groups))
                    act.activation(w_hi[slot][:, :, :, :], w_f[slot][:, :, :, :], ACT.Copy).then_inc(wu_hi_done, 1)

                def block_step(j, i, slot, last):
                    for g in range(groups):
                        count = j * groups + g
                        if g == 0 and not last:
                            half_w(j + 1, i + slot, 1 - slot)
                        for h in range(2):
                            act.wait_ge(up_done, done(count * 2 + h, 4 * groups))
                            act.wait_ge(taps_done, j + 1)
                            act.wait_ge(f_done, freed(count, 2, lead))
                            act.activation(conv[g % 2][h][:, :], ps[h][:, g * BANK:(g + 1) * BANK], ACT.Identity,
                                           scale=column(3, h, slot), bias=column(0, h, slot)).then_inc(tap_done, 1)
                        act.wait_ge(conv_step, 4 * count + 3)
                        act.activation(conv[g % 2][0][:, :], conv[g % 2][0][:, :], ACT.Silu).then_inc(silu_done, 1)

                half_w(0, 0, 0)
                blocks_of(act, block_step)

            @block.vector
            def _(dve):
                dve.sem_inc(f_done, lead)
                dve.sem_inc(wu_done, LEAD)

                def split_w(j, slot, first=False):
                    if not first:
                        dve.wait_ge(f_done, freed(j * groups, groups + 1, lead))
                    dve.tensor_scalar(taps[:, slot, :, :, :], columns[:, :, :, bass.ds(j, 1)], 1.0, None, ALU.mult).then_inc(taps_done, 1)
                    dve.wait_ge(wu_hi_done, done(j))
                    dve.wait_ge(up_done, freed(j * 2 * groups - 1, 2 * groups, 4 * groups))
                    dve.tensor_tensor(w_lo[slot][:, :, :, :], w_f[slot][:, :, :, :], as_f32(w_hi[slot][:, :, :, :]), ALU.subtract).then_inc(wu_done, 1)

                def block_step(j, i, slot, last):
                    for g in range(groups):
                        count = j * groups + g
                        if g == 0 and not last:
                            split_w(j + 1, 1 - slot)
                        for back, kind in ((1, 2), (2, 1)):
                            skip = back if g == 0 else 0
                            for h in range(2):
                                if back == 1:
                                    dve.wait_ge(tap_done, done(count * 2 + h))
                                else:
                                    dve.wait_ge(conv_step, 4 * count + 1 + h)
                                out = conv[g % 2][h][:, skip:]
                                dve.wait_ge(taps_done, j + 1)
                                dve.scalar_tensor_tensor(out=out, in0=ps[h][:, g * BANK - back + skip:(g + 1) * BANK - back],
                                                         scalar=column(kind, h, slot), in1=out, op0=ALU.mult, op1=ALU.add).then_inc(conv_step, 1)
                        dve.wait_ge(silu_done, done(count))
                        dve.wait_ge(conv_step, 4 * count + 4)
                        dve.wait_ge(f_out[g % 2], stored(j * (groups // 2) + g // 2))
                        dve.tensor_tensor(f[g % 2][:, :], conv[g % 2][0][:, :], conv[g % 2][1][:, :], ALU.mult).then_inc(f_done, 1)

                split_w(0, 0, first=True)
                blocks_of(dve, block_step)

            @block.tensor
            def _(pe):
                pe.sem_inc(up_done, 4 * groups)

                def block_step(j, i, slot, last):
                    pe.wait_ge(wu_done, done(j))
                    for g in range(groups):
                        pe.wait_ge(h_in[g], 32)
                        pe.wait_ge(f_done, freed(j * groups + g, groups - (1 if g < groups - 1 else 0), lead))
                        for h in range(2):
                            for k in range(kc):
                                for t, (w, x) in enumerate(((w_hi, 0), (w_hi, 1), (w_lo, 0))):
                                    m = pe.matmul(ps[h][:, g * BANK:(g + 1) * BANK], w[slot][:, h, k, :], hT[x][g][:, k, :],
                                                  start=(k == 0 and t == 0), stop=(k == kc - 1 and t == 2))
                            m.then_inc(up_done, 1)

                blocks_of(pe, block_step)


def phase_down(nc, a, c, s, out):
    seq, d = a["seq"], a["d"]
    groups, per = seq // BANK, BANK // P
    n_ff = a["n_ff2"] // 2
    with ExitStack() as stack:
        n = Names(nc, stack)
        w_f = [n.sb(f"wd_f{i}", [P, d]) for i in range(2)]
        w_hi = [n.sb(f"wd_hi{i}", [P, d], F32R) for i in range(2)]
        w_lo = [n.sb(f"wd_lo{i}", [P, d], F32R) for i in range(2)]
        f_f = [n.sb(f"fd_f{i}", [P, BANK]) for i in range(2)]
        f_hi = [n.sb(f"fd_hi{i}", [P, BANK], F32R) for i in range(2)]
        f_lo = [n.sb(f"fd_lo{i}", [P, BANK], F32R) for i in range(2)]
        gain = n.sb("gain_down", [P, d])
        junk = n.sb("junk_down", [P, d], mybir.dt.bfloat16)
        x2 = [n.sb(f"x2_{i}", [P, d]) for i in range(per)]
        y = [n.sb(f"y{i}", [P, d]) for i in range(per)]
        stat = n.sb("stat_down", [P, per, 4])
        ps = [n.ps(f"down_ps{i}", [P, d]) for i in range(per)]
        load_in = n.sems("down_in", 2)
        x2_in, y_out = n.sems("x2_in", per), n.sems("y_out", per)
        names = ("gain_down_in", "half_done", "split_done", "k_done", "sq_down", "root_down", "recip_down", "scaled_down", "added_down", "y_free")
        gain_in, half_done, split_done, k_done, sq_done, root_done, recip_done, scaled, added, y_free = (n.sem(x) for x in names)
        w_rows = a["w_down"][0].rearrange("(c p) n -> c p n", p=P)
        counted = n_ff - 1 + per

        def slot_free(i, k):
            return i * counted + ((1, per + 1)[k] if k < 2 else per + k)

        out_tiles = out[0].rearrange("(g t p) d -> g t p d", t=per, p=P)
        x2_tiles = s["x2"].rearrange("(g t) p d -> g t p d", t=per)

        with nc.Block() as block:

            @block.sync
            def _(sp):
                sp.dma_start(gain[:, :], a["norm_ffn_post"][0].partition_broadcast(P)).then_inc(gain_in, 16)
                with sp.Fori(0, groups) as i:
                    for k in range(n_ff):
                        sp.wait_ge(split_done, freed(i * n_ff + k))
                        sp.dma_start(w_f[k % 2][:, :], w_rows[k]).then_inc(load_in[k % 2], 16)
                        sp.dma_start(f_f[k % 2][:, :], s["f"][k][:, bass.ts(i, BANK)]).then_inc(load_in[k % 2], 16)
                        if k == 4:
                            for t in range(per):
                                sp.wait_ge(added, freed(i * per + t, per, per))
                                sp.dma_start(x2[t][:, :], x2_tiles[i, t]).then_inc(x2_in[t], 16)

            @block.gpsimd
            def _(pool):
                for sem in (added, y_free):
                    pool.sem_inc(sem, per)
                with pool.Fori(0, groups) as i:
                    for t in range(per):
                        pool.wait_ge(scaled, done(i * per + t, per))
                        pool.wait_ge(x2_in[t], 16 * i + 16)
                        pool.tensor_tensor(y[t][:, :], y[t][:, :], x2[t][:, :], ALU.add).then_inc(added, 1)
                        pool.wait_ge(added, done(i * per + t, per))
                        pool.dma_start(out_tiles[i, t], y[t][:, :]).then_inc(y_out[t], 16)
                    for t in range(per):
                        pool.wait_ge(y_out[t], 16 * i + 16)
                        pool.sem_inc(y_free, 1)

            @block.scalar
            def _(act):
                for sem in (half_done, sq_done):
                    act.sem_inc(sem, LEAD)

                def half(i, k):
                    act.wait_ge(load_in[k % 2], 32 * (i * (n_ff // 2) + k // 2) + 32)
                    act.wait_ge(k_done, slot_free(i, k))
                    act.activation(w_hi[k % 2][:, :], w_f[k % 2][:, :], ACT.Copy)
                    act.activation(f_hi[k % 2][:, :], f_f[k % 2][:, :], ACT.Copy).then_inc(half_done, 1)

                with act.Fori(0, groups) as i:
                    for k in range(n_ff):
                        half(i, k)
                    for t in range(per):
                        count = i * per + t
                        act.wait_ge(k_done, done(i * counted + (n_ff - 1 + t), per + 1))
                        act.wait_ge(sq_done, freed(count, 1, 2))
                        act.activation(junk[:, :], ps[t][:, :], ACT.Square, accum_out=stat[:, t, 0:1]).then_inc(sq_done, 1)
                        act.wait_ge(sq_done, done(count, 2))
                        act.activation(stat[:, t, 1:2], stat[:, t, 0:1], ACT.Sqrt, scale=1.0 / d, bias=c["eps"][:, 0:1]).then_inc(root_done, 1)

            @block.vector
            def _(dve):
                dve.sem_inc(split_done, LEAD)
                dve.sem_inc(scaled, per)
                dve.wait_ge(gain_in, 16)
                with dve.Fori(0, groups) as i:
                    for k in range(n_ff):
                        dve.wait_ge(half_done, done(i * n_ff + k))
                        dve.wait_ge(k_done, slot_free(i, k))
                        dve.tensor_tensor(w_lo[k % 2][:, :], w_f[k % 2][:, :], as_f32(w_hi[k % 2][:, :]), ALU.subtract)
                        dve.tensor_tensor(f_lo[k % 2][:, :], f_f[k % 2][:, :], as_f32(f_hi[k % 2][:, :]), ALU.subtract).then_inc(split_done, 1)
                    for t in range(per):
                        count = i * per + t
                        dve.wait_ge(root_done, count + 1)
                        dve.reciprocal(stat[:, t, 2:3], stat[:, t, 1:2]).then_inc(recip_done, 1)
                        dve.wait_ge(recip_done, count + 1)
                        dve.wait_ge(y_free, freed(count, per, per))
                        dve.scalar_tensor_tensor(out=y[t][:, :], in0=ps[t][:, :], scalar=stat[:, t, 2:3], in1=gain[:, :],
                                                 op0=ALU.mult, op1=ALU.mult).then_inc(scaled, 1)

            @block.tensor
            def _(pe):
                pe.sem_inc(k_done, per + 1)
                with pe.Fori(0, groups) as i:
                    for k in range(n_ff):
                        pe.wait_ge(split_done, done(i * n_ff + k))
                        for t in range(per):
                            if k == 0:
                                pe.wait_ge(scaled, freed(i * per + t, per, per))
                            for j, (x, w) in enumerate(((f_hi, w_hi), (f_hi, w_lo), (f_lo, w_hi))):
                                for half in range(d // BANK):
                                    cols = slice(half * BANK, (half + 1) * BANK)
                                    m = pe.matmul(ps[t][:, cols], x[k % 2][:, t * P:(t + 1) * P], w[k % 2][:, cols],
                                                  start=(k == 0 and j == 0), stop=(k == n_ff - 1 and j == 2))
                            if k == n_ff - 1:
                                m.then_inc(k_done, 1)
                        if k < n_ff - 1:
                            m.then_inc(k_done, 1)


def build(nc, a, out):
    d = a["x"].shape[2]
    seq = a["x"].shape[1]
    a.update(d=d, seq=seq, tiles=seq // P, kc=d // P, d_in=a["w_in"].shape[2], d_pool=a["pool_scale"].shape[1],
             d_attn=a["attn_scale"].shape[1], n_ff2=a["conv_b"].shape[1] // P, conv_width=a["conv_w"].shape[1])
    heads = a["d_attn"] // HEAD_DIM
    n_qk = 2 * a["d_attn"] // P
    scratch = lambda name, shape, dtype: nc.dram_tensor(name, shape, dtype, kind="Internal").ap()
    s = {
        "v": scratch("v_scratch", [heads, P, a["tiles"], 2, HEAD_DIM], F32),
        "qk": scratch("qk_scratch", [n_qk, 2, P, seq], F32),
        "pool": scratch("pool_scratch", [a["d_pool"] // P, P, seq], F32),
        "x2": scratch("x2_scratch", [a["tiles"], P, d], F32),
        "h2T": scratch("h2T_scratch", [2, P, a["kc"], seq], F32),
        "f": scratch("f_scratch", [a["n_ff2"] // 2, P, seq], F32),
        "merged": scratch("merged_scratch", [a["d_pool"] + a["d_attn"], seq], F32),
    }
    with ExitStack() as stack:
        n = Names(nc, stack)
        c = {"ident": n.sb("ident", [P, P]), "ident_r": n.sb("ident_r", [P, P], F32R), "not_before": n.sb("not_before", [P, P], F32R),
             "ones": n.sb("ones", [P, 2]), "eps": n.sb("eps", [P, 1]),
             "cols": n.sb("cols", [P, 4 * a["n_ff2"] + 8])}
        phase_setup(nc, a, c)
        with ExitStack() as inner:
            m = Names(nc, inner)
            hT = [m.sb(f"hT{i}", [P, a["kc"], seq], F32R) for i in range(2)]
            phase_values(nc, a, c, s, hT)
            phase_projections(nc, a, c, s, hT)
        phase_attention(nc, a, c, s)
        phase_mix(nc, a, c, s)
        phase_up(nc, a, c, s)
        phase_down(nc, a, c, s, out)




def kernel(**inputs):
    import numpy as _np
    import concourse.bacc as _bacc
    from concourse.bass_utils import run_bass_kernel_spmd as _run

    nc = _bacc.Bacc("TRN2", target_bir_lowering=False, num_devices=1)
    arrays, args = {}, {}
    for name, value in inputs.items():
        array = _np.ascontiguousarray(value)
        arrays[f"in_{name}"] = array
        args[name] = nc.dram_tensor(f"in_{name}", array.shape, mybir.dt.from_np(array.dtype), kind="ExternalInput").ap()
    out = nc.dram_tensor("layer_out", inputs["x"].shape, F32, kind="ExternalOutput").ap()
    build(nc, args, out)
    result = _run(nc, [arrays], core_ids=[0])
    return result.results[0]["layer_out"]
```

```python
from contextlib import ExitStack


import concourse.bass as bass
from concourse import mybir

F32 = mybir.dt.float32
F32R = mybir.dt.float32r
ALU = mybir.AluOpType
ACT = mybir.ActivationFunctionType
AX = mybir.AxisListType

P = 128
BANK = 512
EPS = 1e-6
MASKED_SCORE = -1e30
POOL_WINDOWS = (2, 4, 8, 16)
HEAD_DIM = 64
LEAD = 2


def done(step, lead=LEAD):
    return step + 1 + lead


def freed(step, ring=LEAD, lead=LEAD):
    return step + 1 + lead - ring


def stored(uses, each=16):
    return each * uses + 16


class Names:

    def __init__(self, nc, stack):
        self.nc, self.stack = nc, stack

    def sb(self, name, shape, dtype=F32):
        return self.stack.enter_context(self.nc.sbuf_tensor(name, shape, dtype))

    def ps(self, name, shape, dtype=F32):
        return self.stack.enter_context(self.nc.psum_tensor(name, shape, dtype))

    def sem(self, name):
        return self.stack.enter_context(self.nc.semaphore(name))

    def sems(self, name, n):
        return [self.sem(f"{name}{i}") for i in range(n)]


def as_f32(tile):
    return tile.bitcast(F32)


def phase_setup(nc, a, c):
    with ExitStack() as stack:
        n = Names(nc, stack)
        n_conv = a["n_ff2"]
        rows = n.sb("rows", [P, 6, P])
        not_before = n.sb("not_before_f", [P, P])
        cols_ps = n.ps("cols_ps", [P, BANK])
        rows_in, zeroed, ident_done, turned, cols_done = (
            n.sem(s) for s in ("rows_in", "zeroed", "ident_done", "turned", "cols_done"))
        with nc.Block() as block:

            @block.sync
            def _(sp):
                sp.dma_start(rows[0:n_conv, 0, :], a["conv_b"][0].rearrange("(j p) -> j p", p=P)).then_inc(rows_in, 16)
                for k in range(a["conv_width"]):
                    sp.dma_start(rows[0:n_conv, 1 + k, :], a["conv_w"][0, k].rearrange("(j p) -> j p", p=P)).then_inc(rows_in, 16)
                for half, name in enumerate(("pool_scale", "attn_scale")):
                    sp.dma_start(rows[4 * half:4 * half + 4, 4, :], a[name][0].rearrange("(j p) -> j p", p=P)).then_inc(rows_in, 16)
                sp.wait_ge(rows_in, 16 * (3 + a["conv_width"]))

            @block.gpsimd
            def _(pool):
                pool.memset(c["ident"][:, :], 0.0).then_inc(zeroed, 1)
                pool.wait_ge(zeroed, 1)
                pool.affine_select(out=c["ident"][:, :], in_=c["ident"][:, :], compare_op=ALU.not_equal, fill=1.0,
                                   base=0, pattern=[[-1, P]], channel_multiplier=1).then_inc(ident_done, 1)
                pool.memset(not_before[:, :], 0.0).then_inc(zeroed, 1)
                pool.wait_ge(zeroed, 2)
                pool.affine_select(out=not_before[:, :], in_=not_before[:, :], compare_op=ALU.is_gt, fill=MASKED_SCORE,
                                   base=0, pattern=[[-1, P]], channel_multiplier=1).then_inc(ident_done, 1)

            @block.tensor
            def _(pe):
                pe.wait_ge(rows_in, 16 * (3 + a["conv_width"]))
                pe.wait_ge(ident_done, 1)
                for k in range(1 + a["conv_width"]):
                    pe.transpose(cols_ps[:, k * n_conv:(k + 1) * n_conv], rows[0:n_conv, k, :],
                                 c["ident"][0:n_conv, 0:n_conv])
                pe.transpose(cols_ps[:, 4 * n_conv:4 * n_conv + 8], rows[0:8, 4, :], c["ident"][0:8, 0:8]).then_inc(turned, 1)

            @block.vector
            def _(dve):
                dve.memset(c["ones"][:, :], 1.0)
                dve.memset(c["eps"][:, :], EPS)
                dve.wait_ge(ident_done, 2)
                dve.tensor_copy(c["ident_r"][:, :], c["ident"][:, :])
                dve.tensor_copy(c["not_before"][:, :], not_before[:, :])
                dve.wait_ge(turned, 1)
                dve.tensor_copy(c["cols"][:, 0:4 * n_conv + 8], cols_ps[:, 0:4 * n_conv + 8]).then_inc(cols_done, 1)


def phase_values(nc, a, c, s, hT):
    tiles, kc, d = a["tiles"], a["kc"], a["d"]
    d_v = a["d_attn"]
    heads = d_v // HEAD_DIM
    v_cols = a["d_in"] - d_v
    with ExitStack() as stack:
        n = Names(nc, stack)
        wv_f = n.sb("wv_f", [P, 2, d_v])
        wv_hi, wv_lo = n.sb("wv_hi", [P, kc, d_v], F32R), n.sb("wv_lo", [P, kc, d_v], F32R)
        xt = [n.sb(f"xt{i}", [P, d]) for i in range(2)]
        squares = n.sb("squares", [P, d], mybir.dt.bfloat16)
        gain = n.sb("gain", [P, d])
        h_hi = [n.sb(f"h_hi{i}", [P, kc, P], F32R) for i in range(2)]
        h_lo = [n.sb(f"h_lo{i}", [P, kc, P], F32R) for i in range(2)]
        v_out = n.sb("v_out", [P, 2, heads, 2, HEAD_DIM], F32R)
        stat = n.sb("stat", [P, 2, 4])
        turn_ps = [n.ps(f"turn_ps{i}", [P, kc * P]) for i in range(2)]
        v_ps = [n.ps(f"v_ps{i}", [P, d_v]) for i in range(2)]
        wv_in, x_in = n.sems("wv_in", 2), n.sems("x_in", 2)
        hT_out, v_stored = n.sems("hT_out", 2), n.sems("v_stored", 2)
        names = ("gain_in", "wv_hi_done", "wv_done", "sq_done", "root_done", "recip_done", "xn_done", "turn_done",
                 "h_hi_done", "h_lo_done", "v_done", "v_hi_done", "v_lo_done")
        (gain_in, wv_hi_done, wv_done, sq_done, root_done, recip_done, xn_done, turn_done,
         h_hi_done, h_lo_done, v_done, v_hi_done, v_lo_done) = (n.sem(x) for x in names)
        x_tiles = a["x"][0].rearrange("(t p) d -> t p d", p=P)
        w_v = a["w_in"][0].rearrange("(c p) n -> p c n", p=P)

        with nc.Block() as block:

            @block.sync
            def _(sp):
                for sem in hT_out + v_stored:
                    sp.sem_inc(sem, 16)

                def load_x(t, slot):
                    sp.wait_ge(turn_done, freed(t))
                    sp.dma_start(xt[slot][:, :], x_tiles[t]).then_inc(x_in[slot], 16)

                load_x(0, 0)
                sp.dma_start(gain[:, :], a["norm_mix_pre"][0].partition_broadcast(P)).then_inc(gain_in, 16)
                for k in range(kc):
                    if k >= 2:
                        sp.wait_ge(wv_done, k - 1)
                    sp.dma_start(wv_f[:, k % 2, :], w_v[:, k, v_cols:]).then_inc(wv_in[k % 2], 16)
                    if k == 1:
                        load_x(1, 1)

                def store_h(t, slot):
                    sp.wait_ge(h_lo_done, done(t))
                    sp.dma_start(as_f32(hT[0][:, :, bass.ts(t, P)]), as_f32(h_hi[slot][:, :, :])).then_inc(hT_out[slot], 16)
                    sp.dma_start(as_f32(hT[1][:, :, bass.ts(t, P)]), as_f32(h_lo[slot][:, :, :])).then_inc(hT_out[slot], 16)

                def store_v(t, slot):
                    sp.wait_ge(v_lo_done, done(t))
                    sp.dma_start(s["v"][:, :, t, :, :].rearrange("h p a e -> p h a e"),
                                 as_f32(v_out[:, slot, :, :, :])).then_inc(v_stored[slot], 16)

                load_x(2, 0)
                store_h(0, 0)
                with sp.Fori(0, tiles // 2 - 2) as i:
                    for e in range(2):
                        load_x(i * 2 + (3 + e), 1 - e)
                        store_h(i * 2 + (1 + e), 1 - e)
                        store_v(i * 2 + e, e)
                load_x(tiles - 1, 1)
                for t in range(tiles - 3, tiles):
                    store_h(t, t % 2)
                    store_v(t - 1, (t - 1) % 2)
                store_v(tiles - 1, 1)
                for e in range(2):
                    sp.wait_ge(hT_out[e], stored(tiles // 2, 32))
                    sp.wait_ge(v_stored[e], stored(tiles // 2))

            @block.scalar
            def _(act):
                for sem in (sq_done, root_done, h_hi_done, v_hi_done):
                    act.sem_inc(sem, LEAD)

                def statistics(t, uses, slot):
                    act.wait_ge(x_in[slot], 16 * uses + 16)
                    act.wait_ge(sq_done, freed(t, 1))
                    act.activation(squares[:, :], xt[slot][:, :], ACT.Square, accum_out=stat[:, slot, 0:1]).then_inc(sq_done, 1)
                    act.wait_ge(sq_done, done(t))
                    act.activation(stat[:, slot, 1:2], stat[:, slot, 0:1], ACT.Sqrt, scale=1.0 / d,
                                   bias=c["eps"][:, 0:1]).then_inc(root_done, 1)

                def h_half(t, uses, slot):
                    act.wait_ge(turn_done, done(t))
                    act.wait_ge(v_done, freed(t))
                    act.wait_ge(hT_out[slot], stored(uses, 32))
                    act.activation(h_hi[slot][:, :, :].rearrange("p c t -> p (c t)"), turn_ps[slot][:, :],
                                   ACT.Copy).then_inc(h_hi_done, 1)

                def v_half(t, uses, slot):
                    act.wait_ge(v_done, done(t))
                    act.wait_ge(v_stored[slot], stored(uses))
                    act.activation(v_out[:, slot, :, 0, :], v_ps[slot][:, :].rearrange("p (h e) -> p h e", h=heads),
                                   ACT.Copy).then_inc(v_hi_done, 1)

                statistics(0, 0, 0)
                statistics(1, 0, 1)
                h_half(0, 0, 0)
                with act.Fori(0, tiles // 2 - 1) as i:
                    for e in range(2):
                        statistics(i * 2 + (2 + e), i + 1, e)
                        h_half(i * 2 + (1 + e), i + e, 1 - e)
                        v_half(i * 2 + e, i, e)
                h_half(tiles - 1, tiles // 2 - 1, 1)
                for e in range(2):
                    v_half(tiles - 2 + e, tiles // 2 - 1, e)

            @block.vector
            def _(dve):
                for sem in (recip_done, xn_done, h_lo_done, v_lo_done):
                    dve.sem_inc(sem, LEAD)
                for k in range(kc):
                    dve.wait_ge(wv_in[k % 2], 16 * (k // 2 + 1))
                    dve.tensor_copy(wv_hi[:, k, :], wv_f[:, k % 2, :]).then_inc(wv_hi_done, 1)
                    dve.wait_ge(wv_hi_done, k + 1)
                    dve.tensor_tensor(wv_lo[:, k, :], wv_f[:, k % 2, :], as_f32(wv_hi[:, k, :]), ALU.subtract).then_inc(wv_done, 1)
                dve.wait_ge(gain_in, 16)

                def scale_x(t, slot):
                    dve.wait_ge(root_done, done(t))
                    dve.reciprocal(stat[:, slot, 2:3], stat[:, slot, 1:2]).then_inc(recip_done, 1)
                    dve.wait_ge(recip_done, done(t))
                    dve.scalar_tensor_tensor(out=xt[slot][:, :], in0=xt[slot][:, :], scalar=stat[:, slot, 2:3],
                                             in1=gain[:, :], op0=ALU.mult, op1=ALU.mult).then_inc(xn_done, 1)

                def h_half(t, uses, slot):
                    dve.wait_ge(h_hi_done, done(t))
                    dve.wait_ge(v_done, freed(t))
                    dve.wait_ge(hT_out[slot], stored(uses, 32))
                    dve.tensor_tensor(h_lo[slot][:, :, :].rearrange("p c t -> p (c t)"), turn_ps[slot][:, :],
                                      as_f32(h_hi[slot][:, :, :].rearrange("p c t -> p (c t)")), ALU.subtract).then_inc(h_lo_done, 1)

                def v_half(t, uses, slot):
                    dve.wait_ge(v_hi_done, done(t))
                    dve.wait_ge(v_stored[slot], stored(uses))
                    dve.tensor_tensor(v_out[:, slot, :, 1, :], v_ps[slot][:, :].rearrange("p (h e) -> p h e", h=heads),
                                      as_f32(v_out[:, slot, :, 0, :]), ALU.subtract).then_inc(v_lo_done, 1)

                scale_x(0, 0)
                scale_x(1, 1)
                h_half(0, 0, 0)
                with dve.Fori(0, tiles // 2 - 1) as i:
                    for e in range(2):
                        scale_x(i * 2 + (2 + e), e)
                        h_half(i * 2 + (1 + e), i + e, 1 - e)
                        v_half(i * 2 + e, i, e)
                h_half(tiles - 1, tiles // 2 - 1, 1)
                for e in range(2):
                    v_half(tiles - 2 + e, tiles // 2 - 1, e)

            @block.tensor
            def _(pe):
                for sem in (turn_done, v_done):
                    pe.sem_inc(sem, LEAD)

                def turn(t, slot):
                    pe.wait_ge(xn_done, done(t))
                    pe.wait_ge(h_lo_done, freed(t))
                    for k in range(kc):
                        m = pe.transpose(turn_ps[slot][:, k * P:(k + 1) * P], xt[slot][:, k * P:(k + 1) * P], c["ident"][:, :])
                    m.then_inc(turn_done, 1)

                def values(t, slot):
                    pe.wait_ge(h_lo_done, done(t))
                    pe.wait_ge(v_lo_done, freed(t))
                    for k in range(kc):
                        for j, (h, w) in enumerate(((h_hi, wv_hi), (h_hi, wv_lo), (h_lo, wv_hi))):
                            m = pe.matmul(v_ps[slot][:, :], h[slot][:, k, :], w[:, k, :],
                                          start=(k == 0 and j == 0), stop=(k == kc - 1 and j == 2))
                    m.then_inc(v_done, 1)

                turn(0, 0)
                pe.wait_ge(wv_done, kc)
                with pe.Fori(0, tiles // 2 - 1) as i:
                    for e in range(2):
                        turn(i * 2 + (e + 1), 1 - e)
                        values(i * 2 + e, e)
                turn(tiles - 1, 1)
                for e in range(2):
                    values(tiles - 2 + e, e)


def phase_projections(nc, a, c, s, hT):
    kc, seq, groups = a["kc"], a["seq"], a["seq"] // BANK
    n_u, n_qk = a["d_pool"] // P, 2 * a["d_attn"] // P
    blocks = n_u + n_qk
    pad = max(POOL_WINDOWS)
    with ExitStack() as stack:
        n = Names(nc, stack)
        w_f = n.sb("w_f", [P, 2, kc, P])
        w_hi = [n.sb(f"w_hi{i}", [P, kc, P], F32R) for i in range(2)]
        w_lo = [n.sb(f"w_lo{i}", [P, kc, P], F32R) for i in range(2)]
        u = n.sb("u", [P, pad + seq])
        run = n.sb("run", [P, 2, pad + seq])
        pooled = n.sb("pooled", [P, seq])
        w_pool = n.sb("w_pool_sb", [P, n_u, P])
        pool_out = n.sb("pool_out", [P, 2, BANK])
        ramp = n.sb("ramp", [P, pad])
        qk_hi, qk_lo = n.sb("qk_hi", [P, 2, BANK], F32R), n.sb("qk_lo", [P, 2, BANK], F32R)
        out_ps = [n.ps(f"out_ps{i}", [P, BANK]) for i in range(8)]
        w_in_, qk_out, group_out = n.sems("w_in", 2), n.sems("qk_out", 2), n.sems("group_out", 2)
        (w_pool_in, w_hi_done, w_lo_done, out_done, u_read, qk_read, pool_step, pool_done, group_done, group_read, hi_done) = (
            n.sem(x) for x in ("w_pool_in", "w_hi_done", "w_lo_done", "out_done", "u_read", "qk_read", "pool_step",
                               "pool_done", "group_done", "group_read", "hi_done"))
        w_cols = a["w_in"][0].rearrange("(c p) (b n) -> b p c n", p=P, n=P)

        def half_of(b):
            return (4 if 1 <= b <= n_u + 1 else 0) if b <= n_u + 1 else 4 * (b % 2)

        def half_of_qk(i, e):
            return 4 if isinstance(i, int) and i == 0 else 4 * e

        with nc.Block() as block:

            @block.sync
            def _(sp):
                for sem in qk_out:
                    sp.sem_inc(sem, 16)

                def load_w(b, slot):
                    sp.wait_ge(w_lo_done, freed(b))
                    sp.dma_start(w_f[:, slot, :, :], w_cols[b]).then_inc(w_in_[slot], 16)

                def store_group(g):
                    for j in range(groups):
                        sp.wait_ge(group_read, g * groups + j + 1)
                        sp.dma_start(s["merged"][g * P:(g + 1) * P, j * BANK:(j + 1) * BANK], pool_out[:, j % 2, :]).then_inc(group_out[j % 2], 16)

                def store(b):
                    for j in range(groups):
                        sp.wait_ge(qk_read, b * groups + j + 1)
                        sp.dma_start(s["qk"][b, 0, :, j * BANK:(j + 1) * BANK], as_f32(qk_hi[:, j % 2, :])).then_inc(qk_out[j % 2], 16)
                        sp.dma_start(s["qk"][b, 1, :, j * BANK:(j + 1) * BANK], as_f32(qk_lo[:, j % 2, :])).then_inc(qk_out[j % 2], 16)

                load_w(0, 0)
                load_w(1, 1)
                sp.dma_start(w_pool[:, :, :], a["w_pool"][0].rearrange("g c d -> c g d")).then_inc(w_pool_in, 16)
                for g in range(n_u):
                    load_w(g + 2, g % 2)
                    if g == n_u - 1:
                        store(0)
                    store_group(g)
                load_w(n_u + 2, 0)
                store(1)
                load_w(n_u + 3, 1)
                with sp.Fori(1, n_qk // 2 - 1) as i:
                    for e in range(2):
                        store(i * 2 + e)
                        load_w(i * 2 + (n_u + 2 + e), e)
                for e in range(2):
                    store(n_qk - 2 + e)
                for e in range(2):
                    sp.wait_ge(qk_out[e], stored(n_qk * groups // 2, 32))
                    sp.wait_ge(group_out[e], 16 * n_u * groups // 2)

            @block.scalar
            def _(act):
                act.sem_inc(hi_done, LEAD)

                def copy_u(b):
                    for j in range(groups):
                        act.wait_ge(out_done, done(b * groups + j, 8))
                        if j == 0 and b >= 1:
                            act.wait_ge(pool_done, b)
                        act.activation(u[:, pad + j * BANK:pad + (j + 1) * BANK], out_ps[half_of(b) + j][:, :], ACT.Copy).then_inc(u_read, 1)

                def copy_group(g):
                    for j in range(groups):
                        count = g * groups + j
                        act.wait_ge(group_done, count + 1)
                        if count >= 2:
                            act.wait_ge(group_out[j % 2], 16 * (count // 2))
                        act.activation(pool_out[:, j % 2, :], out_ps[j][:, :], ACT.Copy).then_inc(group_read, 1)

                def half_qk(i, e):
                    for j in range(groups):
                        count = (i * 2 + e) * groups + j
                        act.wait_ge(out_done, done(count + n_u * groups, 8))
                        act.wait_ge(qk_out[j % 2], stored((i * 2 + e) * (groups // 2) + j // 2, 32))
                        act.activation(qk_hi[:, j % 2, :], out_ps[half_of_qk(i, e) + j][:, :], ACT.Copy).then_inc(hi_done, 1)

                copy_u(0)
                for g in range(n_u - 1):
                    copy_u(g + 1)
                    copy_group(g)
                half_qk(0, 0)
                copy_group(n_u - 1)
                half_qk(0, 1)
                with act.Fori(1, n_qk // 2) as i:
                    for e in range(2):
                        half_qk(i, e)

            @block.vector
            def _(dve):
                for sem in (w_hi_done, w_lo_done):
                    dve.sem_inc(sem, LEAD)

                def split_w(b, i, slot):
                    dve.wait_ge(w_in_[slot], 16 * i + 16)
                    dve.wait_ge(out_done, done(b * groups - 1 - groups, 8))
                    dve.tensor_copy(w_hi[slot][:, :, :], w_f[:, slot, :, :]).then_inc(w_hi_done, 1)
                    dve.wait_ge(w_hi_done, done(b))
                    dve.tensor_tensor(w_lo[slot][:, :, :], w_f[:, slot, :, :], as_f32(w_hi[slot][:, :, :]), ALU.subtract).then_inc(w_lo_done, 1)

                steps = [0]

                def step(ins):
                    steps[0] += 1
                    ins.then_inc(pool_step, 1)
                    dve.wait_ge(pool_step, steps[0])

                split_w(0, 0, 0)
                split_w(1, 0, 1)
                step(dve.memset(u[:, 0:pad], 0.0))
                step(dve.memset(run[:, 0, 0:pad], 0.0))
                step(dve.memset(run[:, 1, 0:pad], 0.0))
                for b, window in enumerate(POOL_WINDOWS):
                    for t in range(pad):
                        last = dve.memset(ramp[:, t:t + 1], 1.0 / min(t + 1, window))
                    step(last)
                    dve.wait_ge(u_read, (b + 1) * groups)
                    src, width, side = u[:, :], 1, 0
                    while width < window:
                        dst = run[:, side, :]
                        step(dve.tensor_tensor(dst[:, pad:], src[:, pad:], src[:, pad - width:pad + seq - width], ALU.add))
                        src, width, side = dst, 2 * width, 1 - side
                    other = run[:, side, :]
                    step(dve.tensor_tensor(other[:, pad:2 * pad], src[:, pad:2 * pad], ramp[:, :], ALU.mult))
                    if b >= 1:
                        dve.wait_ge(group_done, groups * b)
                    step(dve.tensor_tensor(pooled[:, 0:pad], other[:, pad:2 * pad], u[:, pad:2 * pad], ALU.subtract))
                    dve.scalar_tensor_tensor(out=pooled[:, pad:], in0=src[:, 2 * pad:], scalar=1.0 / window,
                                             in1=u[:, 2 * pad:], op0=ALU.mult, op1=ALU.subtract).then_inc(pool_done, 1)
                    split_w(b + 2, (b + 2) // 2, b % 2)

                def split_qk(i, e):
                    for j in range(groups):
                        count = (i * 2 + e) * groups + j
                        dve.wait_ge(hi_done, done(count))
                        dve.wait_ge(qk_out[j % 2], stored((i * 2 + e) * (groups // 2) + j // 2, 32))
                        dve.tensor_tensor(qk_lo[:, j % 2, :], out_ps[half_of_qk(i, e) + j][:, :],
                                          as_f32(qk_hi[:, j % 2, :]), ALU.subtract).then_inc(qk_read, 1)

                for e in range(2):
                    split_qk(0, e)
                    split_w(n_u + 2 + e, n_u // 2 + 1, e)
                with dve.Fori(1, n_qk // 2 - 1) as i:
                    for e in range(2):
                        split_qk(i, e)
                        split_w(i * 2 + (n_u + 2 + e), i + (n_u // 2 + 1), e)
                for e in range(2):
                    split_qk(n_qk // 2 - 1, e)

            @block.tensor
            def _(pe):
                pe.sem_inc(out_done, 8)

                def block_product(b, slot, half, read, count):
                    pe.wait_ge(w_lo_done, done(b))
                    for j in range(groups):
                        if read is not None:
                            pe.wait_ge(read, count + j + 1)
                        for k in range(kc):
                            for t, (w, h) in enumerate(((w_hi, 0), (w_hi, 1), (w_lo, 0))):
                                m = pe.matmul(out_ps[half + j][:, :], w[slot][:, k, :], hT[h][:, k, j * BANK:(j + 1) * BANK],
                                              start=(k == 0 and t == 0), stop=(k == kc - 1 and t == 2))
                        m.then_inc(out_done, 1)

                def group_product(g, read, count):
                    pe.wait_ge(pool_done, g + 1)
                    for j in range(groups):
                        pe.wait_ge(read, count + j + 1)
                        pe.matmul(out_ps[j][:, :], w_pool[:, g, :], pooled[:, j * BANK:(j + 1) * BANK],
                                  start=True, stop=True).then_inc(group_done, 1)

                block_product(0, 0, half_of(0), None, 0)
                block_product(1, 1, half_of(1), None, 0)
                pe.wait_ge(w_pool_in, 16)
                group_product(0, u_read, 0)
                for g in range(1, n_u):
                    block_product(g + 1, (g + 1) % 2, half_of(g + 1), u_read, g * groups)
                    group_product(g, group_read, (g - 1) * groups)
                block_product(n_u + 1, (n_u + 1) % 2, half_of(n_u + 1), qk_read, 0)
                pe.wait_ge(group_read, n_u * groups)
                with pe.Fori(0, n_qk // 2 - 1) as i:
                    for e in range(2):
                        block_product(i * 2 + (n_u + 2 + e), e, 4 * e, qk_read, (i * 2 + e) * groups)


def phase_attention(nc, a, c, s, wide):
    tiles, seq = a["tiles"], a["seq"]
    per = BANK // P
    heads = a["d_attn"] // HEAD_DIM
    scale = HEAD_DIM ** -0.5
    lead = 8
    z_ring, stick_in, wT_ring = 4, 4, 2
    weight_lag, turn_lag, hi_lag, lo_lag, values_lag, read_lag = 1, 3, 3, 4, 5, 6
    units = [(e, q, k * BANK, min((q + 1) * P - k * BANK, BANK), k == q // per, k == 0)
             for e in range(2) for q in range(tiles) for k in range(q // per, -1, -1)]
    total = len(units)
    per_head = total // 2
    last_unit = {(e, q): i for i, (e, q, _, _, _, last) in enumerate(units) if last}
    with ExitStack() as stack:
        n = Names(nc, stack)
        q_hi = [n.sb(f"q_hi{i}", [P, seq], F32R) for i in range(2)]
        q_lo = [n.sb(f"q_lo{i}", [P, seq], F32R) for i in range(2)]
        k_both = [n.sb(f"k_both{i}", [P, seq], F32R) for i in range(2)]
        v_both = [n.sb(f"v_both{i}", [P, tiles, 2, HEAD_DIM], F32R) for i in range(2)]
        rest = [n.sb(f"rest{i}", [P, BANK]) for i in range(stick_in)]
        beta = [n.sb(f"beta{i}", [P, BANK]) for i in range(stick_in)]
        stick = [n.sb(f"stick{i}", [P, seq + 1]) for i in range(2)]
        weight = [n.sb(f"weight{i}", [P, BANK]) for i in range(stick_in)]
        wT_hi = [n.sb(f"wT_hi{i}", [P, BANK], F32R) for i in range(wT_ring)]
        wT_lo = [n.sb(f"wT_lo{i}", [P, BANK], F32R) for i in range(wT_ring)]
        mixed = [n.sb(f"mixed{i}", [HEAD_DIM, seq]) for i in range(2)]
        wo_f = n.sb("wo_f", [P, 2, a["d"]])
        z_ps = [n.ps(f"z_ps{i}", [P, BANK]) for i in range(z_ring)]
        wT_ps = [n.ps(f"wT_ps{i}", [P, BANK]) for i in range(wT_ring)]
        o_ps = [n.ps(f"o_ps{i}", [HEAD_DIM, P]) for i in range(2)]
        head_in, mixed_out = n.sems("head_in", 2), n.sems("mixed_out", 2)
        head_start, one_done, wo_hi_done, wo_done = (n.sem(x) for x in ("head_start", "one_done", "wo_hi_done", "wo_done"))
        wo_in = n.sems("wo_in", 2)
        wo_rows = a["w_out"][0].rearrange("(c p) n -> c p n", p=P)
        (z_done, rest_done, beta_done, stick_done, weight_done, turned, hi_done, lo_done, pv_done, o_read) = (
            n.sem(x) for x in ("z_done", "rest_done", "beta_done", "stick_done", "weight_done",
                               "wT_turned", "wT_hi_done", "wT_lo_done", "pv_done", "o_read"))

        pairs = heads // 2
        last_read = max(weight_lag, turn_lag, hi_lag, lo_lag, values_lag, read_lag)

        def steps(eng, step):
            def behind_of(i, u):
                def behind(lag):
                    v = u - lag
                    if v < 0 and isinstance(i, int) or v >= total:
                        return None
                    return (v, i * total + v) if v >= 0 else (v + total, i * total + v)
                return behind

            for u in range(total):
                step(0, u, behind_of(0, u))
            with eng.Fori(1, pairs) as i:
                for u in range(total):
                    step(i, u, behind_of(i, u))
            for u in range(total, total + last_read):
                step(pairs - 1, u, behind_of(pairs - 1, u))

        def col(q, key):
            return seq - (q + 1) * P + key

        with nc.Block() as block:

            @block.sync
            def _(sp):
                for sem in mixed_out:
                    sp.sem_inc(sem, 16)

                def load_head(pair, e, sem, first=0, end=tiles):
                    half, cols = slice(e * HEAD_DIM, (e + 1) * HEAD_DIM), slice(first * P, end * P)
                    top, bottom = slice(0, HEAD_DIM), slice(HEAD_DIM, P)
                    for part, hi_lo, dst in ((top, 0, q_hi), (bottom, 0, q_hi), (top, 1, q_lo), (bottom, 1, q_lo)):
                        sp.dma_start(as_f32(dst[e][part, cols]), s["qk"][pair, hi_lo, half, cols]).then_inc(sem, 16)
                    for part, hi_lo in ((top, 0), (bottom, 1)):
                        sp.dma_start(as_f32(k_both[e][part, cols]), s["qk"][pair + heads // 2, hi_lo, half, cols]).then_inc(sem, 16)
                    sp.dma_start(as_f32(v_both[e][:, first:end, :, :]), s["v"][pair * 2 + e][:, first:end, :, :]).then_inc(sem, 16)

                def store_head(pair, e):
                    sp.wait_ge(o_read, done((pair * 2 + e + 1) * tiles - 1, lead))
                    sp.dma_start(s["merged"][bass.ds(a["d_pool"] + (pair * 2 + e) * HEAD_DIM, HEAD_DIM), :], mixed[e][:, :]).then_inc(mixed_out[e], 16)

                load_head(0, 0, head_start, 0, per)
                load_head(0, 0, head_in[0], per, tiles)
                load_head(0, 1, head_in[1])
                for k in range(a["kc"]):
                    if k >= 2:
                        sp.wait_ge(wo_done, k - 1)
                    sp.dma_start(wo_f[:, k % 2, :], wo_rows[k]).then_inc(wo_in[k % 2], 16)
                with sp.Fori(0, heads // 2 - 1) as i:
                    for e in range(2):
                        sp.wait_ge(pv_done, done(i * total + (e + 1) * per_head - 1, lead))
                        load_head(i + 1, e, head_in[e])
                        store_head(i, e)
                for e in range(2):
                    store_head(heads // 2 - 1, e)
                for e in range(2):
                    sp.wait_ge(mixed_out[e], stored(heads // 2))

            @block.scalar
            def _(act):
                for sem in (rest_done, beta_done, hi_done, o_read):
                    act.sem_inc(sem, lead)

                def step(i, u, behind):
                    if u < total:
                        t, w = i * total + u, units[u][3]
                        act.wait_ge(z_done, done(t, lead))
                        act.wait_ge(stick_done, freed(t, stick_in, lead))
                        act.activation(rest[u % stick_in][:, 0:w], z_ps[u % z_ring][:, 0:w], ACT.Sigmoid, scale=-scale).then_inc(rest_done, 1)
                        act.wait_ge(weight_done, freed(t, stick_in, lead))
                        act.activation(beta[u % stick_in][:, 0:w], z_ps[u % z_ring][:, 0:w], ACT.Sigmoid, scale=scale).then_inc(beta_done, 1)
                    if behind(hi_lag):
                        v, t = behind(hi_lag)
                        w = units[v][3]
                        act.wait_ge(turned, done(t, lead))
                        act.wait_ge(pv_done, freed(t, wT_ring, lead))
                        act.activation(wT_hi[v % wT_ring][:, 0:w], wT_ps[v % wT_ring][:, 0:w], ACT.Copy).then_inc(hi_done, 1)
                    if behind(read_lag) and units[behind(read_lag)[0]][5]:
                        v, t = behind(read_lag)
                        e, q = units[v][0:2]
                        act.wait_ge(pv_done, done(t, lead))
                        if q == 0:
                            act.wait_ge(mixed_out[e], stored(i if u >= read_lag else i - 1))
                        act.activation(mixed[e][:, q * P:(q + 1) * P], o_ps[q % 2][:, :], ACT.Copy).then_inc(o_read, 1)

                steps(act, step)

            @block.gpsimd
            def _(pool):
                pool.sem_inc(weight_done, lead)

                def step(i, u, behind):
                    if behind(weight_lag):
                        v, t = behind(weight_lag)
                        e, q, key, w, first, _ = units[v]
                        pool.wait_ge(beta_done, done(t, lead))
                        pool.wait_ge(stick_done, done(t, lead))
                        pool.wait_ge(turned, freed(t, stick_in, lead))
                        at = col(q, key) + 1
                        pool.tensor_tensor(weight[v % stick_in][:, 0:w], beta[v % stick_in][:, 0:w], stick[q % 2][:, at:at + w],
                                           ALU.mult).then_inc(weight_done, 1)

                steps(pool, step)

            @block.vector
            def _(dve):
                for sem in (stick_done, lo_done):
                    dve.sem_inc(sem, lead)
                for i in range(2):
                    dve.memset(stick[i][:, seq:seq + 1], 1.0).then_inc(one_done, 1)
                dve.wait_ge(one_done, 2)

                def split_wo(k):
                    dve.wait_ge(wo_in[k % 2], 16 * (k // 2 + 1))
                    for h in range(2):
                        dve.tensor_copy(wide[h][:, k, :], wo_f[:, k % 2, h * BANK:(h + 1) * BANK]).then_inc(wo_hi_done, 1)
                    for h in range(2):
                        dve.wait_ge(wo_hi_done, 2 * k + h + 1)
                        last = dve.tensor_tensor(wide[2 + h][:, k, :], wo_f[:, k % 2, h * BANK:(h + 1) * BANK], as_f32(wide[h][:, k, :]), ALU.subtract)
                    last.then_inc(wo_done, 1)

                def step(i, u, behind):
                    if isinstance(i, int) and i == 0 and per_head <= u < per_head + 4 * a["kc"] and u % 4 == 0:
                        split_wo((u - per_head) // 4)
                    if behind(lo_lag):
                        v, t = behind(lo_lag)
                        w = units[v][3]
                        dve.wait_ge(hi_done, done(t, lead))
                        dve.wait_ge(pv_done, freed(t, wT_ring, lead))
                        dve.tensor_tensor(wT_lo[v % wT_ring][:, 0:w], wT_ps[v % wT_ring][:, 0:w], as_f32(wT_hi[v % wT_ring][:, 0:w]),
                                          ALU.subtract).then_inc(lo_done, 1)
                    if u < total:
                        e, q, key, w, first, _ = units[u]
                        t = i * total + u
                        dve.wait_ge(rest_done, done(t, lead))
                        if first:
                            if e or q >= 2:
                                before = last_unit[(e, q - 2)] if q >= 2 else last_unit[(0, tiles - 2 + q)]
                                dve.wait_ge(weight_done, done(i * total + before, lead))
                            elif not isinstance(i, int):
                                dve.wait_ge(weight_done, done(i * total + (last_unit[(1, tiles - 2 + q)] - total), lead))
                            start = 1.0
                        else:
                            dve.wait_ge(stick_done, freed(t, 1, lead))
                            start = stick[q % 2][:, col(q, key) + w:col(q, key) + w + 1]
                        at = col(q, key)
                        backwards = rest[u % stick_in][:, 0:w][:, ::-1]
                        dve.tensor_tensor_scan(stick[q % 2][:, at:at + w][:, ::-1], backwards, backwards, start,
                                               ALU.mult, ALU.bypass).then_inc(stick_done, 1)

                steps(dve, step)

            @block.tensor
            def _(pe):
                for sem in (z_done, turned, pv_done):
                    pe.sem_inc(sem, lead)

                def scores(i, u):
                    e, q, key, w, first, _ = units[u]
                    if isinstance(i, int) and u == 0:
                        pe.wait_ge(head_start, 16 * 7)
                    elif isinstance(i, int) and e == 0:
                        if first and q == per:
                            pe.wait_ge(head_in[e], 16 * 7)
                    elif u % per_head == 0:
                        pe.wait_ge(head_in[e], 16 * 7 * i + 16 * 7)
                    pe.wait_ge(beta_done, freed(i * total + u, z_ring, lead))
                    for k, half in enumerate((q_hi, q_lo)):
                        m = pe.matmul(z_ps[u % z_ring][:, 0:w], half[e][:, q * P:(q + 1) * P], k_both[e][:, key:key + w],
                                      start=(k == 0), stop=(k == 1))
                        if first and k == 0:
                            pe.matmul(z_ps[u % z_ring][:, w - P:w], c["ident_r"][:, :], c["not_before"][:, :], start=False, stop=False)
                    m.then_inc(z_done, 1)

                def turn(u, t):
                    w = units[u][3]
                    pe.wait_ge(weight_done, done(t, lead))
                    pe.wait_ge(lo_done, freed(t, wT_ring, lead))
                    for b in range(w // P):
                        m = pe.transpose(wT_ps[u % wT_ring][:, b * P:(b + 1) * P], weight[u % stick_in][:, b * P:(b + 1) * P], c["ident"][:, :])
                    m.then_inc(turned, 1)

                def values(i, u, t):
                    e, q, key, w, first, last = units[u]
                    pe.wait_ge(lo_done, done(t, lead))
                    if first:
                        pe.wait_ge(o_read, freed(i * (2 * tiles) + (e * tiles + q), 2, lead))
                    for b in range(w // P):
                        for k, (half, x) in enumerate(((0, wT_hi), (0, wT_lo), (1, wT_hi))):
                            m = pe.matmul(o_ps[q % 2][:, :], v_both[e][:, key // P + b, half, :], x[u % wT_ring][:, b * P:(b + 1) * P],
                                          start=(first and b == 0 and k == 0), stop=(last and b == w // P - 1 and k == 2))
                    m.then_inc(pv_done, 1)

                def step(i, u, behind):
                    if u < total:
                        scores(i, u)
                    if behind(turn_lag):
                        turn(*behind(turn_lag))
                    if behind(values_lag):
                        values(i if u >= values_lag else i - 1, *behind(values_lag))

                steps(pe, step)


def phase_mix(nc, a, c, s, wide, up_start):
    tiles, kc, d = a["tiles"], a["kc"], a["d"]
    n_pool = a["d_pool"] // P
    part_width = a["d_pool"]
    scales = c["cols"][:, 4 * a["n_ff2"]:4 * a["n_ff2"] + kc]
    with ExitStack() as stack:
        n = Names(nc, stack)
        w_hi, w_lo = wide[0:2], wide[2:4]
        merged = [n.sb(f"merged{i}", [P, kc, P]) for i in range(2)]
        m_hi = [n.sb(f"m_hi{i}", [P, kc, P], F32R) for i in range(2)]
        m_lo = [n.sb(f"m_lo{i}", [P, kc, P], F32R) for i in range(2)]
        squares = n.sb("m_squares", [P, kc, P])
        junk = n.sb("junk", [P, d], mybir.dt.bfloat16)
        sums = n.sb("sums", [P, 2, P])
        xt = [n.sb(f"xo{i}", [P, d]) for i in range(2)]
        mix = [n.sb(f"mix{i}", [P, d]) for i in range(2)]
        hn = [n.sb(f"hn{i}", [P, d]) for i in range(2)]
        h_hi = [n.sb(f"h2_hi{i}", [P, kc, P], F32R) for i in range(2)]
        h_lo = [n.sb(f"h2_lo{i}", [P, kc, P], F32R) for i in range(2)]
        gains = n.sb("gains_mix", [P, 2, d])
        stat = n.sb("stat_mix", [P, 2, 12])
        pool_ps, attn_ps = n.ps("pool_ps", [P, d]), n.ps("attn_ps", [P, d])
        turn_ps = n.ps("h2_turn_ps", [P, d])
        ss_ps = n.ps("ss_ps", [P, 2, 2])
        merged_in, x_in, x2_out, hT_out = (n.sems(x, 2) for x in ("merged_in", "xo_in", "x2_out", "h2T_out"))
        names = ("gain_post_in", "gain_pre_in", "start_h_in", "start_w_in", "start_hi_done", "m_sq", "m_sum", "m_scaled", "m_hi_done", "m_lo_done", "ss_done",
                 "roots_done", "recips_done", "pool_mm_done", "mix_mm_done", "pool_scaled", "mix_done", "mix_sq", "mix_root", "mix_recip", "y_done",
                 "x2_done", "x2_stored", "x2_sq", "x2_root", "x2_recip", "hn_done", "h2_turned", "h2_hi_done", "h2_lo_done")
        (gain_post_in, gain_pre_in, start_h_in, start_w_in, start_hi_done, m_sq, m_sum, m_scaled, m_hi_done, m_lo_done, ss_done, roots_done, recips_done,
         pool_mm_done, mix_mm_done, pool_scaled, mix_done, mix_sq, mix_root, mix_recip, y_done, x2_done, x2_stored, x2_sq, x2_root, x2_recip,
         hn_done, turned, hi_done, lo_done) = (n.sem(x) for x in names)
        x_tiles = a["x"][0].rearrange("(t p) d -> t p d", p=P)
        w_up = a["w_up"][0].rearrange("(c p) (h b n) -> b p h c n", p=P, h=2, n=P)
        m_cols = s["merged"].rearrange("(c p) t -> p c t", p=P)

        def steps(eng, step):
            for t in range(2):
                step(t, t % 2, 0)
            with eng.Fori(0, tiles // 2 - 2) as i:
                for e in range(2):
                    step(i * 2 + (2 + e), e, i + 1)
            for t in range(tiles - 2, tiles + 2):
                step(t, t % 2, t // 2)

        def is_tile(t):
            return not isinstance(t, int) or 0 <= t < tiles

        with nc.Block() as block:

            @block.sync
            def _(sp):
                for sem in hT_out:
                    sp.sem_inc(sem, 16)

                def load_merged(t, slot):
                    sp.wait_ge(m_lo_done, freed(t))
                    sp.dma_start(merged[slot][:, :, :], m_cols[:, :, bass.ts(t, P)]).then_inc(merged_in[slot], 16)

                def load_x(t, slot):
                    sp.wait_ge(hn_done, freed(t))
                    sp.wait_ge(x2_stored, freed(t))
                    sp.dma_start(xt[slot][:, :], x_tiles[t]).then_inc(x_in[slot], 16)

                def store_h(t, slot):
                    sp.wait_ge(lo_done, done(t))
                    sp.dma_start(s["h2T"][0][:, :, bass.ts(t, P)], as_f32(h_hi[slot][:, :, :])).then_inc(hT_out[slot], 16)
                    sp.dma_start(s["h2T"][1][:, :, bass.ts(t, P)], as_f32(h_lo[slot][:, :, :])).then_inc(hT_out[slot], 16)

                load_merged(0, 0)
                load_merged(1, 1)
                load_x(0, 0)
                load_x(1, 1)
                for i, (name, sem) in enumerate((("norm_mix_post", gain_post_in), ("norm_ffn_pre", gain_pre_in))):
                    sp.dma_start(gains[:, i, :], a[name][0].partition_broadcast(P)).then_inc(sem, 16)

                def step(t, slot, uses):
                    if is_tile(t + 1) and not (isinstance(t, int) and t == 0):
                        load_merged(t + 1, 1 - slot)
                    if is_tile(t) and not (isinstance(t, int) and t < 2):
                        load_x(t, slot)
                    if is_tile(t - 2):
                        store_h(t - 2, slot)
                    if isinstance(t, int) and t >= tiles - 2:
                        part = t - (tiles - 2)
                        rows = slice(part * kc // 4, (part + 1) * kc // 4)
                        if part == 0:
                            for e in range(2):
                                sp.wait_ge(hT_out[e], stored(BANK // P // 2, 32))
                        if part < 2:
                            sp.dma_start(up_start["w_f"][:, part, :, :], w_up[0][:, part, :, :]).then_inc(start_w_in, 16)
                        for h in range(2):
                            sp.dma_start(as_f32(up_start["h"][h][:, rows, :]), s["h2T"][h][:, rows, 0:BANK]).then_inc(start_h_in, 16)

                steps(sp, step)
                for e in range(2):
                    sp.wait_ge(hT_out[e], stored(tiles // 2, 32))
                sp.wait_ge(start_h_in, 128)

            @block.gpsimd
            def _(pool):
                for sem in (x2_done, x2_stored):
                    pool.sem_inc(sem, LEAD)

                def step(t, slot, uses):
                    if is_tile(t):
                        pool.wait_ge(y_done, done(t))
                        pool.wait_ge(x_in[slot], 16 * uses + 16)
                        pool.tensor_tensor(xt[slot][:, :], xt[slot][:, :], mix[slot][:, :], ALU.add).then_inc(x2_done, 1)
                        pool.wait_ge(x2_done, done(t))
                        pool.dma_start(s["x2"][t], xt[slot][:, :]).then_inc(x2_out[slot], 16)
                        pool.wait_ge(x2_out[slot], 16 * uses + 16)
                        pool.sem_inc(x2_stored, 1)

                steps(pool, step)

            @block.scalar
            def _(act):
                for sem in (m_sq, m_hi_done, roots_done, pool_scaled, mix_sq, mix_root, x2_sq, x2_root, hi_done):
                    act.sem_inc(sem, LEAD)

                def root(out, in_, width, sem):
                    act.activation(out, in_, ACT.Sqrt, scale=1.0 / width, bias=c["eps"][:, 0:1]).then_inc(sem, 1)

                def square_merged(t, slot, uses):
                    act.wait_ge(merged_in[slot], 16 * uses + 16)
                    act.wait_ge(m_sum, freed(t, 1))
                    act.activation(squares[:, :, :], merged[slot][:, :, :], ACT.Square).then_inc(m_sq, 1)

                def half_merged(t, slot):
                    act.wait_ge(m_scaled, done(t))
                    act.wait_ge(mix_mm_done, freed(t))
                    act.activation(m_hi[slot][:, :, :], merged[slot][:, :, :], ACT.Copy).then_inc(m_hi_done, 1)

                def step(t, slot, uses):
                    if is_tile(t):
                        act.wait_ge(ss_done, done(t))
                        act.wait_ge(recips_done, freed(t))
                        root(stat[:, slot, 0:2], ss_ps[:, slot, :], part_width, roots_done)
                    if is_tile(t + 1):
                        square_merged(t + 1, 1 - slot, uses + slot)
                    if is_tile(t):
                        act.wait_ge(recips_done, done(t))
                        act.wait_ge(pool_mm_done, done(t))
                        act.wait_ge(x2_done, freed(t))
                        act.activation(mix[slot][:, :], pool_ps[:, :], ACT.Copy, scale=stat[:, slot, 2:3]).then_inc(pool_scaled, 1)
                    if is_tile(t + 1):
                        half_merged(t + 1, 1 - slot)
                    if is_tile(t - 1):
                        act.wait_ge(x2_done, done(t - 1))
                        act.activation(junk[:, :], xt[1 - slot][:, :], ACT.Square, accum_out=stat[:, 1 - slot, 7:8]).then_inc(x2_sq, 1)
                        act.wait_ge(x2_sq, done(t - 1))
                        root(stat[:, 1 - slot, 8:9], stat[:, 1 - slot, 7:8], d, x2_root)
                    if is_tile(t - 2):
                        act.wait_ge(turned, done(t - 2))
                        act.wait_ge(hT_out[slot], stored(uses - 1, 32))
                        act.activation(h_hi[slot][:, :, :].rearrange("p c t -> p (c t)"), turn_ps[:, :], ACT.Copy).then_inc(hi_done, 1)
                    if is_tile(t):
                        act.wait_ge(mix_done, done(t))
                        act.wait_ge(x2_sq, freed(t, 1))
                        act.activation(junk[:, :], mix[slot][:, :], ACT.Square, accum_out=stat[:, slot, 4:5]).then_inc(mix_sq, 1)
                        act.wait_ge(mix_sq, done(t))
                        root(stat[:, slot, 5:6], stat[:, slot, 4:5], d, mix_root)

                square_merged(0, 0, 0)
                half_merged(0, 0)
                steps(act, step)
                act.wait_ge(start_w_in, 32)
                act.activation(up_start["w_hi"][:, :, :, :], up_start["w_f"][:, :, :, :], ACT.Copy).then_inc(start_hi_done, 1)

            @block.vector
            def _(dve):
                for sem in (m_sum, m_scaled, m_lo_done, recips_done, mix_done, mix_recip, y_done, x2_recip, hn_done, lo_done):
                    dve.sem_inc(sem, LEAD)

                def prepare(t, slot):
                    dve.wait_ge(m_sq, done(t))
                    dve.wait_ge(ss_done, freed(t, 1))
                    dve.tensor_reduce(sums[:, :, :], squares[:, :, :].rearrange("p (h c) t -> p h t c", h=2), AX.X, ALU.add).then_inc(m_sum, 1)
                    dve.tensor_tensor(merged[slot][:, :, :], merged[slot][:, :, :], scales.unsqueeze(2).broadcast_to([P, kc, P]),
                                      ALU.mult).then_inc(m_scaled, 1)
                    dve.wait_ge(m_hi_done, done(t))
                    dve.wait_ge(mix_mm_done, freed(t))
                    dve.tensor_tensor(m_lo[slot][:, :, :], merged[slot][:, :, :], as_f32(m_hi[slot][:, :, :]), ALU.subtract).then_inc(m_lo_done, 1)

                prepare(0, 0)
                dve.wait_ge(gain_post_in, 16)
                dve.wait_ge(gain_pre_in, 16)

                def step(t, slot, uses):
                    if is_tile(t):
                        dve.wait_ge(roots_done, done(t))
                        dve.reciprocal(stat[:, slot, 2:4], stat[:, slot, 0:2]).then_inc(recips_done, 1)
                    if is_tile(t - 1):
                        dve.wait_ge(mix_root, done(t - 1))
                        dve.reciprocal(stat[:, 1 - slot, 6:7], stat[:, 1 - slot, 5:6]).then_inc(mix_recip, 1)
                        dve.wait_ge(mix_recip, done(t - 1))
                        dve.scalar_tensor_tensor(out=mix[1 - slot][:, :], in0=mix[1 - slot][:, :], scalar=stat[:, 1 - slot, 6:7],
                                                 in1=gains[:, 0, :], op0=ALU.mult, op1=ALU.mult).then_inc(y_done, 1)
                    if is_tile(t + 1):
                        prepare(t + 1, 1 - slot)
                    if is_tile(t - 2):
                        dve.wait_ge(hi_done, done(t - 2))
                        dve.wait_ge(hT_out[slot], stored(uses - 1, 32))
                        dve.tensor_tensor(h_lo[slot][:, :, :].rearrange("p c t -> p (c t)"), turn_ps[:, :],
                                          as_f32(h_hi[slot][:, :, :].rearrange("p c t -> p (c t)")), ALU.subtract).then_inc(lo_done, 1)
                    if is_tile(t - 1):
                        dve.wait_ge(x2_root, done(t - 1))
                        dve.reciprocal(stat[:, 1 - slot, 9:10], stat[:, 1 - slot, 8:9]).then_inc(x2_recip, 1)
                        dve.wait_ge(x2_recip, done(t - 1))
                        dve.wait_ge(turned, freed(t - 1))
                        dve.scalar_tensor_tensor(out=hn[1 - slot][:, :], in0=xt[1 - slot][:, :], scalar=stat[:, 1 - slot, 9:10],
                                                 in1=gains[:, 1, :], op0=ALU.mult, op1=ALU.mult).then_inc(hn_done, 1)
                    if is_tile(t):
                        dve.wait_ge(pool_scaled, done(t))
                        dve.wait_ge(mix_mm_done, done(t))
                        dve.scalar_tensor_tensor(out=mix[slot][:, :], in0=attn_ps[:, :], scalar=stat[:, slot, 3:4], in1=mix[slot][:, :],
                                                 op0=ALU.mult, op1=ALU.add).then_inc(mix_done, 1)

                steps(dve, step)
                dve.wait_ge(start_hi_done, 1)
                dve.tensor_tensor(up_start["w_lo"][:, :, :, :], up_start["w_f"][:, :, :, :], as_f32(up_start["w_hi"][:, :, :, :]), ALU.subtract)

            @block.tensor
            def _(pe):
                for sem in (ss_done, pool_mm_done, mix_mm_done, turned):
                    pe.sem_inc(sem, LEAD)

                def token_sums(t, slot):
                    pe.wait_ge(m_sum, done(t))
                    pe.wait_ge(roots_done, freed(t, 1))
                    for h in range(2):
                        m = pe.matmul(ss_ps[:, slot, h:h + 1], sums[:, h, :], c["ones"][:, 0:1], start=True, stop=True)
                    m.then_inc(ss_done, 1)

                def turn(t, slot):
                    pe.wait_ge(hn_done, done(t))
                    pe.wait_ge(lo_done, freed(t, 1))
                    for k in range(kc):
                        m = pe.transpose(turn_ps[:, k * P:(k + 1) * P], hn[slot][:, k * P:(k + 1) * P], c["ident"][:, :])
                    m.then_inc(turned, 1)

                def part_product(part, t, slot):
                    bank, sem, free = ((pool_ps, pool_mm_done, pool_scaled), (attn_ps, mix_mm_done, mix_done))[part]
                    pe.wait_ge(free, freed(t, 1))
                    for k in range(n_pool):
                        row = part * n_pool + k
                        for j, (m, w) in enumerate(((m_hi, w_hi), (m_hi, w_lo), (m_lo, w_hi))):
                            for half in range(d // BANK):
                                cols = slice(half * BANK, (half + 1) * BANK)
                                mm = pe.matmul(bank[:, cols], m[slot][:, row, :], w[half][:, row, :],
                                               start=(k == 0 and j == 0), stop=(k == n_pool - 1 and j == 2))
                    mm.then_inc(sem, 1)

                def step(t, slot, uses):
                    if is_tile(t):
                        pe.wait_ge(m_lo_done, done(t))
                        part_product(0, t, slot)
                    if is_tile(t - 2):
                        turn(t - 2, slot)
                    if is_tile(t):
                        part_product(1, t, slot)
                    if is_tile(t + 1):
                        token_sums(t + 1, 1 - slot)

                token_sums(0, 0)
                steps(pe, step)


def phase_up(nc, a, c, s, wide, up_start, down_start):
    kc, seq = a["kc"], a["seq"]
    groups = seq // BANK
    n_ff = a["n_ff2"] // 2
    lead = 4
    with ExitStack() as stack:
        n = Names(nc, stack)
        hT = [[up_start["h"][i], n.sb(f"h2T{i}", [P, kc, BANK], F32R), wide[2 * i], wide[2 * i + 1]] for i in range(2)]
        w_f = [up_start["w_f"], n.sb("wu_f1", [P, 2, kc, P])]
        w_hi = [up_start["w_hi"], n.sb("wu_hi1", [P, 2, kc, P], F32R)]
        w_lo = [up_start["w_lo"], n.sb("wu_lo1", [P, 2, kc, P], F32R)]
        conv = [[n.sb(f"conv{i}_{x}", [P, BANK]) for x in range(2)] for i in range(2)]
        f = [n.sb(f"f{i}", [P, BANK]) for i in range(2)]
        ps = [n.ps("gate_ps", [P, seq]), n.ps("value_ps", [P, seq])]
        w_in_, f_out = n.sems("wu_in", 2), n.sems("f_out", 2)
        h_in = n.sems("h2T_in", groups)
        start_in = n.sem("down_start_in")
        names = ("wu_hi_done", "wu_done", "up_done", "tap_done", "conv_step", "silu_done", "f_done", "taps_done")
        wu_hi_done, wu_done, up_done, tap_done, conv_step, silu_done, f_done, taps_done = (n.sem(x) for x in names)
        w_cols = a["w_up"][0].rearrange("(c p) (h b n) -> b p h c n", p=P, h=2, n=P)
        taps = n.sb("taps", [P, 2, 4, 2, 1])
        columns = c["cols"][:, 0:4 * a["n_ff2"]].rearrange("p (k h j) -> p k h j", k=4, h=2)

        def column(kind, h, slot):
            return taps[:, slot, kind, h, :]

        with nc.Block() as block:

            @block.sync
            def _(sp):
                for sem in f_out:
                    sp.sem_inc(sem, 16)

                def load_w(j, slot):
                    sp.wait_ge(wu_done, freed(j))
                    for h in range(2):
                        sp.dma_start(w_f[slot][:, h, :, :], w_cols[j][:, h, :, :]).then_inc(w_in_[slot], 16)

                def load_h(j):
                    for i in range(2):
                        sp.dma_start(as_f32(hT[i][j][:, :, :]), s["h2T"][i][:, :, j * BANK:(j + 1) * BANK]).then_inc(h_in[j], 16)

                sp.sem_inc(w_in_[0], 32)
                sp.sem_inc(h_in[0], 32)
                load_h(1)
                load_w(1, 1)
                for j in range(2, groups):
                    load_h(j)

                def store(j, g):
                    sp.wait_ge(f_done, done(j * groups + g, lead))
                    sp.dma_start(s["f"][j][:, g * BANK:(g + 1) * BANK], f[g % 2][:, :]).then_inc(f_out[g % 2], 16)

                with sp.Fori(0, n_ff // 2 - 1) as i:
                    for e in range(2):
                        load_w(i * 2 + (2 + e), e)
                        for g in range(groups):
                            store(i * 2 + e, g)
                sp.wait_ge(f_out[0], stored(groups))
                for k in range(2):
                    sp.dma_start(down_start["w_f"][k][:, :], a["w_down"][0][k * P:(k + 1) * P, :]).then_inc(start_in, 16)
                    sp.dma_start(down_start["f_f"][k][:, :], s["f"][k][:, 0:BANK]).then_inc(start_in, 16)
                for e in range(2):
                    for g in range(groups):
                        store(n_ff - 2 + e, g)
                for e in range(2):
                    sp.wait_ge(f_out[e], stored(n_ff * groups // 2))
                sp.wait_ge(start_in, 64)

            def blocks_of(eng, block_step):
                with eng.Fori(0, n_ff // 2 - 1) as i:
                    for e in range(2):
                        block_step(i * 2 + e, i, e, False)
                for e in range(2):
                    block_step(n_ff - 2 + e, n_ff // 2 - 1, e, e == 1)

            @block.scalar
            def _(act):
                for sem in (tap_done, silu_done):
                    act.sem_inc(sem, LEAD)
                act.sem_inc(wu_hi_done, done(0))

                def half_w(j, i, slot):
                    act.wait_ge(w_in_[slot], 32 * i + 32)
                    act.wait_ge(up_done, freed(j * 2 * groups - 1, 2 * groups, 4 * groups))
                    act.activation(w_hi[slot][:, :, :, :], w_f[slot][:, :, :, :], ACT.Copy).then_inc(wu_hi_done, 1)

                def block_step(j, i, slot, last):
                    for g in range(groups):
                        count = j * groups + g
                        if g == 0 and not last:
                            half_w(j + 1, i + slot, 1 - slot)
                        for h in range(2):
                            act.wait_ge(up_done, done(count * 2 + h, 4 * groups))
                            act.wait_ge(taps_done, j + 1)
                            act.wait_ge(f_done, freed(count, 2, lead))
                            act.activation(conv[g % 2][h][:, :], ps[h][:, g * BANK:(g + 1) * BANK], ACT.Identity,
                                           scale=column(3, h, slot), bias=column(0, h, slot)).then_inc(tap_done, 1)
                        act.wait_ge(conv_step, 4 * count + 3)
                        act.activation(conv[g % 2][0][:, :], conv[g % 2][0][:, :], ACT.Silu).then_inc(silu_done, 1)

                blocks_of(act, block_step)

            @block.vector
            def _(dve):
                dve.sem_inc(f_done, lead)
                dve.sem_inc(wu_done, done(0))

                def copy_taps(j, slot):
                    dve.tensor_scalar(taps[:, slot, :, :, :], columns[:, :, :, bass.ds(j, 1)], 1.0, None, ALU.mult).then_inc(taps_done, 1)

                def split_w(j, slot):
                    dve.wait_ge(f_done, freed(j * groups, groups + 1, lead))
                    copy_taps(j, slot)
                    dve.wait_ge(wu_hi_done, done(j))
                    dve.wait_ge(up_done, freed(j * 2 * groups - 1, 2 * groups, 4 * groups))
                    dve.tensor_tensor(w_lo[slot][:, :, :, :], w_f[slot][:, :, :, :], as_f32(w_hi[slot][:, :, :, :]), ALU.subtract).then_inc(wu_done, 1)

                def block_step(j, i, slot, last):
                    for g in range(groups):
                        count = j * groups + g
                        if g == 0 and not last:
                            split_w(j + 1, 1 - slot)
                        for back, kind in ((1, 2), (2, 1)):
                            skip = back if g == 0 else 0
                            for h in range(2):
                                if back == 1:
                                    dve.wait_ge(tap_done, done(count * 2 + h))
                                else:
                                    dve.wait_ge(conv_step, 4 * count + 1 + h)
                                out = conv[g % 2][h][:, skip:]
                                dve.wait_ge(taps_done, j + 1)
                                dve.scalar_tensor_tensor(out=out, in0=ps[h][:, g * BANK - back + skip:(g + 1) * BANK - back],
                                                         scalar=column(kind, h, slot), in1=out, op0=ALU.mult, op1=ALU.add).then_inc(conv_step, 1)
                        dve.wait_ge(silu_done, done(count))
                        dve.wait_ge(conv_step, 4 * count + 4)
                        dve.wait_ge(f_out[g % 2], stored(j * (groups // 2) + g // 2))
                        dve.tensor_tensor(f[g % 2][:, :], conv[g % 2][0][:, :], conv[g % 2][1][:, :], ALU.mult).then_inc(f_done, 1)

                copy_taps(0, 0)
                blocks_of(dve, block_step)

            @block.tensor
            def _(pe):
                pe.sem_inc(up_done, 4 * groups)

                def block_step(j, i, slot, last):
                    pe.wait_ge(wu_done, done(j))
                    for g in range(groups):
                        pe.wait_ge(h_in[g], 32)
                        pe.wait_ge(f_done, freed(j * groups + g, groups - (1 if g < groups - 1 else 0), lead))
                        for h in range(2):
                            for k in range(kc):
                                for t, (w, x) in enumerate(((w_hi, 0), (w_hi, 1), (w_lo, 0))):
                                    m = pe.matmul(ps[h][:, g * BANK:(g + 1) * BANK], w[slot][:, h, k, :], hT[x][g][:, k, :],
                                                  start=(k == 0 and t == 0), stop=(k == kc - 1 and t == 2))
                            m.then_inc(up_done, 1)

                blocks_of(pe, block_step)


def phase_down(nc, a, c, s, out, down_start):
    seq, d = a["seq"], a["d"]
    groups, per = seq // BANK, BANK // P
    n_ff = a["n_ff2"] // 2
    with ExitStack() as stack:
        n = Names(nc, stack)
        w_f, f_f = down_start["w_f"], down_start["f_f"]
        w_hi = [n.sb(f"wd_hi{i}", [P, d], F32R) for i in range(2)]
        w_lo = [n.sb(f"wd_lo{i}", [P, d], F32R) for i in range(2)]
        f_hi = [n.sb(f"fd_hi{i}", [P, BANK], F32R) for i in range(2)]
        f_lo = [n.sb(f"fd_lo{i}", [P, BANK], F32R) for i in range(2)]
        gain = n.sb("gain_down", [P, d])
        junk = n.sb("junk_down", [P, d], mybir.dt.bfloat16)
        x2 = [n.sb(f"x2_{i}", [P, d]) for i in range(per)]
        y = [n.sb(f"y{i}", [P, d]) for i in range(per)]
        stat = n.sb("stat_down", [P, per, 4])
        ps = [n.ps(f"down_ps{i}", [P, d]) for i in range(per)]
        load_in = n.sems("down_in", 2)
        x2_in, y_out = n.sems("x2_in", per), n.sems("y_out", per)
        names = ("gain_down_in", "half_done", "split_done", "k_done", "sq_down", "root_down", "recip_down", "scaled_down", "added_down", "y_free")
        gain_in, half_done, split_done, k_done, sq_done, root_done, recip_done, scaled, added, y_free = (n.sem(x) for x in names)
        w_rows = a["w_down"][0].rearrange("(c p) n -> c p n", p=P)
        counted = n_ff - 1 + per

        def slot_free(i, k):
            return i * counted + ((1, per + 1)[k] if k < 2 else per + k)

        out_tiles = out[0].rearrange("(g t p) d -> g t p d", t=per, p=P)
        x2_tiles = s["x2"].rearrange("(g t) p d -> g t p d", t=per)

        with nc.Block() as block:

            @block.sync
            def _(sp):
                sp.dma_start(gain[:, :], a["norm_ffn_post"][0].partition_broadcast(P)).then_inc(gain_in, 16)
                for sem in load_in:
                    sp.sem_inc(sem, 32)

                def load(i, k):
                    sp.wait_ge(split_done, freed(i * n_ff + k))
                    sp.dma_start(w_f[k % 2][:, :], w_rows[k]).then_inc(load_in[k % 2], 16)
                    sp.dma_start(f_f[k % 2][:, :], s["f"][k][:, bass.ts(i, BANK)]).then_inc(load_in[k % 2], 16)

                def group(i, last):
                    for k in range(2, n_ff):
                        load(i, k)
                        if k == 4:
                            for t in range(per):
                                sp.wait_ge(added, freed(i * per + t, per, per))
                                sp.dma_start(x2[t][:, :], x2_tiles[i, t]).then_inc(x2_in[t], 16)
                    if not last:
                        load(i + 1, 0)
                        load(i + 1, 1)

                with sp.Fori(0, groups - 1) as i:
                    group(i, False)
                group(groups - 1, True)

            @block.gpsimd
            def _(pool):
                for sem in (added, y_free):
                    pool.sem_inc(sem, per)
                with pool.Fori(0, groups) as i:
                    for t in range(per):
                        pool.wait_ge(scaled, done(i * per + t, per))
                        pool.wait_ge(x2_in[t], 16 * i + 16)
                        pool.tensor_tensor(y[t][:, :], y[t][:, :], x2[t][:, :], ALU.add).then_inc(added, 1)
                        pool.wait_ge(added, done(i * per + t, per))
                        pool.dma_start(out_tiles[i, t], y[t][:, :]).then_inc(y_out[t], 16)
                    for t in range(per):
                        pool.wait_ge(y_out[t], 16 * i + 16)
                        pool.sem_inc(y_free, 1)

            @block.scalar
            def _(act):
                for sem in (half_done, sq_done):
                    act.sem_inc(sem, LEAD)

                def half(i, k):
                    act.wait_ge(load_in[k % 2], 32 * (i * (n_ff // 2) + k // 2) + 32)
                    act.wait_ge(k_done, slot_free(i, k))
                    act.activation(w_hi[k % 2][:, :], w_f[k % 2][:, :], ACT.Copy)
                    act.activation(f_hi[k % 2][:, :], f_f[k % 2][:, :], ACT.Copy).then_inc(half_done, 1)

                def statistics(i, t):
                    count = i * per + t
                    act.wait_ge(k_done, done(i * counted + (n_ff - 1 + t), per + 1))
                    act.wait_ge(sq_done, freed(count, 1, 2))
                    act.activation(junk[:, :], ps[t][:, :], ACT.Square, accum_out=stat[:, t, 0:1]).then_inc(sq_done, 1)
                    act.wait_ge(sq_done, done(count, 2))
                    act.activation(stat[:, t, 1:2], stat[:, t, 0:1], ACT.Sqrt, scale=1.0 / d, bias=c["eps"][:, 0:1]).then_inc(root_done, 1)

                def group(i, last):
                    for k in range(2, n_ff):
                        half(i, k)
                    if not last:
                        half(i + 1, 0)
                    for t in range(per):
                        statistics(i, t)
                    if not last:
                        half(i + 1, 1)

                half(0, 0)
                half(0, 1)
                with act.Fori(0, groups - 1) as i:
                    group(i, False)
                group(groups - 1, True)

            @block.vector
            def _(dve):
                dve.sem_inc(split_done, LEAD)
                dve.sem_inc(scaled, per)

                def split(i, k):
                    dve.wait_ge(half_done, done(i * n_ff + k))
                    dve.wait_ge(k_done, slot_free(i, k))
                    dve.tensor_tensor(w_lo[k % 2][:, :], w_f[k % 2][:, :], as_f32(w_hi[k % 2][:, :]), ALU.subtract)
                    dve.tensor_tensor(f_lo[k % 2][:, :], f_f[k % 2][:, :], as_f32(f_hi[k % 2][:, :]), ALU.subtract).then_inc(split_done, 1)

                def scale(i, t):
                    count = i * per + t
                    dve.wait_ge(root_done, count + 1)
                    dve.reciprocal(stat[:, t, 2:3], stat[:, t, 1:2]).then_inc(recip_done, 1)
                    dve.wait_ge(recip_done, count + 1)
                    dve.wait_ge(y_free, freed(count, per, per))
                    dve.scalar_tensor_tensor(out=y[t][:, :], in0=ps[t][:, :], scalar=stat[:, t, 2:3], in1=gain[:, :],
                                             op0=ALU.mult, op1=ALU.mult).then_inc(scaled, 1)

                def group(i, last):
                    for k in range(2, n_ff):
                        split(i, k)
                    if not last:
                        split(i + 1, 0)
                    for t in range(per):
                        scale(i, t)
                    if not last:
                        split(i + 1, 1)

                split(0, 0)
                split(0, 1)
                dve.wait_ge(gain_in, 16)
                with dve.Fori(0, groups - 1) as i:
                    group(i, False)
                group(groups - 1, True)

            @block.tensor
            def _(pe):
                pe.sem_inc(k_done, per + 1)
                with pe.Fori(0, groups) as i:
                    for k in range(n_ff):
                        pe.wait_ge(split_done, done(i * n_ff + k))
                        for t in range(per):
                            if k == 0:
                                pe.wait_ge(scaled, freed(i * per + t, per, per))
                            for j, (x, w) in enumerate(((f_hi, w_hi), (f_hi, w_lo), (f_lo, w_hi))):
                                for half in range(d // BANK):
                                    cols = slice(half * BANK, (half + 1) * BANK)
                                    m = pe.matmul(ps[t][:, cols], x[k % 2][:, t * P:(t + 1) * P], w[k % 2][:, cols],
                                                  start=(k == 0 and j == 0), stop=(k == n_ff - 1 and j == 2))
                            if k == n_ff - 1:
                                m.then_inc(k_done, 1)
                        if k < n_ff - 1:
                            m.then_inc(k_done, 1)


def build(nc, a, out):
    d = a["x"].shape[2]
    seq = a["x"].shape[1]
    a.update(d=d, seq=seq, tiles=seq // P, kc=d // P, d_in=a["w_in"].shape[2], d_pool=a["pool_scale"].shape[1],
             d_attn=a["attn_scale"].shape[1], n_ff2=a["conv_b"].shape[1] // P, conv_width=a["conv_w"].shape[1])
    heads = a["d_attn"] // HEAD_DIM
    n_qk = 2 * a["d_attn"] // P
    scratch = lambda name, shape, dtype: nc.dram_tensor(name, shape, dtype, kind="Internal").ap()
    s = {
        "v": scratch("v_scratch", [heads, P, a["tiles"], 2, HEAD_DIM], F32),
        "qk": scratch("qk_scratch", [n_qk, 2, P, seq], F32),
        "x2": scratch("x2_scratch", [a["tiles"], P, d], F32),
        "h2T": scratch("h2T_scratch", [2, P, a["kc"], seq], F32),
        "f": scratch("f_scratch", [a["n_ff2"] // 2, P, seq], F32),
        "merged": scratch("merged_scratch", [a["d_pool"] + a["d_attn"], seq], F32),
    }
    with ExitStack() as stack:
        n = Names(nc, stack)
        c = {"ident": n.sb("ident", [P, P]), "ident_r": n.sb("ident_r", [P, P], F32R), "not_before": n.sb("not_before", [P, P], F32R),
             "ones": n.sb("ones", [P, 2]), "eps": n.sb("eps", [P, 1]),
             "cols": n.sb("cols", [P, 4 * a["n_ff2"] + 8])}
        phase_setup(nc, a, c)
        with ExitStack() as inner:
            m = Names(nc, inner)
            hT = [m.sb(f"hT{i}", [P, a["kc"], seq], F32R) for i in range(2)]
            phase_values(nc, a, c, s, hT)
            phase_projections(nc, a, c, s, hT)
        wide = [n.sb(f"wide{i}", [P, a["kc"], BANK], F32R) for i in range(4)]
        phase_attention(nc, a, c, s, wide)
        up_start = {"h": [n.sb(f"up_start_h{i}", [P, a["kc"], BANK], F32R) for i in range(2)],
                    "w_f": n.sb("wu_f0", [P, 2, a["kc"], P]),
                    "w_hi": n.sb("wu_hi0", [P, 2, a["kc"], P], F32R), "w_lo": n.sb("wu_lo0", [P, 2, a["kc"], P], F32R)}
        phase_mix(nc, a, c, s, wide, up_start)
        down_start = {"w_f": [n.sb(f"wd_f{i}", [P, d]) for i in range(2)], "f_f": [n.sb(f"fd_f{i}", [P, BANK]) for i in range(2)]}
        phase_up(nc, a, c, s, wide, up_start, down_start)
        phase_down(nc, a, c, s, out, down_start)




def kernel(**inputs):
    import numpy as _np
    import concourse.bacc as _bacc
    from concourse.bass_utils import run_bass_kernel_spmd as _run

    nc = _bacc.Bacc("TRN2", target_bir_lowering=False, num_devices=1)
    arrays, args = {}, {}
    for name, value in inputs.items():
        array = _np.ascontiguousarray(value)
        arrays[f"in_{name}"] = array
        args[name] = nc.dram_tensor(f"in_{name}", array.shape, mybir.dt.from_np(array.dtype), kind="ExternalInput").ap()
    out = nc.dram_tensor("layer_out", inputs["x"].shape, F32, kind="ExternalOutput").ap()
    build(nc, args, out)
    result = _run(nc, [arrays], core_ids=[0])
    return result.results[0]["layer_out"]
```

```python
from contextlib import ExitStack

import concourse.bass as bass
from concourse import mybir

F32 = mybir.dt.float32
F32R = mybir.dt.float32r
ALU = mybir.AluOpType
ACT = mybir.ActivationFunctionType
AX = mybir.AxisListType

P = 128
BANK = 512
EPS = 1e-6
MASKED_SCORE = -1e30
POOL_WINDOWS = (2, 4, 8, 16)
HEAD_DIM = 64
LEAD = 2


def done(step, lead=LEAD):
    return step + 1 + lead


def freed(step, ring=LEAD, lead=LEAD):
    return step + 1 + lead - ring


def stored(uses, each=16):
    return each * uses + 16


class Names:

    def __init__(self, nc, stack):
        self.nc, self.stack = nc, stack

    def sb(self, name, shape, dtype=F32):
        return self.stack.enter_context(self.nc.sbuf_tensor(name, shape, dtype))

    def ps(self, name, shape, dtype=F32):
        return self.stack.enter_context(self.nc.psum_tensor(name, shape, dtype))

    def sem(self, name):
        return self.stack.enter_context(self.nc.semaphore(name))

    def sems(self, name, n):
        return [self.sem(f"{name}{i}") for i in range(n)]


def as_f32(tile):
    return tile.bitcast(F32)


def phase_setup(nc, a, c, start):
    with ExitStack() as stack:
        n = Names(nc, stack)
        n_conv = a["n_ff2"]
        rows = n.sb("rows", [P, 6, P])
        not_before = n.sb("not_before_f", [P, P])
        cols_ps = n.ps("cols_ps", [P, BANK])
        rows_in, zeroed, ident_done, turned, cols_done = (
            n.sem(s) for s in ("rows_in", "zeroed", "ident_done", "turned", "cols_done"))
        with nc.Block() as block:

            @block.sync
            def _(sp):
                x_tiles = a["x"][0].rearrange("(t p) d -> t p d", p=P)
                w_v = a["w_in"][0].rearrange("(c p) n -> p c n", p=P)
                sp.dma_start(start["xt"][0][:, :], x_tiles[0]).then_inc(start["x_in"][0], 16)
                sp.dma_start(rows[0:n_conv, 0, :], a["conv_b"][0].rearrange("(j p) -> j p", p=P)).then_inc(rows_in, 16)
                for k in range(a["conv_width"]):
                    sp.dma_start(rows[0:n_conv, 1 + k, :], a["conv_w"][0, k].rearrange("(j p) -> j p", p=P)).then_inc(rows_in, 16)
                for half, name in enumerate(("pool_scale", "attn_scale")):
                    sp.dma_start(rows[4 * half:4 * half + 4, 4, :], a[name][0].rearrange("(j p) -> j p", p=P)).then_inc(rows_in, 16)
                sp.dma_start(start["gain"][:, :], a["norm_mix_pre"][0].partition_broadcast(P)).then_inc(start["gain_in"], 16)
                for k in range(3):
                    sp.dma_start(start["wv_f"][:, k, :], w_v[:, k, a["d_in"] - a["d_attn"]:]).then_inc(start["wv_in"][k], 16)
                sp.dma_start(start["xt"][1][:, :], x_tiles[1]).then_inc(start["x_in"][1], 16)
                sp.wait_ge(rows_in, 16 * (3 + a["conv_width"]))

            @block.gpsimd
            def _(pool):
                pool.memset(c["ident"][:, :], 0.0).then_inc(zeroed, 1)
                pool.wait_ge(zeroed, 1)
                pool.affine_select(out=c["ident"][:, :], in_=c["ident"][:, :], compare_op=ALU.not_equal, fill=1.0,
                                   base=0, pattern=[[-1, P]], channel_multiplier=1).then_inc(ident_done, 1)
                pool.memset(not_before[:, :], 0.0).then_inc(zeroed, 1)
                pool.wait_ge(zeroed, 2)
                pool.affine_select(out=not_before[:, :], in_=not_before[:, :], compare_op=ALU.is_gt, fill=MASKED_SCORE,
                                   base=0, pattern=[[-1, P]], channel_multiplier=1).then_inc(ident_done, 1)

            @block.tensor
            def _(pe):
                pe.wait_ge(rows_in, 16 * (3 + a["conv_width"]))
                pe.wait_ge(ident_done, 1)
                for k in range(1 + a["conv_width"]):
                    pe.transpose(cols_ps[:, k * n_conv:(k + 1) * n_conv], rows[0:n_conv, k, :],
                                 c["ident"][0:n_conv, 0:n_conv])
                pe.transpose(cols_ps[:, 4 * n_conv:4 * n_conv + 8], rows[0:8, 4, :], c["ident"][0:8, 0:8]).then_inc(turned, 1)

            @block.vector
            def _(dve):
                dve.memset(c["ones"][:, :], 1.0)
                dve.memset(c["eps"][:, :], EPS)
                dve.wait_ge(ident_done, 2)
                dve.tensor_copy(c["ident_r"][:, :], c["ident"][:, :])
                dve.tensor_copy(c["not_before"][:, :], not_before[:, :])
                dve.wait_ge(turned, 1)
                dve.tensor_copy(c["cols"][:, 0:4 * n_conv + 8], cols_ps[:, 0:4 * n_conv + 8]).then_inc(cols_done, 1)


def phase_values(nc, a, c, s, hT, start, w_first, bridge):
    tiles, kc, d = a["tiles"], a["kc"], a["d"]
    d_v = a["d_attn"]
    heads = d_v // HEAD_DIM
    with ExitStack() as stack:
        n = Names(nc, stack)
        xt, gain, wv_f, x_in, gain_in, wv_in = (start[x] for x in ("xt", "gain", "wv_f", "x_in", "gain_in", "wv_in"))
        wv_hi, wv_lo = n.sb("wv_hi", [P, kc, d_v], F32R), n.sb("wv_lo", [P, kc, d_v], F32R)
        squares = bridge[:, 3, :].bitcast(mybir.dt.bfloat16)
        h_hi = [n.sb(f"h_hi{i}", [P, kc, P], F32R) for i in range(2)]
        h_lo = [n.sb(f"h_lo{i}", [P, kc, P], F32R) for i in range(2)]
        v_out = n.sb("v_out", [P, heads, 2, HEAD_DIM], F32R)
        stat = n.sb("stat", [P, 2, 4])
        turn_ps = [n.ps(f"turn_ps{i}", [P, kc * P]) for i in range(2)]
        v_ps = [n.ps(f"v_ps{i}", [P, d_v]) for i in range(2)]
        w_start_in = n.sem("w_start_in")
        hT_out, v_stored = n.sems("hT_out", 2), n.sem("v_stored")
        names = ("wv_hi_done", "wv_done", "sq_done", "root_done", "recip_done", "xn_done", "turn_done",
                 "h_hi_done", "h_lo_done", "v_done", "v_hi_done", "v_lo_done")
        (wv_hi_done, wv_done, sq_done, root_done, recip_done, xn_done, turn_done,
         h_hi_done, h_lo_done, v_done, v_hi_done, v_lo_done) = (n.sem(x) for x in names)
        x_tiles = a["x"][0].rearrange("(t p) d -> t p d", p=P)
        w_cols = a["w_in"][0].rearrange("(c p) (b n) -> b p c n", p=P, n=P)

        with nc.Block() as block:

            @block.sync
            def _(sp):
                for sem in hT_out + [v_stored]:
                    sp.sem_inc(sem, 16)

                def load_x(t, slot):
                    sp.wait_ge(turn_done, freed(t))
                    sp.dma_start(xt[slot][:, :], x_tiles[t]).then_inc(x_in[slot], 16)

                def store_h(t, slot):
                    sp.wait_ge(h_lo_done, done(t))
                    sp.dma_start(as_f32(hT[0][:, :, bass.ts(t, P)]), as_f32(h_hi[slot][:, :, :])).then_inc(hT_out[slot], 16)
                    sp.dma_start(as_f32(hT[1][:, :, bass.ts(t, P)]), as_f32(h_lo[slot][:, :, :])).then_inc(hT_out[slot], 16)

                def store_v(t):
                    sp.wait_ge(v_lo_done, done(t))
                    sp.dma_start(s["v"][:, :, t, :, :].rearrange("h p a e -> p h a e"),
                                 as_f32(v_out[:, :, :, :])).then_inc(v_stored, 16)

                w_v = a["w_in"][0].rearrange("(c p) n -> p c n", p=P)
                for k in range(3, kc):
                    sp.wait_ge(wv_done, k - 2)
                    sp.dma_start(wv_f[:, k % 3, :], w_v[:, k, a["d_in"] - d_v:]).then_inc(wv_in[k % 3], 16)
                load_x(2, 0)
                store_h(0, 0)
                with sp.Fori(0, tiles // 2 - 2) as i:
                    for e in range(2):
                        load_x(i * 2 + (3 + e), 1 - e)
                        store_h(i * 2 + (1 + e), 1 - e)
                        store_v(i * 2 + e)
                load_x(tiles - 1, 1)
                for t in range(tiles - 3, tiles):
                    store_h(t, t % 2)
                    store_v(t - 1)
                sp.dma_start(w_first[:, :, :], w_cols[0]).then_inc(w_start_in, 16)
                store_v(tiles - 1)
                sp.wait_ge(w_start_in, 16)
                for e in range(2):
                    sp.wait_ge(hT_out[e], stored(tiles // 2, 32))
                sp.wait_ge(v_stored, stored(tiles))

            @block.scalar
            def _(act):
                for sem in (sq_done, root_done, h_hi_done, v_hi_done):
                    act.sem_inc(sem, LEAD)

                def statistics(t, uses, slot):
                    act.wait_ge(x_in[slot], 16 * uses + 16)
                    act.wait_ge(sq_done, freed(t, 1))
                    act.activation(squares, xt[slot][:, :], ACT.Square, accum_out=stat[:, slot, 0:1]).then_inc(sq_done, 1)
                    act.wait_ge(sq_done, done(t))
                    act.activation(stat[:, slot, 1:2], stat[:, slot, 0:1], ACT.Sqrt, scale=1.0 / d,
                                   bias=c["eps"][:, 0:1]).then_inc(root_done, 1)

                def h_half(t, uses, slot):
                    act.wait_ge(turn_done, done(t))
                    act.wait_ge(v_done, freed(t))
                    act.wait_ge(hT_out[slot], stored(uses, 32))
                    act.activation(h_hi[slot][:, :, :].rearrange("p c t -> p (c t)"), turn_ps[slot][:, :],
                                   ACT.Copy).then_inc(h_hi_done, 1)

                def v_half(t, slot):
                    act.wait_ge(v_done, done(t))
                    act.wait_ge(v_stored, stored(t))
                    act.activation(v_out[:, :, 0, :], v_ps[slot][:, :].rearrange("p (h e) -> p h e", h=heads),
                                   ACT.Copy).then_inc(v_hi_done, 1)

                def wv_half(k):
                    act.wait_ge(wv_in[k % 3], 16 * (k // 3 + 1))
                    act.activation(wv_hi[:, k, :], wv_f[:, k % 3, :], ACT.Copy).then_inc(wv_hi_done, 1)

                for k in range(kc):
                    if k == 2:
                        statistics(0, 0, 0)
                    elif k == 5:
                        h_half(0, 0, 0)
                    wv_half(k)
                statistics(1, 0, 1)
                with act.Fori(0, tiles // 2 - 1) as i:
                    for e in range(2):
                        statistics(i * 2 + (2 + e), i + 1, e)
                        h_half(i * 2 + (1 + e), i + e, 1 - e)
                        v_half(i * 2 + e, e)
                h_half(tiles - 1, tiles // 2 - 1, 1)
                for e in range(2):
                    v_half(tiles - 2 + e, e)

            @block.vector
            def _(dve):
                for sem in (recip_done, xn_done, h_lo_done, v_lo_done):
                    dve.sem_inc(sem, LEAD)
                dve.wait_ge(gain_in, 16)

                def scale_x(t, slot):
                    dve.wait_ge(root_done, done(t))
                    dve.reciprocal(stat[:, slot, 2:3], stat[:, slot, 1:2]).then_inc(recip_done, 1)
                    dve.wait_ge(recip_done, done(t))
                    dve.scalar_tensor_tensor(out=xt[slot][:, :], in0=xt[slot][:, :], scalar=stat[:, slot, 2:3],
                                             in1=gain[:, :], op0=ALU.mult, op1=ALU.mult).then_inc(xn_done, 1)

                def h_half(t, uses, slot):
                    dve.wait_ge(h_hi_done, done(t))
                    dve.wait_ge(v_done, freed(t))
                    dve.wait_ge(hT_out[slot], stored(uses, 32))
                    dve.tensor_tensor(h_lo[slot][:, :, :].rearrange("p c t -> p (c t)"), turn_ps[slot][:, :],
                                      as_f32(h_hi[slot][:, :, :].rearrange("p c t -> p (c t)")), ALU.subtract).then_inc(h_lo_done, 1)

                def v_half(t, slot):
                    dve.wait_ge(v_hi_done, done(t))
                    dve.wait_ge(v_stored, stored(t))
                    dve.tensor_tensor(v_out[:, :, 1, :], v_ps[slot][:, :].rearrange("p (h e) -> p h e", h=heads),
                                      as_f32(v_out[:, :, 0, :]), ALU.subtract).then_inc(v_lo_done, 1)

                def wv_half(k):
                    dve.wait_ge(wv_hi_done, k + 1)
                    dve.tensor_tensor(wv_lo[:, k, :], wv_f[:, k % 3, :], as_f32(wv_hi[:, k, :]), ALU.subtract).then_inc(wv_done, 1)

                for k in range(kc):
                    if k == 2:
                        scale_x(0, 0)
                    elif k == 5:
                        h_half(0, 0, 0)
                    wv_half(k)
                scale_x(1, 1)
                with dve.Fori(0, tiles // 2 - 1) as i:
                    for e in range(2):
                        scale_x(i * 2 + (2 + e), e)
                        h_half(i * 2 + (1 + e), i + e, 1 - e)
                        v_half(i * 2 + e, e)
                h_half(tiles - 1, tiles // 2 - 1, 1)
                for e in range(2):
                    v_half(tiles - 2 + e, e)

            @block.tensor
            def _(pe):
                for sem in (turn_done, v_done):
                    pe.sem_inc(sem, LEAD)

                def turn(t, slot):
                    pe.wait_ge(xn_done, done(t))
                    pe.wait_ge(h_lo_done, freed(t))
                    for k in range(kc):
                        m = pe.transpose(turn_ps[slot][:, k * P:(k + 1) * P], xt[slot][:, k * P:(k + 1) * P], c["ident"][:, :])
                    m.then_inc(turn_done, 1)

                def values(t, slot):
                    pe.wait_ge(h_lo_done, done(t))
                    pe.wait_ge(v_lo_done, freed(t))
                    for k in range(kc):
                        for j, (h, w) in enumerate(((h_hi, wv_hi), (h_hi, wv_lo), (h_lo, wv_hi))):
                            m = pe.matmul(v_ps[slot][:, :], h[slot][:, k, :], w[:, k, :],
                                          start=(k == 0 and j == 0), stop=(k == kc - 1 and j == 2))
                    m.then_inc(v_done, 1)

                turn(0, 0)
                pe.wait_ge(wv_done, kc)
                with pe.Fori(0, tiles // 2 - 1) as i:
                    for e in range(2):
                        turn(i * 2 + (e + 1), 1 - e)
                        values(i * 2 + e, e)
                turn(tiles - 1, 1)
                for e in range(2):
                    values(tiles - 2 + e, e)


def phase_projections(nc, a, c, s, hT, w_first, bridge):
    kc, seq, groups = a["kc"], a["seq"], a["seq"] // BANK
    n_u, n_qk = a["d_pool"] // P, 2 * a["d_attn"] // P
    pad = max(POOL_WINDOWS)
    with ExitStack() as stack:
        n = Names(nc, stack)
        w_f = [w_first, n.sb("w_f1", [P, kc, P])]
        w_hi = [n.sb(f"w_hi{i}", [P, kc, P], F32R) for i in range(2)]
        w_lo = [n.sb(f"w_lo{i}", [P, kc, P], F32R) for i in range(2)]
        u = n.sb("u", [P, pad + seq])
        run = n.sb("run", [P, 2, pad + seq])
        pooled = n.sb("pooled", [P, seq])
        w_pool = bridge[:, 0, :].rearrange("c (g d) -> c g d", g=n_u)
        pool_out = n.sb("pool_out", [P, 2, BANK])
        ramp = n.sb("ramp", [P, pad])
        qk_hi, qk_lo = n.sb("qk_hi", [P, 2, BANK], F32R), n.sb("qk_lo", [P, 2, BANK], F32R)
        out_ps = [n.ps(f"out_ps{i}", [P, BANK]) for i in range(8)]
        w_in_, qk_out, group_out = n.sems("w_in", 2), n.sems("qk_out", 2), n.sems("group_out", 2)
        (w_pool_in, w_hi_done, w_lo_done, out_done, u_read, qk_read, pool_step, pool_done, group_done, group_read, hi_done) = (
            n.sem(x) for x in ("w_pool_in", "w_hi_done", "w_lo_done", "out_done", "u_read", "qk_read", "pool_step",
                               "pool_done", "group_done", "group_read", "hi_done"))
        w_cols = a["w_in"][0].rearrange("(c p) (b n) -> b p c n", p=P, n=P)

        def half_of(b):
            return (4 if 1 <= b <= n_u + 1 else 0) if b <= n_u + 1 else 4 * (b % 2)

        def half_of_qk(i, e):
            return 4 if isinstance(i, int) and i == 0 else 4 * e

        with nc.Block() as block:

            @block.sync
            def _(sp):
                for sem in qk_out:
                    sp.sem_inc(sem, 16)

                def load_w(b, slot):
                    sp.wait_ge(w_lo_done, freed(b))
                    sp.dma_start(w_f[slot][:, :, :], w_cols[b]).then_inc(w_in_[slot], 16)

                def store_group(g):
                    for j in range(groups):
                        sp.wait_ge(group_read, g * groups + j + 1)
                        sp.dma_start(s["merged"][g * P:(g + 1) * P, j * BANK:(j + 1) * BANK], pool_out[:, j % 2, :]).then_inc(group_out[j % 2], 16)

                def store(b):
                    for j in range(groups):
                        sp.wait_ge(qk_read, b * groups + j + 1)
                        sp.dma_start(s["qk"][b, 0, :, j * BANK:(j + 1) * BANK], as_f32(qk_hi[:, j % 2, :])).then_inc(qk_out[j % 2], 16)
                        sp.dma_start(s["qk"][b, 1, :, j * BANK:(j + 1) * BANK], as_f32(qk_lo[:, j % 2, :])).then_inc(qk_out[j % 2], 16)

                sp.sem_inc(w_in_[0], 16)
                load_w(1, 1)
                sp.dma_start(w_pool[:, :, :], a["w_pool"][0].rearrange("g c d -> c g d")).then_inc(w_pool_in, 16)
                for g in range(n_u):
                    load_w(g + 2, g % 2)
                    if g == n_u - 1:
                        store(0)
                    store_group(g)
                load_w(n_u + 2, 0)
                store(1)
                load_w(n_u + 3, 1)
                with sp.Fori(1, n_qk // 2 - 1) as i:
                    for e in range(2):
                        store(i * 2 + e)
                        load_w(i * 2 + (n_u + 2 + e), e)
                for e in range(2):
                    store(n_qk - 2 + e)
                for e in range(2):
                    sp.wait_ge(qk_out[e], stored(n_qk * groups // 2, 32))
                    sp.wait_ge(group_out[e], 16 * n_u * groups // 2)

            @block.scalar
            def _(act):
                act.sem_inc(hi_done, LEAD)

                def copy_u(b):
                    for j in range(groups):
                        act.wait_ge(out_done, done(b * groups + j, 8))
                        if j == 0 and b >= 1:
                            act.wait_ge(pool_done, b)
                        act.activation(u[:, pad + j * BANK:pad + (j + 1) * BANK], out_ps[half_of(b) + j][:, :], ACT.Copy).then_inc(u_read, 1)

                def copy_group(g):
                    for j in range(groups):
                        count = g * groups + j
                        act.wait_ge(group_done, count + 1)
                        if count >= 2:
                            act.wait_ge(group_out[j % 2], 16 * (count // 2))
                        act.activation(pool_out[:, j % 2, :], out_ps[j][:, :], ACT.Copy).then_inc(group_read, 1)

                def half_qk(i, e):
                    for j in range(groups):
                        count = (i * 2 + e) * groups + j
                        act.wait_ge(out_done, done(count + n_u * groups, 8))
                        act.wait_ge(qk_out[j % 2], stored((i * 2 + e) * (groups // 2) + j // 2, 32))
                        act.activation(qk_hi[:, j % 2, :], out_ps[half_of_qk(i, e) + j][:, :], ACT.Copy).then_inc(hi_done, 1)

                copy_u(0)
                for g in range(n_u - 1):
                    copy_u(g + 1)
                    copy_group(g)
                half_qk(0, 0)
                copy_group(n_u - 1)
                half_qk(0, 1)
                with act.Fori(1, n_qk // 2) as i:
                    for e in range(2):
                        half_qk(i, e)

            @block.vector
            def _(dve):
                for sem in (w_hi_done, w_lo_done):
                    dve.sem_inc(sem, LEAD)

                def split_w(b, i, slot):
                    dve.wait_ge(w_in_[slot], 16 * i + 16)
                    dve.wait_ge(out_done, done(b * groups - 1 - groups, 8))
                    dve.tensor_copy(w_hi[slot][:, :, :], w_f[slot][:, :, :]).then_inc(w_hi_done, 1)
                    dve.wait_ge(w_hi_done, done(b))
                    dve.tensor_tensor(w_lo[slot][:, :, :], w_f[slot][:, :, :], as_f32(w_hi[slot][:, :, :]), ALU.subtract).then_inc(w_lo_done, 1)

                steps = [0]

                def step(instruction):
                    steps[0] += 1
                    instruction.then_inc(pool_step, 1)
                    dve.wait_ge(pool_step, steps[0])

                split_w(0, 0, 0)
                split_w(1, 0, 1)
                step(dve.memset(u[:, 0:pad], 0.0))
                step(dve.memset(run[:, 0, 0:pad], 0.0))
                step(dve.memset(run[:, 1, 0:pad], 0.0))
                for b, window in enumerate(POOL_WINDOWS):
                    for t in range(pad):
                        last = dve.memset(ramp[:, t:t + 1], 1.0 / min(t + 1, window))
                    step(last)
                    dve.wait_ge(u_read, (b + 1) * groups)
                    src, width, side = u[:, :], 1, 0
                    while width < window:
                        dst = run[:, side, :]
                        step(dve.tensor_tensor(dst[:, pad:], src[:, pad:], src[:, pad - width:pad + seq - width], ALU.add))
                        src, width, side = dst, 2 * width, 1 - side
                    other = run[:, side, :]
                    step(dve.tensor_tensor(other[:, pad:2 * pad], src[:, pad:2 * pad], ramp[:, :], ALU.mult))
                    if b >= 1:
                        dve.wait_ge(group_done, groups * b)
                    step(dve.tensor_tensor(pooled[:, 0:pad], other[:, pad:2 * pad], u[:, pad:2 * pad], ALU.subtract))
                    dve.scalar_tensor_tensor(out=pooled[:, pad:], in0=src[:, 2 * pad:], scalar=1.0 / window,
                                             in1=u[:, 2 * pad:], op0=ALU.mult, op1=ALU.subtract).then_inc(pool_done, 1)
                    split_w(b + 2, (b + 2) // 2, b % 2)

                def split_qk(i, e):
                    for j in range(groups):
                        count = (i * 2 + e) * groups + j
                        dve.wait_ge(hi_done, done(count))
                        dve.wait_ge(qk_out[j % 2], stored((i * 2 + e) * (groups // 2) + j // 2, 32))
                        dve.tensor_tensor(qk_lo[:, j % 2, :], out_ps[half_of_qk(i, e) + j][:, :],
                                          as_f32(qk_hi[:, j % 2, :]), ALU.subtract).then_inc(qk_read, 1)

                for e in range(2):
                    split_qk(0, e)
                    split_w(n_u + 2 + e, n_u // 2 + 1, e)
                with dve.Fori(1, n_qk // 2 - 1) as i:
                    for e in range(2):
                        split_qk(i, e)
                        split_w(i * 2 + (n_u + 2 + e), i + (n_u // 2 + 1), e)
                for e in range(2):
                    split_qk(n_qk // 2 - 1, e)

            @block.tensor
            def _(pe):
                pe.sem_inc(out_done, 8)

                def block_product(b, slot, half, read, count):
                    pe.wait_ge(w_lo_done, done(b))
                    for j in range(groups):
                        if read is not None:
                            pe.wait_ge(read, count + j + 1)
                        for k in range(kc):
                            for t, (w, h) in enumerate(((w_hi, 0), (w_hi, 1), (w_lo, 0))):
                                m = pe.matmul(out_ps[half + j][:, :], w[slot][:, k, :], hT[h][:, k, j * BANK:(j + 1) * BANK],
                                              start=(k == 0 and t == 0), stop=(k == kc - 1 and t == 2))
                        m.then_inc(out_done, 1)

                def group_product(g, read, count):
                    pe.wait_ge(pool_done, g + 1)
                    for j in range(groups):
                        pe.wait_ge(read, count + j + 1)
                        pe.matmul(out_ps[j][:, :], w_pool[:, g, :], pooled[:, j * BANK:(j + 1) * BANK],
                                  start=True, stop=True).then_inc(group_done, 1)

                block_product(0, 0, half_of(0), None, 0)
                block_product(1, 1, half_of(1), None, 0)
                pe.wait_ge(w_pool_in, 16)
                group_product(0, u_read, 0)
                for g in range(1, n_u):
                    block_product(g + 1, (g + 1) % 2, half_of(g + 1), u_read, g * groups)
                    group_product(g, group_read, (g - 1) * groups)
                block_product(n_u + 1, (n_u + 1) % 2, half_of(n_u + 1), qk_read, 0)
                pe.wait_ge(group_read, n_u * groups)
                with pe.Fori(0, n_qk // 2 - 1) as i:
                    for e in range(2):
                        block_product(i * 2 + (n_u + 2 + e), e, 4 * e, qk_read, (i * 2 + e) * groups)


def phase_attention(nc, a, c, s, wide, bridge):
    tiles, seq = a["tiles"], a["seq"]
    per = BANK // P
    heads = a["d_attn"] // HEAD_DIM
    scale = HEAD_DIM ** -0.5
    lead = 8
    z_ring, stick_in, weight_ring, wT_ring = 4, 5, 4, 2
    weight_lag, turn_lag, hi_lag, lo_lag, values_lag, read_lag = 1, 4, 4, 5, 6, 6
    units = [(e, q, k * BANK, min((q + 1) * P - k * BANK, BANK), k == q // per, k == 0)
             for e in range(2) for q in range(tiles) for k in range(q // per, -1, -1)]
    total = len(units)
    per_head = total // 2
    last_unit = {(e, q): i for i, (e, q, _, _, _, last) in enumerate(units) if last}
    with ExitStack() as stack:
        n = Names(nc, stack)
        q_hi = [n.sb(f"q_hi{i}", [P, seq], F32R) for i in range(2)]
        q_lo = [n.sb(f"q_lo{i}", [P, seq], F32R) for i in range(2)]
        k_both = [n.sb(f"k_both{i}", [P, seq], F32R) for i in range(2)]
        v_both = [n.sb(f"v_both{i}", [P, tiles, 2, HEAD_DIM], F32R) for i in range(2)]
        rest = [n.sb(f"rest{i}", [P, BANK]) for i in range(stick_in)]
        beta = [n.sb(f"beta{i}", [P, BANK]) for i in range(stick_in)]
        stick = [n.sb(f"stick{i}", [P, seq + 1]) for i in range(2)]
        weight = [n.sb(f"weight{i}", [P, BANK]) for i in range(weight_ring)]
        wT = [n.sb(f"wT{i}", [P, per, 2, P], F32R) for i in range(wT_ring)]
        mixed = [n.sb(f"mixed{i}", [P, seq]) for i in range(2)]
        wo_f = bridge[:, 0:2, :]
        z_ps = [n.ps(f"z_ps{i}", [P, BANK]) for i in range(z_ring)]
        wT_ps = [n.ps(f"wT_ps{i}", [P, BANK]) for i in range(wT_ring)]
        o_ps = [n.ps(f"o_ps{i}", [P, 2, P]) for i in range(2)]
        head_in, mixed_out = n.sems("head_in", 2), n.sems("mixed_out", 2)
        head_parts = ((0, per, n.sem("head_start")), (per, 2 * per, n.sem("head_second")), (2 * per, tiles, head_in[0]))
        one_done, wo_hi_done, wo_done = (n.sem(x) for x in ("one_done", "wo_hi_done", "wo_done"))
        wo_in = n.sems("wo_in", 2)
        wo_rows = a["w_out"][0].rearrange("(c p) n -> c p n", p=P)
        (z_done, rest_done, beta_done, stick_done, weight_done, turned, hi_done, lo_done, pv_done, o_read) = (
            n.sem(x) for x in ("z_done", "rest_done", "beta_done", "stick_done", "weight_done",
                               "wT_turned", "wT_hi_done", "wT_lo_done", "pv_done", "o_read"))

        pairs = heads // 2
        last_read = max(weight_lag, turn_lag, hi_lag, lo_lag, values_lag, read_lag)

        def steps(eng, step):
            def behind_of(i, u):
                def behind(lag):
                    v = u - lag
                    if v < 0 and isinstance(i, int) or v >= total:
                        return None
                    return (v, i * total + v) if v >= 0 else (v + total, i * total + v)
                return behind

            for u in range(total):
                step(0, u, behind_of(0, u))
            with eng.Fori(1, pairs) as i:
                for u in range(total):
                    step(i, u, behind_of(i, u))
            for u in range(total, total + last_read):
                step(pairs - 1, u, behind_of(pairs - 1, u))

        def col(q, key):
            return seq - (q + 1) * P + key

        def wo_part(i, u):
            m = (u - per_head) // 2
            return m if isinstance(i, int) and i == 0 and (u - per_head) % 2 == 0 and 0 <= m < 2 * a["kc"] else None

        with nc.Block() as block:

            @block.sync
            def _(sp):
                for sem in mixed_out:
                    sp.sem_inc(sem, 16)

                def load_head(pair, e, sem, first=0, end=tiles):
                    half, cols = slice(e * HEAD_DIM, (e + 1) * HEAD_DIM), slice(first * P, end * P)
                    for hi_lo, dst in enumerate((q_hi, q_lo)):
                        twice = s["qk"][pair, hi_lo, half, cols].unsqueeze(0).broadcast_to([2, HEAD_DIM, (end - first) * P])
                        sp.dma_start(as_f32(dst[e][:, cols]), twice).then_inc(sem, 16)
                    sp.dma_start(as_f32(k_both[e][:, cols]), s["qk"][pair + heads // 2, :, half, cols]).then_inc(sem, 16)
                    sp.dma_start(as_f32(v_both[e][:, first:end, :, :]), s["v"][pair * 2 + e][:, first:end, :, :]).then_inc(sem, 16)

                def store_head(pair, e):
                    sp.wait_ge(o_read, done((pair * 2 + e + 1) * tiles - 1, lead))
                    row = (pair * 2 + e) * HEAD_DIM
                    sp.dma_start(s["merged"][bass.ds(a["d_pool"] + row, HEAD_DIM), :], mixed[e][0:HEAD_DIM, :]).then_inc(mixed_out[e], 16)
                    sp.dma_start(s["attn_low"][bass.ds(row, HEAD_DIM), :], mixed[e][HEAD_DIM:P, :]).then_inc(mixed_out[e], 16)

                for first, end, sem in head_parts:
                    load_head(0, 0, sem, first, end)
                load_head(0, 1, head_in[1])
                for m in range(2 * a["kc"]):
                    if m >= 2:
                        sp.wait_ge(wo_done, m - 1)
                    sp.dma_start(wo_f[:, m % 2, :], wo_rows[m // 2][:, (m % 2) * BANK:(m % 2 + 1) * BANK]).then_inc(wo_in[m % 2], 16)
                with sp.Fori(0, heads // 2 - 1) as i:
                    for e in range(2):
                        sp.wait_ge(pv_done, done(i * total + (e + 1) * per_head - 1, lead))
                        load_head(i + 1, e, head_in[e])
                        store_head(i, e)
                for e in range(2):
                    store_head(heads // 2 - 1, e)
                for e in range(2):
                    sp.wait_ge(mixed_out[e], stored(heads // 2, 32))

            @block.scalar
            def _(act):
                for sem in (rest_done, beta_done, hi_done):
                    act.sem_inc(sem, lead)

                def step(i, u, behind):
                    if u < total:
                        t, w = i * total + u, units[u][3]
                        act.wait_ge(z_done, done(t, lead))
                        act.wait_ge(stick_done, freed(t, stick_in, lead))
                        act.activation(rest[u % stick_in][:, 0:w], z_ps[u % z_ring][:, 0:w], ACT.Sigmoid, scale=-scale).then_inc(rest_done, 1)
                        act.wait_ge(weight_done, freed(t, stick_in, lead))
                        act.activation(beta[u % stick_in][:, 0:w], z_ps[u % z_ring][:, 0:w], ACT.Sigmoid, scale=scale).then_inc(beta_done, 1)
                    if behind(hi_lag):
                        v, t = behind(hi_lag)
                        w = units[v][3]
                        act.wait_ge(turned, done(t, lead))
                        act.wait_ge(pv_done, freed(t, wT_ring, lead))
                        act.activation(wT[v % wT_ring][:, 0:w // P, 0, :], wT_ps[v % wT_ring][:, 0:w].rearrange("p (b k) -> p b k", k=P), ACT.Copy).then_inc(hi_done, 1)

                steps(act, step)

            @block.gpsimd
            def _(pool):
                pool.sem_inc(weight_done, lead)

                def low_wo(m):
                    k, h = m // 2, m % 2
                    pool.wait_ge(wo_hi_done, m + 1)
                    pool.tensor_tensor(wide[2 + h][:, k, :], wo_f[:, h, :], as_f32(wide[h][:, k, :]), ALU.subtract).then_inc(wo_done, 1)

                def step(i, u, behind):
                    if wo_part(i, u) is not None:
                        low_wo(wo_part(i, u))
                    if behind(weight_lag):
                        v, t = behind(weight_lag)
                        e, q, key, w, first, _ = units[v]
                        pool.wait_ge(beta_done, done(t, lead))
                        pool.wait_ge(stick_done, done(t, lead))
                        pool.wait_ge(turned, freed(t, weight_ring, lead))
                        at = col(q, key) + 1
                        pool.tensor_tensor(weight[v % weight_ring][:, 0:w], beta[v % stick_in][:, 0:w], stick[q % 2][:, at:at + w],
                                           ALU.mult).then_inc(weight_done, 1)

                steps(pool, step)

            @block.vector
            def _(dve):
                for sem in (stick_done, lo_done, o_read):
                    dve.sem_inc(sem, lead)
                for i in range(2):
                    dve.memset(stick[i][:, seq:seq + 1], 1.0).then_inc(one_done, 1)
                dve.wait_ge(one_done, 2)

                def high_wo(m):
                    k, h = m // 2, m % 2
                    dve.wait_ge(wo_in[h], 16 * (k + 1))
                    dve.tensor_copy(wide[h][:, k, :], wo_f[:, h, :]).then_inc(wo_hi_done, 1)

                def step(i, u, behind):
                    if wo_part(i, u) is not None:
                        high_wo(wo_part(i, u))
                    if behind(lo_lag):
                        v, t = behind(lo_lag)
                        w = units[v][3]
                        dve.wait_ge(hi_done, done(t, lead))
                        dve.wait_ge(pv_done, freed(t, wT_ring, lead))
                        dve.tensor_tensor(wT[v % wT_ring][:, 0:w // P, 1, :], wT_ps[v % wT_ring][:, 0:w].rearrange("p (b k) -> p b k", k=P),
                                          as_f32(wT[v % wT_ring][:, 0:w // P, 0, :]), ALU.subtract).then_inc(lo_done, 1)
                    if u < total:
                        e, q, key, w, first, _ = units[u]
                        t = i * total + u
                        dve.wait_ge(rest_done, done(t, lead))
                        if first:
                            if e or q >= 2:
                                before = last_unit[(e, q - 2)] if q >= 2 else last_unit[(0, tiles - 2 + q)]
                                dve.wait_ge(weight_done, done(i * total + before, lead))
                            elif not isinstance(i, int):
                                dve.wait_ge(weight_done, done(i * total + (last_unit[(1, tiles - 2 + q)] - total), lead))
                            start = 1.0
                        else:
                            dve.wait_ge(stick_done, freed(t, 1, lead))
                            start = stick[q % 2][:, col(q, key) + w:col(q, key) + w + 1]
                        at = col(q, key)
                        backwards = rest[u % stick_in][:, 0:w][:, ::-1]
                        dve.tensor_tensor_scan(stick[q % 2][:, at:at + w][:, ::-1], backwards, backwards, start,
                                               ALU.mult, ALU.bypass).then_inc(stick_done, 1)

                    if behind(read_lag) and units[behind(read_lag)[0]][5]:
                        v, t = behind(read_lag)
                        e, q = units[v][0:2]
                        dve.wait_ge(pv_done, done(t, lead))
                        if q == 0:
                            dve.wait_ge(mixed_out[e], stored(i if u >= read_lag else i - 1, 32))
                        dve.tensor_reduce(mixed[e][:, q * P:(q + 1) * P], o_ps[q % 2][:, :, :].rearrange("e h k -> e k h"), AX.X,
                                          ALU.add).then_inc(o_read, 1)

                steps(dve, step)

            @block.tensor
            def _(pe):
                for sem in (z_done, turned, pv_done):
                    pe.sem_inc(sem, lead)

                def scores(i, u):
                    e, q, key, w, first, _ = units[u]
                    if isinstance(i, int) and i == 0 and e == 0:
                        for start, _, sem in head_parts:
                            if first and q == start:
                                pe.wait_ge(sem, 16 * 4)
                    elif u % per_head == 0:
                        pe.wait_ge(head_in[e], 16 * 4 * i + 16 * 4)
                    pe.wait_ge(beta_done, freed(i * total + u, z_ring, lead))
                    for k, half in enumerate((q_hi, q_lo)):
                        m = pe.matmul(z_ps[u % z_ring][:, 0:w], half[e][:, q * P:(q + 1) * P], k_both[e][:, key:key + w],
                                      start=(k == 0), stop=(k == 1))
                        if first and k == 0:
                            pe.matmul(z_ps[u % z_ring][:, w - P:w], c["ident_r"][:, :], c["not_before"][:, :], start=False, stop=False)
                    m.then_inc(z_done, 1)

                def turn(u, t):
                    w = units[u][3]
                    pe.wait_ge(weight_done, done(t, lead))
                    pe.wait_ge(lo_done, freed(t, wT_ring, lead))
                    for b in range(w // P):
                        m = pe.transpose(wT_ps[u % wT_ring][:, b * P:(b + 1) * P], weight[u % weight_ring][:, b * P:(b + 1) * P], c["ident"][:, :])
                    m.then_inc(turned, 1)

                def values(i, u, t):
                    e, q, key, w, first, last = units[u]
                    pe.wait_ge(lo_done, done(t, lead))
                    if first:
                        pe.wait_ge(o_read, freed(i * (2 * tiles) + (e * tiles + q), 2, lead))
                    for b in range(w // P):
                        m = pe.matmul(o_ps[q % 2][:, :, :], v_both[e][:, key // P + b, :, :], wT[u % wT_ring][:, b, :, :],
                                      start=(first and b == 0), stop=(last and b == w // P - 1))
                    m.then_inc(pv_done, 1)

                def step(i, u, behind):
                    if u < total:
                        scores(i, u)
                    if behind(turn_lag):
                        turn(*behind(turn_lag))
                    if behind(values_lag):
                        values(i if u >= values_lag else i - 1, *behind(values_lag))

                steps(pe, step)


def phase_mix(nc, a, c, s, wide, bridge, up_start):
    tiles, kc, d = a["tiles"], a["kc"], a["d"]
    n_pool = a["d_pool"] // P
    part_width = a["d_pool"]
    scales = c["cols"][:, 4 * a["n_ff2"]:4 * a["n_ff2"] + kc]
    with ExitStack() as stack:
        n = Names(nc, stack)
        w_hi, w_lo = wide[0:2], wide[2:4]
        merged = [n.sb(f"merged{i}", [P, kc, P]) for i in range(2)]
        attn_low = [n.sb(f"attn_low{i}", [P, kc - n_pool, P]) for i in range(2)]
        m_hi = [n.sb(f"m_hi{i}", [P, kc, P], F32R) for i in range(2)]
        m_lo = [n.sb(f"m_lo{i}", [P, kc, P], F32R) for i in range(2)]
        squares = n.sb("m_squares", [P, kc, P])
        junk = n.sb("junk", [P, d], mybir.dt.bfloat16)
        sums = n.sb("sums", [P, 2, P])
        xt = [n.sb(f"xo{i}", [P, d]) for i in range(2)]
        mix = [n.sb(f"mix{i}", [P, d]) for i in range(2)]
        hn = [n.sb(f"hn{i}", [P, d]) for i in range(2)]
        h_hi = [n.sb(f"h2_hi{i}", [P, kc, P], F32R) for i in range(2)]
        h_lo = [n.sb(f"h2_lo{i}", [P, kc, P], F32R) for i in range(2)]
        gains = bridge[:, :, :].rearrange("p (g c) n -> p g (c n)", g=2)
        stat = n.sb("stat_mix", [P, 2, 12])
        pool_ps, attn_ps = n.ps("pool_ps", [P, d]), n.ps("attn_ps", [P, d])
        turn_ps = n.ps("h2_turn_ps", [P, d])
        ss_ps = n.ps("ss_ps", [P, 2, 2])
        merged_in, x_in, x2_out, hT_out = (n.sems(x, 2) for x in ("merged_in", "xo_in", "x2_out", "h2T_out"))
        names = ("gain_post_in", "gain_pre_in", "start_h_in", "start_w_in", "start_hi_done", "m_whole", "m_sq", "m_sum", "m_scaled", "m_hi_done", "m_lo_done", "ss_done",
                 "roots_done", "recips_done", "pool_mm_done", "mix_mm_done", "pool_scaled", "mix_done", "mix_sq", "mix_root", "mix_recip", "y_done",
                 "x2_done", "x2_stored", "x2_sq", "x2_root", "x2_recip", "hn_done", "h2_turned", "h2_hi_done", "h2_lo_done")
        (gain_post_in, gain_pre_in, start_h_in, start_w_in, start_hi_done, m_whole, m_sq, m_sum, m_scaled, m_hi_done, m_lo_done, ss_done, roots_done, recips_done,
         pool_mm_done, mix_mm_done, pool_scaled, mix_done, mix_sq, mix_root, mix_recip, y_done, x2_done, x2_stored, x2_sq, x2_root, x2_recip,
         hn_done, turned, hi_done, lo_done) = (n.sem(x) for x in names)
        x_tiles = a["x"][0].rearrange("(t p) d -> t p d", p=P)
        w_up = a["w_up"][0].rearrange("(c p) (h b n) -> b p h c n", p=P, h=2, n=P)
        m_cols = s["merged"].rearrange("(c p) t -> p c t", p=P)
        low_cols = s["attn_low"].rearrange("(c p) t -> p c t", p=P)

        def steps(eng, step, after_loop=2):
            for t in range(2):
                step(t, t % 2, 0)
            with eng.Fori(0, (tiles - after_loop) // 2 - 1) as i:
                for e in range(2):
                    step(i * 2 + (2 + e), e, i + 1)
            for t in range(tiles - after_loop, tiles + 2):
                step(t, t % 2, t // 2)

        def is_tile(t):
            return not isinstance(t, int) or 0 <= t < tiles

        with nc.Block() as block:

            @block.sync
            def _(sp):
                for sem in hT_out:
                    sp.sem_inc(sem, 16)

                def load_merged(t, slot):
                    sp.wait_ge(m_lo_done, freed(t))
                    sp.dma_start(attn_low[slot][:, :, :], low_cols[:, :, bass.ts(t, P)]).then_inc(merged_in[slot], 16)
                    sp.dma_start(merged[slot][:, :, :], m_cols[:, :, bass.ts(t, P)]).then_inc(merged_in[slot], 16)

                def load_x(t, slot):
                    sp.wait_ge(hn_done, freed(t))
                    sp.wait_ge(x2_stored, freed(t))
                    sp.dma_start(xt[slot][:, :], x_tiles[t]).then_inc(x_in[slot], 16)

                def store_h(t, slot):
                    sp.wait_ge(lo_done, done(t))
                    sp.dma_start(s["h2T"][0][:, :, bass.ts(t, P)], as_f32(h_hi[slot][:, :, :])).then_inc(hT_out[slot], 16)
                    sp.dma_start(s["h2T"][1][:, :, bass.ts(t, P)], as_f32(h_lo[slot][:, :, :])).then_inc(hT_out[slot], 16)

                load_merged(0, 0)
                load_merged(1, 1)
                load_x(0, 0)
                load_x(1, 1)
                for i, (name, sem) in enumerate((("norm_mix_post", gain_post_in), ("norm_ffn_pre", gain_pre_in))):
                    sp.dma_start(gains[:, i, :], a[name][0].partition_broadcast(P)).then_inc(sem, 16)

                def step(t, slot, uses):
                    if is_tile(t + 2) and not (isinstance(t, int) and t >= tiles - 2):
                        load_merged(t + 2, slot)
                    if is_tile(t) and not (isinstance(t, int) and t < 2):
                        load_x(t, slot)
                    if is_tile(t - 2):
                        store_h(t - 2, slot)
                    if isinstance(t, int) and tiles - 4 <= t < tiles:
                        part = t - (tiles - 4)
                        rows = slice(part * kc // 4, (part + 1) * kc // 4)
                        if part == 0:
                            for e in range(2):
                                sp.wait_ge(hT_out[e], stored(BANK // P // 2, 32))
                        if part < 2:
                            sp.dma_start(up_start["w_f"][:, part, :, :], w_up[0][:, part, :, :]).then_inc(start_w_in, 16)
                        for h in range(2):
                            sp.dma_start(as_f32(up_start["h"][h][:, rows, :]), s["h2T"][h][:, rows, 0:BANK]).then_inc(start_h_in, 16)

                steps(sp, step, after_loop=4)
                for e in range(2):
                    sp.wait_ge(hT_out[e], stored(tiles // 2, 32))
                sp.wait_ge(start_h_in, 128)

            @block.gpsimd
            def _(pool):
                for sem in (x2_done, x2_stored):
                    pool.sem_inc(sem, LEAD)

                def step(t, slot, uses):
                    if is_tile(t):
                        pool.wait_ge(y_done, done(t))
                        pool.wait_ge(x_in[slot], 16 * uses + 16)
                        pool.tensor_tensor(xt[slot][:, :], xt[slot][:, :], mix[slot][:, :], ALU.add).then_inc(x2_done, 1)
                        pool.wait_ge(x2_done, done(t))
                        pool.dma_start(s["x2"][t], xt[slot][:, :]).then_inc(x2_out[slot], 16)
                        pool.wait_ge(x2_out[slot], 16 * uses + 16)
                        pool.sem_inc(x2_stored, 1)

                steps(pool, step)

            @block.scalar
            def _(act):
                for sem in (m_sq, m_hi_done, roots_done, pool_scaled, mix_sq, mix_root, x2_sq, x2_root, hi_done):
                    act.sem_inc(sem, LEAD)

                def root(out, in_, width, sem):
                    act.activation(out, in_, ACT.Sqrt, scale=1.0 / width, bias=c["eps"][:, 0:1]).then_inc(sem, 1)

                def square_merged(t, slot, uses):
                    act.wait_ge(m_whole, done(t))
                    act.wait_ge(m_sum, freed(t, 1))
                    act.activation(squares[:, :, :], merged[slot][:, :, :], ACT.Square).then_inc(m_sq, 1)

                def half_merged(t, slot):
                    act.wait_ge(m_scaled, done(t))
                    act.wait_ge(mix_mm_done, freed(t))
                    act.activation(m_hi[slot][:, :, :], merged[slot][:, :, :], ACT.Copy).then_inc(m_hi_done, 1)

                def step(t, slot, uses):
                    if is_tile(t):
                        act.wait_ge(ss_done, done(t))
                        act.wait_ge(recips_done, freed(t))
                        root(stat[:, slot, 0:2], ss_ps[:, slot, :], part_width, roots_done)
                    if is_tile(t + 1):
                        square_merged(t + 1, 1 - slot, uses + slot)
                    if is_tile(t):
                        act.wait_ge(recips_done, done(t))
                        act.wait_ge(pool_mm_done, done(t))
                        act.wait_ge(x2_done, freed(t))
                        act.activation(mix[slot][:, :], pool_ps[:, :], ACT.Copy, scale=stat[:, slot, 2:3]).then_inc(pool_scaled, 1)
                    if is_tile(t + 1):
                        half_merged(t + 1, 1 - slot)
                    if is_tile(t - 1):
                        act.wait_ge(x2_done, done(t - 1))
                        act.activation(junk[:, :], xt[1 - slot][:, :], ACT.Square, accum_out=stat[:, 1 - slot, 7:8]).then_inc(x2_sq, 1)
                        act.wait_ge(x2_sq, done(t - 1))
                        root(stat[:, 1 - slot, 8:9], stat[:, 1 - slot, 7:8], d, x2_root)
                    if is_tile(t - 2):
                        act.wait_ge(turned, done(t - 2))
                        act.wait_ge(hT_out[slot], stored(uses - 1, 32))
                        act.activation(h_hi[slot][:, :, :].rearrange("p c t -> p (c t)"), turn_ps[:, :], ACT.Copy).then_inc(hi_done, 1)
                    if is_tile(t):
                        act.wait_ge(mix_done, done(t))
                        act.wait_ge(x2_sq, freed(t, 1))
                        act.activation(junk[:, :], mix[slot][:, :], ACT.Square, accum_out=stat[:, slot, 4:5]).then_inc(mix_sq, 1)
                        act.wait_ge(mix_sq, done(t))
                        root(stat[:, slot, 5:6], stat[:, slot, 4:5], d, mix_root)

                square_merged(0, 0, 0)
                half_merged(0, 0)
                steps(act, step)
                act.wait_ge(start_w_in, 32)
                act.activation(up_start["w_hi"][:, :, :, :], up_start["w_f"][:, :, :, :], ACT.Copy).then_inc(start_hi_done, 1)

            @block.vector
            def _(dve):
                for sem in (m_whole, m_sum, m_scaled, m_lo_done, recips_done, mix_done, mix_recip, y_done, x2_recip, hn_done, lo_done):
                    dve.sem_inc(sem, LEAD)

                def whole(t, slot, uses):
                    dve.wait_ge(merged_in[slot], 32 * uses + 32)
                    dve.tensor_tensor(merged[slot][:, n_pool:, :], merged[slot][:, n_pool:, :], attn_low[slot][:, :, :], ALU.add).then_inc(m_whole, 1)

                def prepare(t, slot):
                    dve.wait_ge(m_sq, done(t))
                    dve.tensor_tensor(merged[slot][:, :, :], merged[slot][:, :, :], scales.unsqueeze(2).broadcast_to([P, kc, P]),
                                      ALU.mult).then_inc(m_scaled, 1)
                    dve.wait_ge(ss_done, freed(t, 1))
                    dve.tensor_reduce(sums[:, :, :], squares[:, :, :].rearrange("p (h c) t -> p h t c", h=2), AX.X, ALU.add).then_inc(m_sum, 1)
                    dve.wait_ge(m_hi_done, done(t))
                    dve.wait_ge(mix_mm_done, freed(t))
                    dve.tensor_tensor(m_lo[slot][:, :, :], merged[slot][:, :, :], as_f32(m_hi[slot][:, :, :]), ALU.subtract).then_inc(m_lo_done, 1)

                whole(0, 0, 0)
                prepare(0, 0)
                whole(1, 1, 0)
                dve.wait_ge(gain_post_in, 16)
                dve.wait_ge(gain_pre_in, 16)

                def step(t, slot, uses):
                    if is_tile(t):
                        dve.wait_ge(roots_done, done(t))
                        dve.reciprocal(stat[:, slot, 2:4], stat[:, slot, 0:2]).then_inc(recips_done, 1)
                    if is_tile(t - 1):
                        dve.wait_ge(mix_root, done(t - 1))
                        dve.reciprocal(stat[:, 1 - slot, 6:7], stat[:, 1 - slot, 5:6]).then_inc(mix_recip, 1)
                        dve.wait_ge(mix_recip, done(t - 1))
                        dve.scalar_tensor_tensor(out=mix[1 - slot][:, :], in0=mix[1 - slot][:, :], scalar=stat[:, 1 - slot, 6:7],
                                                 in1=gains[:, 0, :], op0=ALU.mult, op1=ALU.mult).then_inc(y_done, 1)
                    if is_tile(t + 1):
                        prepare(t + 1, 1 - slot)
                    if is_tile(t - 2):
                        dve.wait_ge(hi_done, done(t - 2))
                        dve.wait_ge(hT_out[slot], stored(uses - 1, 32))
                        dve.tensor_tensor(h_lo[slot][:, :, :].rearrange("p c t -> p (c t)"), turn_ps[:, :],
                                          as_f32(h_hi[slot][:, :, :].rearrange("p c t -> p (c t)")), ALU.subtract).then_inc(lo_done, 1)
                    if is_tile(t - 1):
                        dve.wait_ge(x2_root, done(t - 1))
                        dve.reciprocal(stat[:, 1 - slot, 9:10], stat[:, 1 - slot, 8:9]).then_inc(x2_recip, 1)
                        dve.wait_ge(x2_recip, done(t - 1))
                        dve.wait_ge(turned, freed(t - 1))
                        dve.scalar_tensor_tensor(out=hn[1 - slot][:, :], in0=xt[1 - slot][:, :], scalar=stat[:, 1 - slot, 9:10],
                                                 in1=gains[:, 1, :], op0=ALU.mult, op1=ALU.mult).then_inc(hn_done, 1)
                    if is_tile(t):
                        dve.wait_ge(pool_scaled, done(t))
                        dve.wait_ge(mix_mm_done, done(t))
                        dve.scalar_tensor_tensor(out=mix[slot][:, :], in0=attn_ps[:, :], scalar=stat[:, slot, 3:4], in1=mix[slot][:, :],
                                                 op0=ALU.mult, op1=ALU.add).then_inc(mix_done, 1)
                    if is_tile(t + 2) and not (isinstance(t, int) and t >= tiles - 2):
                        whole(t + 2, slot, uses + 1)

                steps(dve, step)
                dve.wait_ge(start_hi_done, 1)
                dve.tensor_tensor(up_start["w_lo"][:, :, :, :], up_start["w_f"][:, :, :, :], as_f32(up_start["w_hi"][:, :, :, :]), ALU.subtract)

            @block.tensor
            def _(pe):
                for sem in (ss_done, pool_mm_done, mix_mm_done, turned):
                    pe.sem_inc(sem, LEAD)

                def token_sums(t, slot):
                    pe.wait_ge(m_sum, done(t))
                    pe.wait_ge(roots_done, freed(t, 1))
                    for h in range(2):
                        m = pe.matmul(ss_ps[:, slot, h:h + 1], sums[:, h, :], c["ones"][:, 0:1], start=True, stop=True)
                    m.then_inc(ss_done, 1)

                def turn(t, slot):
                    pe.wait_ge(hn_done, done(t))
                    pe.wait_ge(lo_done, freed(t, 1))
                    for k in range(kc):
                        m = pe.transpose(turn_ps[:, k * P:(k + 1) * P], hn[slot][:, k * P:(k + 1) * P], c["ident"][:, :])
                    m.then_inc(turned, 1)

                def part_product(part, t, slot):
                    bank, sem, free = ((pool_ps, pool_mm_done, pool_scaled), (attn_ps, mix_mm_done, mix_done))[part]
                    pe.wait_ge(free, freed(t, 1))
                    for k in range(n_pool):
                        row = part * n_pool + k
                        for j, (m, w) in enumerate(((m_hi, w_hi), (m_hi, w_lo), (m_lo, w_hi))):
                            for half in range(d // BANK):
                                cols = slice(half * BANK, (half + 1) * BANK)
                                mm = pe.matmul(bank[:, cols], m[slot][:, row, :], w[half][:, row, :],
                                               start=(k == 0 and j == 0), stop=(k == n_pool - 1 and j == 2))
                    mm.then_inc(sem, 1)

                def step(t, slot, uses):
                    if is_tile(t):
                        pe.wait_ge(m_lo_done, done(t))
                        part_product(0, t, slot)
                    if is_tile(t - 2):
                        turn(t - 2, slot)
                    if is_tile(t):
                        part_product(1, t, slot)
                    if is_tile(t + 1):
                        token_sums(t + 1, 1 - slot)

                token_sums(0, 0)
                steps(pe, step)


def phase_up(nc, a, c, s, wide, up_start, down_start):
    kc, seq = a["kc"], a["seq"]
    groups = seq // BANK
    n_ff = a["n_ff2"] // 2
    lead = 4
    with ExitStack() as stack:
        n = Names(nc, stack)
        hT = [[up_start["h"][i], n.sb(f"h2T{i}", [P, kc, BANK], F32R), wide[2 * i], wide[2 * i + 1]] for i in range(2)]
        w_f = [up_start["w_f"], n.sb("wu_f1", [P, 2, kc, P])]
        w_hi = [up_start["w_hi"], n.sb("wu_hi1", [P, 2, kc, P], F32R)]
        w_lo = [up_start["w_lo"], n.sb("wu_lo1", [P, 2, kc, P], F32R)]
        conv = [[n.sb(f"conv{i}_{x}", [P, BANK]) for x in range(2)] for i in range(2)]
        f = [n.sb(f"f{i}", [P, BANK]) for i in range(2)]
        ps = [n.ps("gate_ps", [P, seq]), n.ps("value_ps", [P, seq])]
        w_in_, f_out = n.sems("wu_in", 2), n.sems("f_out", 2)
        h_in = n.sems("h2T_in", groups)
        start_in, start_hi_done = n.sems("down_start_in", 2), n.sem("down_hi_done")
        names = ("wu_hi_done", "wu_done", "up_done", "tap_done", "conv_step", "silu_done", "f_done", "taps_done")
        wu_hi_done, wu_done, up_done, tap_done, conv_step, silu_done, f_done, taps_done = (n.sem(x) for x in names)
        w_cols = a["w_up"][0].rearrange("(c p) (h b n) -> b p h c n", p=P, h=2, n=P)
        taps = n.sb("taps", [P, 2, 4, 2, 1])
        columns = c["cols"][:, 0:4 * a["n_ff2"]].rearrange("p (k h j) -> p k h j", k=4, h=2)

        def column(kind, h, slot):
            return taps[:, slot, kind, h, :]

        with nc.Block() as block:

            @block.sync
            def _(sp):
                for sem in f_out:
                    sp.sem_inc(sem, 16)

                def load_w(j, slot):
                    sp.wait_ge(wu_done, freed(j))
                    for h in range(2):
                        sp.dma_start(w_f[slot][:, h, :, :], w_cols[j][:, h, :, :]).then_inc(w_in_[slot], 16)

                def load_h(j):
                    for i in range(2):
                        sp.dma_start(as_f32(hT[i][j][:, :, :]), s["h2T"][i][:, :, j * BANK:(j + 1) * BANK]).then_inc(h_in[j], 16)

                sp.sem_inc(w_in_[0], 32)
                sp.sem_inc(h_in[0], 32)
                load_h(1)
                load_w(1, 1)
                for j in range(2, groups):
                    load_h(j)

                def store(j, g):
                    sp.wait_ge(f_done, done(j * groups + g, lead))
                    sp.dma_start(s["f"][j][:, g * BANK:(g + 1) * BANK], f[g % 2][:, :]).then_inc(f_out[g % 2], 16)

                with sp.Fori(0, n_ff // 2 - 1) as i:
                    for e in range(2):
                        load_w(i * 2 + (2 + e), e)
                        for g in range(groups):
                            store(i * 2 + e, g)
                sp.wait_ge(f_out[0], stored(groups))
                for k in range(2):
                    sp.dma_start(down_start["w_f"][k], a["w_down"][0][k * P:(k + 1) * P, :]).then_inc(start_in[k], 16)
                    sp.dma_start(down_start["f_f"][k], s["f"][k][:, 0:BANK]).then_inc(start_in[k], 16)
                for e in range(2):
                    for g in range(groups):
                        store(n_ff - 2 + e, g)
                for e in range(2):
                    sp.wait_ge(f_out[e], stored(n_ff * groups // 2))
                for k in range(2):
                    sp.wait_ge(start_in[k], 32)

            def blocks_of(eng, block_step):
                with eng.Fori(0, n_ff // 2 - 1) as i:
                    for e in range(2):
                        block_step(i * 2 + e, i, e, False)
                for e in range(2):
                    block_step(n_ff - 2 + e, n_ff // 2 - 1, e, e == 1)

            @block.scalar
            def _(act):
                for sem in (tap_done, silu_done):
                    act.sem_inc(sem, LEAD)
                act.sem_inc(wu_hi_done, done(0))

                def half_w(j, i, slot):
                    act.wait_ge(w_in_[slot], 32 * i + 32)
                    act.wait_ge(up_done, freed(j * 2 * groups - 1, 2 * groups, 4 * groups))
                    act.activation(w_hi[slot][:, :, :, :], w_f[slot][:, :, :, :], ACT.Copy).then_inc(wu_hi_done, 1)

                def block_step(j, i, slot, last):
                    for g in range(groups):
                        count = j * groups + g
                        if g == 0 and not last:
                            half_w(j + 1, i + slot, 1 - slot)
                        for h in range(2):
                            act.wait_ge(up_done, done(count * 2 + h, 4 * groups))
                            act.wait_ge(taps_done, j + 1)
                            act.wait_ge(f_done, freed(count, 2, lead))
                            act.activation(conv[g % 2][h][:, :], ps[h][:, g * BANK:(g + 1) * BANK], ACT.Identity,
                                           scale=column(3, h, slot), bias=column(0, h, slot)).then_inc(tap_done, 1)
                        act.wait_ge(conv_step, 4 * count + 3)
                        act.activation(conv[g % 2][0][:, :], conv[g % 2][0][:, :], ACT.Silu).then_inc(silu_done, 1)

                blocks_of(act, block_step)
                act.wait_ge(start_in[0], 32)
                act.wait_ge(up_done, done((n_ff - 1) * 2 * groups - 1, 4 * groups))
                act.activation(down_start["w_hi"], down_start["w_f"][0], ACT.Copy).then_inc(start_hi_done, 1)
                act.activation(down_start["f_hi"], down_start["f_f"][0], ACT.Copy).then_inc(start_hi_done, 1)

            @block.vector
            def _(dve):
                dve.sem_inc(f_done, lead)
                dve.sem_inc(wu_done, done(0))

                def copy_taps(j, slot):
                    dve.tensor_scalar(taps[:, slot, :, :, :], columns[:, :, :, bass.ds(j, 1)], 1.0, None, ALU.mult).then_inc(taps_done, 1)

                def split_w(j, slot):
                    dve.wait_ge(f_done, freed(j * groups, groups + 1, lead))
                    copy_taps(j, slot)
                    dve.wait_ge(wu_hi_done, done(j))
                    dve.wait_ge(up_done, freed(j * 2 * groups - 1, 2 * groups, 4 * groups))
                    dve.tensor_tensor(w_lo[slot][:, :, :, :], w_f[slot][:, :, :, :], as_f32(w_hi[slot][:, :, :, :]), ALU.subtract).then_inc(wu_done, 1)

                def block_step(j, i, slot, last):
                    for g in range(groups):
                        count = j * groups + g
                        if g == 0 and not last:
                            split_w(j + 1, 1 - slot)
                        for back, kind in ((1, 2), (2, 1)):
                            skip = back if g == 0 else 0
                            for h in range(2):
                                if back == 1:
                                    dve.wait_ge(tap_done, done(count * 2 + h))
                                else:
                                    dve.wait_ge(conv_step, 4 * count + 1 + h)
                                out = conv[g % 2][h][:, skip:]
                                dve.wait_ge(taps_done, j + 1)
                                dve.scalar_tensor_tensor(out=out, in0=ps[h][:, g * BANK - back + skip:(g + 1) * BANK - back],
                                                         scalar=column(kind, h, slot), in1=out, op0=ALU.mult, op1=ALU.add).then_inc(conv_step, 1)
                        dve.wait_ge(silu_done, done(count))
                        dve.wait_ge(conv_step, 4 * count + 4)
                        dve.wait_ge(f_out[g % 2], stored(j * (groups // 2) + g // 2))
                        dve.tensor_tensor(f[g % 2][:, :], conv[g % 2][0][:, :], conv[g % 2][1][:, :], ALU.mult).then_inc(f_done, 1)

                copy_taps(0, 0)
                blocks_of(dve, block_step)
                dve.wait_ge(start_hi_done, 2)
                for x in ("w", "f"):
                    dve.tensor_tensor(down_start[x + "_lo"], down_start[x + "_f"][0], as_f32(down_start[x + "_hi"]), ALU.subtract)

            @block.tensor
            def _(pe):
                pe.sem_inc(up_done, 4 * groups)

                def block_step(j, i, slot, last):
                    pe.wait_ge(wu_done, done(j))
                    for g in range(groups):
                        pe.wait_ge(h_in[g], 32)
                        pe.wait_ge(f_done, freed(j * groups + g, groups - (1 if g < groups - 1 else 0), lead))
                        for h in range(2):
                            for k in range(kc):
                                for t, (w, x) in enumerate(((w_hi, 0), (w_hi, 1), (w_lo, 0))):
                                    m = pe.matmul(ps[h][:, g * BANK:(g + 1) * BANK], w[slot][:, h, k, :], hT[x][g][:, k, :],
                                                  start=(k == 0 and t == 0), stop=(k == kc - 1 and t == 2))
                            m.then_inc(up_done, 1)

                blocks_of(pe, block_step)


def phase_down(nc, a, c, s, out, down_start):
    seq, d = a["seq"], a["d"]
    groups, per = seq // BANK, BANK // P
    n_ff = a["n_ff2"] // 2
    with ExitStack() as stack:
        n = Names(nc, stack)
        w_f, f_f = down_start["w_f"], down_start["f_f"]
        w_hi = [down_start["w_hi"], n.sb("wd_hi1", [P, d], F32R)]
        w_lo = [down_start["w_lo"], n.sb("wd_lo1", [P, d], F32R)]
        f_hi = [down_start["f_hi"], n.sb("fd_hi1", [P, BANK], F32R)]
        f_lo = [down_start["f_lo"], n.sb("fd_lo1", [P, BANK], F32R)]
        gain = n.sb("gain_down", [P, d])
        junk = n.sb("junk_down", [P, d], mybir.dt.bfloat16)
        x2 = [n.sb(f"x2_{i}", [P, d]) for i in range(per)]
        y = [n.sb(f"y{i}", [P, d]) for i in range(per)]
        stat = n.sb("stat_down", [P, per, 4])
        ps = [n.ps(f"down_ps{i}", [P, d]) for i in range(per)]
        load_in = n.sems("down_in", 2)
        x2_in, y_out = n.sems("x2_in", per), n.sems("y_out", per)
        names = ("gain_down_in", "half_done", "split_done", "k_done", "sq_down", "root_down", "recip_down", "scaled_down", "added_down", "y_free")
        gain_in, half_done, split_done, k_done, sq_done, root_done, recip_done, scaled, added, y_free = (n.sem(x) for x in names)
        w_rows = a["w_down"][0].rearrange("(c p) n -> c p n", p=P)
        counted = n_ff - 1 + per

        def slot_free(i, k):
            return i * counted + ((1, per + 1)[k] if k < 2 else per + k)

        out_tiles = out[0].rearrange("(g t p) d -> g t p d", t=per, p=P)
        x2_tiles = s["x2"].rearrange("(g t) p d -> g t p d", t=per)

        with nc.Block() as block:

            @block.sync
            def _(sp):
                sp.dma_start(gain[:, :], a["norm_ffn_post"][0].partition_broadcast(P)).then_inc(gain_in, 16)
                for sem in load_in:
                    sp.sem_inc(sem, 32)

                def load(i, k):
                    sp.wait_ge(split_done, freed(i * n_ff + k))
                    sp.dma_start(w_f[k % 2][:, :], w_rows[k]).then_inc(load_in[k % 2], 16)
                    sp.dma_start(f_f[k % 2][:, :], s["f"][k][:, bass.ts(i, BANK)]).then_inc(load_in[k % 2], 16)

                def group(i, last):
                    for k in range(2, n_ff):
                        load(i, k)
                        if k == 4:
                            for t in range(per):
                                sp.wait_ge(added, freed(i * per + t, per, per))
                                sp.dma_start(x2[t][:, :], x2_tiles[i, t]).then_inc(x2_in[t], 16)
                    if not last:
                        load(i + 1, 0)
                        load(i + 1, 1)

                with sp.Fori(0, groups - 1) as i:
                    group(i, False)
                group(groups - 1, True)

            @block.gpsimd
            def _(pool):
                for sem in (added, y_free):
                    pool.sem_inc(sem, per)
                with pool.Fori(0, groups) as i:
                    for t in range(per):
                        pool.wait_ge(scaled, done(i * per + t, per))
                        pool.wait_ge(x2_in[t], 16 * i + 16)
                        pool.tensor_tensor(y[t][:, :], y[t][:, :], x2[t][:, :], ALU.add).then_inc(added, 1)
                        pool.wait_ge(added, done(i * per + t, per))
                        pool.dma_start(out_tiles[i, t], y[t][:, :]).then_inc(y_out[t], 16)
                    for t in range(per):
                        pool.wait_ge(y_out[t], 16 * i + 16)
                        pool.sem_inc(y_free, 1)

            @block.scalar
            def _(act):
                act.sem_inc(half_done, done(0))
                act.sem_inc(sq_done, LEAD)

                def half(i, k):
                    act.wait_ge(load_in[k % 2], 32 * (i * (n_ff // 2) + k // 2) + 32)
                    act.wait_ge(k_done, slot_free(i, k))
                    act.activation(w_hi[k % 2][:, :], w_f[k % 2][:, :], ACT.Copy)
                    act.activation(f_hi[k % 2][:, :], f_f[k % 2][:, :], ACT.Copy).then_inc(half_done, 1)

                def statistics(i, t):
                    count = i * per + t
                    act.wait_ge(k_done, done(i * counted + (n_ff - 1 + t), per + 1))
                    act.wait_ge(sq_done, freed(count, 1, 2))
                    act.activation(junk[:, :], ps[t][:, :], ACT.Square, accum_out=stat[:, t, 0:1]).then_inc(sq_done, 1)
                    act.wait_ge(sq_done, done(count, 2))
                    act.activation(stat[:, t, 1:2], stat[:, t, 0:1], ACT.Sqrt, scale=1.0 / d, bias=c["eps"][:, 0:1]).then_inc(root_done, 1)

                def group(i, last):
                    for k in range(2, n_ff):
                        half(i, k)
                    if not last:
                        half(i + 1, 0)
                    for t in range(per):
                        statistics(i, t)
                    if not last:
                        half(i + 1, 1)

                half(0, 1)
                with act.Fori(0, groups - 1) as i:
                    group(i, False)
                group(groups - 1, True)

            @block.vector
            def _(dve):
                dve.sem_inc(split_done, done(0))
                dve.sem_inc(scaled, per)

                def split(i, k):
                    dve.wait_ge(half_done, done(i * n_ff + k))
                    dve.wait_ge(k_done, slot_free(i, k))
                    dve.tensor_tensor(w_lo[k % 2][:, :], w_f[k % 2][:, :], as_f32(w_hi[k % 2][:, :]), ALU.subtract)
                    dve.tensor_tensor(f_lo[k % 2][:, :], f_f[k % 2][:, :], as_f32(f_hi[k % 2][:, :]), ALU.subtract).then_inc(split_done, 1)

                def scale(i, t):
                    count = i * per + t
                    dve.wait_ge(root_done, count + 1)
                    dve.reciprocal(stat[:, t, 2:3], stat[:, t, 1:2]).then_inc(recip_done, 1)
                    dve.wait_ge(recip_done, count + 1)
                    dve.wait_ge(y_free, freed(count, per, per))
                    dve.scalar_tensor_tensor(out=y[t][:, :], in0=ps[t][:, :], scalar=stat[:, t, 2:3], in1=gain[:, :],
                                             op0=ALU.mult, op1=ALU.mult).then_inc(scaled, 1)

                def group(i, last):
                    for k in range(2, n_ff):
                        split(i, k)
                    if not last:
                        split(i + 1, 0)
                    for t in range(per):
                        scale(i, t)
                    if not last:
                        split(i + 1, 1)

                split(0, 1)
                dve.wait_ge(gain_in, 16)
                with dve.Fori(0, groups - 1) as i:
                    group(i, False)
                group(groups - 1, True)

            @block.tensor
            def _(pe):
                pe.sem_inc(k_done, per + 1)
                with pe.Fori(0, groups) as i:
                    for k in range(n_ff):
                        pe.wait_ge(split_done, done(i * n_ff + k))
                        for t in range(per):
                            if k == 0:
                                pe.wait_ge(scaled, freed(i * per + t, per, per))
                            for j, (x, w) in enumerate(((f_hi, w_hi), (f_hi, w_lo), (f_lo, w_hi))):
                                for half in range(d // BANK):
                                    cols = slice(half * BANK, (half + 1) * BANK)
                                    m = pe.matmul(ps[t][:, cols], x[k % 2][:, t * P:(t + 1) * P], w[k % 2][:, cols],
                                                  start=(k == 0 and j == 0), stop=(k == n_ff - 1 and j == 2))
                            if k == n_ff - 1:
                                m.then_inc(k_done, 1)
                        if k < n_ff - 1:
                            m.then_inc(k_done, 1)


def build(nc, a, out):
    d = a["x"].shape[2]
    seq = a["x"].shape[1]
    a.update(d=d, seq=seq, tiles=seq // P, kc=d // P, d_in=a["w_in"].shape[2], d_pool=a["pool_scale"].shape[1],
             d_attn=a["attn_scale"].shape[1], n_ff2=a["conv_b"].shape[1] // P, conv_width=a["conv_w"].shape[1])
    heads = a["d_attn"] // HEAD_DIM
    n_qk = 2 * a["d_attn"] // P

    def scratch(name, shape, dtype):
        return nc.dram_tensor(name, shape, dtype, kind="Internal").ap()

    s = {
        "v": scratch("v_scratch", [heads, P, a["tiles"], 2, HEAD_DIM], F32),
        "qk": scratch("qk_scratch", [n_qk, 2, P, seq], F32),
        "x2": scratch("x2_scratch", [a["tiles"], P, d], F32),
        "h2T": scratch("h2T_scratch", [2, P, a["kc"], seq], F32),
        "f": scratch("f_scratch", [a["n_ff2"] // 2, P, seq], F32),
        "merged": scratch("merged_scratch", [a["d_pool"] + a["d_attn"], seq], F32),
        "attn_low": scratch("attn_low_scratch", [a["d_attn"], seq], F32),
    }
    with ExitStack() as stack:
        n = Names(nc, stack)
        c = {"ident": n.sb("ident", [P, P]), "ident_r": n.sb("ident_r", [P, P], F32R), "not_before": n.sb("not_before", [P, P], F32R),
             "ones": n.sb("ones", [P, 2]), "eps": n.sb("eps", [P, 1]),
             "cols": n.sb("cols", [P, 4 * a["n_ff2"] + 8])}
        bridge = n.sb("bridge", [P, 4, BANK])
        with ExitStack() as inner:
            m = Names(nc, inner)
            hT = [m.sb(f"hT{i}", [P, a["kc"], seq], F32R) for i in range(2)]
            w_first = m.sb("w_f0", [P, a["kc"], P])
            with ExitStack() as first:
                f = Names(nc, first)
                start = {"xt": [f.sb(f"xt{i}", [P, d]) for i in range(2)], "gain": f.sb("gain", [P, d]),
                         "wv_f": bridge[:, 0:3, :],
                         "x_in": f.sems("x_in", 2), "gain_in": f.sem("gain_in"), "wv_in": f.sems("wv_in", 3)}
                phase_setup(nc, a, c, start)
                phase_values(nc, a, c, s, hT, start, w_first, bridge)
            phase_projections(nc, a, c, s, hT, w_first, bridge)
        wide = [n.sb(f"wide{i}", [P, a["kc"], BANK], F32R) for i in range(4)]
        phase_attention(nc, a, c, s, wide, bridge)
        up_start = {"h": [n.sb(f"up_start_h{i}", [P, a["kc"], BANK], F32R) for i in range(2)],
                    "w_f": n.sb("wu_f0", [P, 2, a["kc"], P]),
                    "w_hi": n.sb("wu_hi0", [P, 2, a["kc"], P], F32R), "w_lo": n.sb("wu_lo0", [P, 2, a["kc"], P], F32R)}
        phase_mix(nc, a, c, s, wide, bridge, up_start)
        down_start = {"w_f": [bridge[:, 0:2, :].rearrange("p c n -> p (c n)"), n.sb("wd_f1", [P, d])[:, :]],
                      "f_f": [bridge[:, 2, :], bridge[:, 3, :]]}
        for half in ("hi", "lo"):
            flat = up_start["w_" + half][:, :, :, :].rearrange("p h c n -> p (h c n)")
            down_start["w_" + half], down_start["f_" + half] = flat[:, 0:d], flat[:, d:d + BANK]
        phase_up(nc, a, c, s, wide, up_start, down_start)
        phase_down(nc, a, c, s, out, down_start)



def kernel(**inputs):
    import numpy as _np
    import concourse.bacc as _bacc
    from concourse.bass_utils import run_bass_kernel_spmd as _run

    nc = _bacc.Bacc("TRN2", target_bir_lowering=False, num_devices=1)
    arrays, args = {}, {}
    for name, value in inputs.items():
        array = _np.ascontiguousarray(value)
        arrays[f"in_{name}"] = array
        args[name] = nc.dram_tensor(f"in_{name}", array.shape, mybir.dt.from_np(array.dtype), kind="ExternalInput").ap()
    out = nc.dram_tensor("layer_out", inputs["x"].shape, F32, kind="ExternalOutput").ap()
    build(nc, args, out)
    result = _run(nc, [arrays], core_ids=[0])
    return result.results[0]["layer_out"]
```
